# Optimizing a Trainium2 kernel written in Bass

```python
import math, functools
import jax, jax.numpy as jnp
from jax import lax
import numpy as np

D_MODEL = 1024
BATCH = 1
SEQ = 256
DEPTH = 1
DEC_BATCH = 8
DEC_SEQ = 8
PAST_LEN = 256
PAGE_SIZE = 128

MLSTM_HEADS = 4
MLSTM_HEAD_DIM = D_MODEL // MLSTM_HEADS
MLSTM_WIDTH = MLSTM_HEADS * MLSTM_HEAD_DIM
MLSTM_CHUNK = 128
FOX_HEADS = 8
FOX_HEAD_DIM = D_MODEL // FOX_HEADS
FOX_WIDTH = FOX_HEADS * FOX_HEAD_DIM
Q_BLOCK = 128
N_GROUPS = 4
EXPERTS_PER_GROUP = 8
N_EXPERTS = N_GROUPS * EXPERTS_PER_GROUP
TOP_K_IN_GROUP = 2
D_EXPERT = D_MODEL // 4
RMS_EPS = 1e-6
SPLIT_SIZES = (MLSTM_WIDTH, MLSTM_WIDTH, MLSTM_WIDTH, MLSTM_WIDTH, MLSTM_HEADS, MLSTM_HEADS,
               FOX_WIDTH, FOX_WIDTH, FOX_WIDTH, FOX_HEADS, D_MODEL, D_MODEL)
N_IN = sum(SPLIT_SIZES)

kernel_name = "hybrid_mlstm_fox_hmoe_step"

def rmsnorm(x, g):
    xf = x.astype(jnp.float32)
    y = xf * lax.rsqrt(jnp.mean(xf * xf, axis=-1, keepdims=True) + RMS_EPS)
    return (y * g.astype(jnp.float32)).astype(x.dtype)

def mlstm_chunk(carry, xs):
    C, n, m = carry
    q, k, v, ig, lf = xs
    L = q.shape[2]
    b = jnp.cumsum(lf, axis=-1)
    causal = jnp.tril(jnp.ones((L, L), dtype=bool))
    log_w = jnp.where(causal, b[..., :, None] - b[..., None, :] + ig[..., None, :], -jnp.inf)
    log_inter = b + m[..., None]
    m_t = jnp.maximum(log_inter, jnp.max(log_w, axis=-1))
    w_intra = jnp.exp(log_w - m_t[..., None])
    w_inter = jnp.exp(log_inter - m_t)
    s = jnp.einsum('bhtd,bhsd->bhts', q, k) * w_intra
    num = w_inter[..., None] * jnp.einsum('bhtd,bhde->bhte', q, C) + jnp.einsum('bhts,bhse->bhte', s, v)
    den = w_inter * jnp.einsum('bhtd,bhd->bht', q, n) + jnp.sum(s, axis=-1)
    h = num / jnp.maximum(jnp.abs(den), jnp.exp(-m_t))[..., None]
    m_new = m_t[..., -1]
    decay_state = jnp.exp(b[..., -1] + m - m_new)
    w_rows = jnp.exp(b[..., -1:] - b + ig - m_new[..., None])
    C_new = decay_state[..., None, None] * C + jnp.einsum('bhs,bhsd,bhse->bhde', w_rows, k, v)
    n_new = decay_state[..., None] * n + jnp.einsum('bhs,bhsd->bhd', w_rows, k)
    return (C_new, n_new, m_new), h

def mlstm_sequence(q, k, v, ig, lf, C0, n0, m0):
    B, H, T, Dh = q.shape
    L = MLSTM_CHUNK if T % MLSTM_CHUNK == 0 else T
    n_chunks = T // L

    def chunkify(a):
        return jnp.moveaxis(a.reshape(a.shape[:2] + (n_chunks, L) + a.shape[3:]), 2, 0)

    carry0 = (C0.astype(jnp.float32), n0.astype(jnp.float32), m0.astype(jnp.float32))
    (C, n, m), h = lax.scan(mlstm_chunk, carry0,
                            (chunkify(q), chunkify(k), chunkify(v), chunkify(ig), chunkify(lf)))
    h = jnp.moveaxis(h, 0, 2).reshape(B, H, T, Dh)
    return h, C, n, m

def fox_attention(q, k, v, F_q, F_k, q_start):
    B, T, H, Dh = q.shape
    S = k.shape[1]
    k_pos = jnp.arange(S)
    q_pos = q_start + jnp.arange(T)
    Fk_t = jnp.transpose(F_k, (0, 2, 1))
    scale = Dh ** -0.5

    def attend(blk):
        qb, Fqb, pb = blk
        s = jnp.einsum('bqhd,bkhd->bhqk', qb, k).astype(jnp.float32) * scale
        s = s + jnp.transpose(Fqb, (0, 2, 1))[..., None] - Fk_t[:, :, None, :]
        s = jnp.where(k_pos[None, :] <= pb[:, None], s, -jnp.inf)
        p = jax.nn.softmax(s, axis=-1)
        return jnp.einsum('bhqk,bkhd->bqhd', p.astype(v.dtype), v)

    if T > Q_BLOCK and T % Q_BLOCK == 0:
        nb = T // Q_BLOCK
        blocks = (jnp.moveaxis(q.reshape(B, nb, Q_BLOCK, H, Dh), 1, 0),
                  jnp.moveaxis(F_q.reshape(B, nb, Q_BLOCK, H), 1, 0),
                  q_pos.reshape(nb, Q_BLOCK))
        out = lax.map(attend, blocks)
        return jnp.moveaxis(out, 0, 1).reshape(B, T, H, Dh)
    return attend((q, F_q, q_pos))

def hierarchical_moe(h, w_router_group, b_router_group, w_router_expert, b_router_expert, w_gate, w_up, w_down):
    B, T, D = h.shape
    t = h.reshape(B * T, D)
    g_prob = jax.nn.softmax((t @ w_router_group).astype(jnp.float32) + b_router_group.astype(jnp.float32), axis=-1)
    g_p, g_idx = lax.top_k(g_prob, 1)
    g_onehot = jax.nn.one_hot(g_idx[:, 0], N_GROUPS, dtype=jnp.float32)
    e_logits = ((t @ w_router_expert).astype(jnp.float32) + b_router_expert.astype(jnp.float32)
                ).reshape(B * T, N_GROUPS, EXPERTS_PER_GROUP)
    e_in = jnp.einsum('ng,nge->ne', g_onehot, e_logits)
    e_prob = jax.nn.softmax(e_in, axis=-1)
    e_p, e_idx = lax.top_k(e_prob, TOP_K_IN_GROUP)
    e_p = e_p / jnp.sum(e_p, axis=-1, keepdims=True)
    w_group = jnp.sum(jax.nn.one_hot(e_idx, EXPERTS_PER_GROUP, dtype=jnp.float32) * e_p[..., None], axis=1) * g_p
    combine = (g_onehot[:, :, None] * w_group[:, None, :]).astype(h.dtype)
    out = jnp.zeros_like(t)
    for g in range(N_GROUPS):
        sl = slice(g * EXPERTS_PER_GROUP, (g + 1) * EXPERTS_PER_GROUP)
        hg = jax.nn.silu(jnp.einsum('nd,edf->nef', t, w_gate[sl])) * jnp.einsum('nd,edf->nef', t, w_up[sl])
        out = out + jnp.einsum('nef,efd->nd', hg * combine[:, g, :, None], w_down[sl])
    return out.reshape(B, T, D)

def hybrid_layer(x, k_past, v_past, lf_past, C0, n0, m0,
                 norm1_g, w_in, b_igate, b_fgate_mlstm, b_fgate_fox, mlstm_norm_g, q_norm_g, k_norm_g,
                 w_branch_mlstm, w_branch_fox, w_out, norm2_g, w_router_group, b_router_group,
                 w_router_expert, b_router_expert, w_gate, w_up, w_down):
    f32 = jnp.float32
    B, T, _ = x.shape
    h = rmsnorm(x, norm1_g)
    proj = h @ w_in
    bounds = np.cumsum(SPLIT_SIZES)[:-1].tolist()
    mq, mk, mv, mo, mi, mf, fq, fk, fv, ff, ga, gb = jnp.split(proj, bounds, axis=-1)

    def heads_first(a):
        return a.reshape(B, T, MLSTM_HEADS, MLSTM_HEAD_DIM).transpose(0, 2, 1, 3).astype(f32)
    q_a = heads_first(mq)
    k_a = heads_first(mk) * (MLSTM_HEAD_DIM ** -0.5)
    v_a = heads_first(mv)
    ig = (mi.astype(f32) + b_igate.astype(f32)).transpose(0, 2, 1)
    lf_a = jax.nn.log_sigmoid(mf.astype(f32) + b_fgate_mlstm.astype(f32)).transpose(0, 2, 1)
    h_a, C, n, m = mlstm_sequence(q_a, k_a, v_a, ig, lf_a, C0, n0, m0)
    h_a = rmsnorm(h_a.transpose(0, 2, 1, 3), mlstm_norm_g).reshape(B, T, MLSTM_WIDTH)
    h_a = (jax.nn.sigmoid(mo.astype(f32)) * h_a).astype(x.dtype)
    branch_a = h_a @ w_branch_mlstm

    q_b = rmsnorm(fq.reshape(B, T, FOX_HEADS, FOX_HEAD_DIM), q_norm_g)
    k_b = rmsnorm(fk.reshape(B, T, FOX_HEADS, FOX_HEAD_DIM), k_norm_g)
    v_b = fv.reshape(B, T, FOX_HEADS, FOX_HEAD_DIM)
    lf_b = jax.nn.log_sigmoid(ff.astype(f32) + b_fgate_fox.astype(f32))
    past_len = k_past.shape[1]
    k_all = jnp.concatenate([k_past.astype(k_b.dtype), k_b], axis=1)
    v_all = jnp.concatenate([v_past.astype(v_b.dtype), v_b], axis=1)
    F_all = jnp.cumsum(jnp.concatenate([lf_past.astype(f32), lf_b], axis=1), axis=1)
    o_b = fox_attention(q_b, k_all, v_all, F_all[:, past_len:], F_all, past_len)
    branch_b = o_b.reshape(B, T, FOX_WIDTH).astype(x.dtype) @ w_branch_fox

    merged = jax.nn.sigmoid(ga) * branch_a + jax.nn.sigmoid(gb) * branch_b
    x = x + merged @ w_out
    x = x + hierarchical_moe(rmsnorm(x, norm2_g), w_router_group, b_router_group,
                             w_router_expert, b_router_expert, w_gate, w_up, w_down)
    return x, k_b, v_b, lf_b, C, n, m

def setup_inputs(seed: int = 0) -> dict:
    key = jax.random.key(seed)
    ks = jax.random.split(key, 32)
    n_pages = PAST_LEN // PAGE_SIZE
    n_phys = (DEC_BATCH * n_pages * 5) // 4

    def normal(k, shape, scale=1.0, shift=0.0):
        return shift + scale * jax.random.normal(k, shape, jnp.float32)

    page_table = jax.random.permutation(ks[9], n_phys)[:DEC_BATCH * n_pages].reshape(DEC_BATCH, n_pages).astype(jnp.int32)
    return {
        "x_prompt": normal(ks[0], (BATCH, SEQ, D_MODEL)),
        "x_sample": normal(ks[1], (DEC_BATCH, DEC_SEQ, D_MODEL)),
        "cache_k": normal(ks[2], (DEPTH, n_phys, PAGE_SIZE, FOX_HEADS, FOX_HEAD_DIM)),
        "cache_v": normal(ks[3], (DEPTH, n_phys, PAGE_SIZE, FOX_HEADS, FOX_HEAD_DIM)),
        "cache_lf": jax.nn.log_sigmoid(normal(ks[4], (DEPTH, n_phys, PAGE_SIZE, FOX_HEADS), 0.5, 3.0)),
        "state_C": normal(ks[5], (DEPTH, DEC_BATCH, MLSTM_HEADS, MLSTM_HEAD_DIM, MLSTM_HEAD_DIM), 0.1),
        "state_n": normal(ks[6], (DEPTH, DEC_BATCH, MLSTM_HEADS, MLSTM_HEAD_DIM), 0.1),
        "state_m": normal(ks[7], (DEPTH, DEC_BATCH, MLSTM_HEADS), 0.5, 1.0),
        "page_table": page_table,
        "norm1_g": normal(ks[10], (DEPTH, D_MODEL), 0.05, 1.0),
        "w_in": normal(ks[11], (DEPTH, D_MODEL, N_IN), D_MODEL ** -0.5),
        "b_igate": normal(ks[12], (DEPTH, MLSTM_HEADS), 0.1),
        "b_fgate_mlstm": normal(ks[13], (DEPTH, MLSTM_HEADS), 0.5, 3.0),
        "b_fgate_fox": normal(ks[14], (DEPTH, FOX_HEADS), 0.5, 3.0),
        "mlstm_norm_g": normal(ks[15], (DEPTH, MLSTM_HEADS, MLSTM_HEAD_DIM), 0.05, 1.0),
        "q_norm_g": normal(ks[16], (DEPTH, FOX_HEAD_DIM), 0.05, 1.0),
        "k_norm_g": normal(ks[17], (DEPTH, FOX_HEAD_DIM), 0.05, 1.0),
        "w_branch_mlstm": normal(ks[18], (DEPTH, MLSTM_WIDTH, D_MODEL), MLSTM_WIDTH ** -0.5),
        "w_branch_fox": normal(ks[19], (DEPTH, FOX_WIDTH, D_MODEL), FOX_WIDTH ** -0.5),
        "w_out": normal(ks[20], (DEPTH, D_MODEL, D_MODEL), D_MODEL ** -0.5),
        "norm2_g": normal(ks[21], (DEPTH, D_MODEL), 0.05, 1.0),
        "w_router_group": normal(ks[22], (DEPTH, D_MODEL, N_GROUPS), D_MODEL ** -0.5),
        "b_router_group": normal(ks[23], (DEPTH, N_GROUPS), 0.01),
        "w_router_expert": normal(ks[24], (DEPTH, D_MODEL, N_EXPERTS), D_MODEL ** -0.5),
        "b_router_expert": normal(ks[25], (DEPTH, N_EXPERTS), 0.01),
        "w_gate": normal(ks[26], (DEPTH, N_EXPERTS, D_MODEL, D_EXPERT), D_MODEL ** -0.5),
        "w_up": normal(ks[27], (DEPTH, N_EXPERTS, D_MODEL, D_EXPERT), D_MODEL ** -0.5),
        "w_down": normal(ks[28], (DEPTH, N_EXPERTS, D_EXPERT, D_MODEL), D_EXPERT ** -0.5),
    }

def reference(x_prompt, x_sample, cache_k, cache_v, cache_lf, state_C, state_n, state_m, page_table,
              norm1_g, w_in, b_igate, b_fgate_mlstm, b_fgate_fox, mlstm_norm_g, q_norm_g, k_norm_g,
              w_branch_mlstm, w_branch_fox, w_out, norm2_g, w_router_group, b_router_group,
              w_router_expert, b_router_expert, w_gate, w_up, w_down):
    f32 = jnp.float32
    bp = x_prompt.shape[0]
    bs = x_sample.shape[0]
    n_pages = page_table.shape[1]
    past = n_pages * PAGE_SIZE
    xp, xs = x_prompt, x_sample
    kp_l, vp_l, lfp_l, Cp_l, np_l, mp_l = [], [], [], [], [], []
    ks_l, vs_l, lfs_l, Cs_l, ns_l, ms_l = [], [], [], [], [], []
    for l in range(DEPTH):
        layer_params = (norm1_g[l], w_in[l], b_igate[l], b_fgate_mlstm[l], b_fgate_fox[l], mlstm_norm_g[l],
                        q_norm_g[l], k_norm_g[l], w_branch_mlstm[l], w_branch_fox[l], w_out[l], norm2_g[l],
                        w_router_group[l], b_router_group[l], w_router_expert[l], b_router_expert[l],
                        w_gate[l], w_up[l], w_down[l])
        empty_kv = jnp.zeros((bp, 0, FOX_HEADS, FOX_HEAD_DIM), xp.dtype)
        empty_lf = jnp.zeros((bp, 0, FOX_HEADS), f32)
        C0 = jnp.zeros((bp, MLSTM_HEADS, MLSTM_HEAD_DIM, MLSTM_HEAD_DIM), f32)
        n0 = jnp.zeros((bp, MLSTM_HEADS, MLSTM_HEAD_DIM), f32)
        m0 = jnp.zeros((bp, MLSTM_HEADS), f32)
        xp, kp, vp, lfp, Cp, nstp, mp = hybrid_layer(xp, empty_kv, empty_kv, empty_lf, C0, n0, m0, *layer_params)
        k_past = cache_k[l][page_table].reshape(bs, past, FOX_HEADS, FOX_HEAD_DIM)
        v_past = cache_v[l][page_table].reshape(bs, past, FOX_HEADS, FOX_HEAD_DIM)
        lf_past = cache_lf[l][page_table].reshape(bs, past, FOX_HEADS)
        xs, kss, vss, lfss, Cs, nsts, ms = hybrid_layer(xs, k_past, v_past, lf_past,
                                                         state_C[l], state_n[l], state_m[l], *layer_params)
        kp_l.append(kp); vp_l.append(vp); lfp_l.append(lfp); Cp_l.append(Cp); np_l.append(nstp); mp_l.append(mp)
        ks_l.append(kss); vs_l.append(vss); lfs_l.append(lfss); Cs_l.append(Cs); ns_l.append(nsts); ms_l.append(ms)
    return (xp, xs,
            jnp.stack(kp_l), jnp.stack(vp_l), jnp.stack(lfp_l),
            jnp.stack(ks_l), jnp.stack(vs_l), jnp.stack(lfs_l),
            jnp.stack(Cp_l), jnp.stack(np_l), jnp.stack(mp_l),
            jnp.stack(Cs_l), jnp.stack(ns_l), jnp.stack(ms_l))


_drawn_inputs = setup_inputs


def setup_inputs(seed=0):
    import zlib

    import numpy as np

    out = dict(_drawn_inputs(seed))
    spreads = {}
    factors = {'cache_lf': 2.984,
     'q_norm_g': 3.793,
     'b_router_group': 4.434,
     'b_router_expert': 4.105,
     'mlstm_norm_g': 2.792}
    for name, (base, spread) in spreads.items():
        noise = np.random.default_rng([zlib.crc32(name.encode()), seed]).standard_normal(out[name].shape)
        drawn = base * np.exp(spread * noise) if base else spread * noise
        out[name] = __import__('jax').numpy.asarray(drawn.astype(out[name].dtype))
    for name, factor in factors.items():
        out[name] = (out[name] * factor).astype(out[name].dtype)
    return out
```

```python
from contextlib import ExitStack

import concourse.bass as bass
from concourse import mybir

ALU = mybir.AluOpType
ACT = mybir.ActivationFunctionType
AX_X = mybir.AxisListType.X
F32 = mybir.dt.float32
F32R = mybir.dt.float32r
I32 = mybir.dt.int32
U32 = mybir.dt.uint32

P = 128
D = 1024
KC = D // P
TP, BS, TS = 256, 8, 8
NS = BS * TS
NT = TP + NS
TILE0 = (0, 128, 256)
ROWS = (128, 128, NS)
HM, DM = 4, 256
DE = DM + 1
HF, DF = 8, 128
PAST, PAGE = 256, 128
KEYS = PAST + TS
NPAGES = PAST // PAGE
NPHYS = BS * NPAGES * 5 // 4
NE, EPG, NG, FE = 32, 8, 4, 256
EPS = 1e-6
NEG = -1e30
CW = 256
UN = KC * CW
SECTIONS = ("mk", "mq", "mv", "mo", "ga", "gb", "fk", "fq", "fv", "bm", "bf", "out")
CPS = D // CW
NCH = len(SECTIONS) * CPS
BY_FEATURE = ("mk", "mq", "mo", "ga", "gb", "bm", "bf")
NRING = 3
CAP = 64
SLOTS = 2 * NT
XC = SLOTS + CAP
RAW1, RAWM = 2, 12
EB = RAWM // 3
JB = 8
DIAG = TS * HF + TS


def stages():
    at = {c: [] for c in range(NCH)}
    for n in range(1, 6):
        at[n - 1].append(("G", n, 0))
    for t in range(3):
        at[5 + t].append(("KT", t, 0))
    for n in range(2 * HM):
        at[12 + n].append(("P2", n // HM, n % HM))
        at[11 + n].append(("P1", n // HM, n % HM))
    at[15] += [("F1", 0, 0), ("F2", 0, 0)]
    at[19].append(("F1", 1, 0))
    at[20].append(("F2", 1, 0))
    for h in range(HM):
        at[20 + h].append(("SA", h, 0))
        for b in range(BS):
            at[20 + h].append(("SB", h, b))
    at[23].append(("F1", 2, 0))
    at[23].append(("F2", 2, 0))
    for t in range(3):
        at[27 + t].append(("N1", 0, t))
        at[28 + t].append(("N2", 0, t))
        at[31 + t].append(("N1", 1, t))
        at[32 + t].append(("N2", 1, t))
    line = []
    for n in range(HF + 3):
        line += [(k, n - s, 0) for s, k in ((3, "FS4"), (2, "FS3"), (1, "FS2"), (0, "FS1")) if 0 <= n - s < BS]
        line += [(k, n - s, 0) for s, k in ((2, "FP3"), (1, "FP2"), (0, "FP1")) if 0 <= n - s < HF]
    cut = (len(line) + 3) // 4
    for n, st in enumerate(line):
        at[35 + n // cut].append(st)
    return at


def banks_of(st):
    kind, x, y = st
    if kind == "G":
        return {1: (3,), 2: (4, 5, 6), 3: (3, 7), 4: (3, 7, 4, 5, 6), 5: (3,)}[x]
    if kind == "P2":
        return (4, 6, 7) if x == 0 else (5, 4, 6, 7)
    if kind == "SB":
        return ((5, 4) if y == BS - 1 else ()) + (6, 7)
    return {"KT": (6, 7), "P1": (3,), "F1": (), "F2": (6, 7), "SA": (3,), "N1": (), "N2": (6, 7),
            "FP1": (3, 4), "FP2": (5,), "FP3": (6,), "FS1": (3,), "FS2": (5,), "FS3": (4,), "FS4": (7,)}[kind]


class Steps:

    def __init__(self, eng, step):
        self.eng, self.step, self.seen = eng, step, {}

    def __call__(self, ins, event=None):
        s = event if event is not None else self.step
        self.seen[s.name] = self.seen.get(s.name, 0) + 1
        ins.then_inc(s, 1)
        self.eng.wait_ge(s, self.seen[s.name])


def hybrid_step(nc, A, O):
    AT = stages()
    fill, count = {}, {b: 0 for b in range(8)}
    for c in range(NCH):
        for st in AT[c]:
            for b in banks_of(st):
                fill[st, b] = count[b]
                count[b] += 1
    ctx = ExitStack()
    with ctx:
        handles = {}

        def sem(name):
            if name not in handles:
                
                handles[name] = ctx.enter_context(nc.semaphore(name))
            return handles[name]

        FW, RW = 34460, 18432
        fm = ctx.enter_context(nc.sbuf_tensor("fm", [P, FW], F32))
        rm = ctx.enter_context(nc.sbuf_tensor("rm", [P, RW], F32R))
        im = ctx.enter_context(nc.sbuf_tensor("im", [P, 56 + NE * JB], I32))
        pt = im[0:1, 0:BS * NPAGES]
        slot_i = im[:, 16:22]
        flag_i = im[0:1, 22:23]
        off_i = im[0:1, 24:24 + NE]
        blk_i = im[0:1, 56:56 + NE * JB]
        bank = [ctx.enter_context(nc.psum_tensor(f"bank{b}", [P, 512], F32)) for b in range(8)]
        y_slots = nc.dram_tensor("y_slots", [XC, D], F32).ap()
        x1_dram = nc.dram_tensor("x1_rows", [P, 3, D], F32).ap()
        top = [0]

        def take(n):
            top[0] += n
            assert top[0] <= FW, top[0]
            return fm[:, top[0] - n:top[0]]

        def cube(ap, a):
            return ap.rearrange("p (a b) -> p a b", a=a)

        ident, upto, ones, last = take(128), take(128), take(128), take(128)
        maskT, mask, after, before = take(128), take(128), take(128), take(128)
        negs = take(256)
        upto8, maskT8, mask8, last8 = take(64), take(64), take(64), take(64)
        e8, blk8, first8, maskHT = take(64), take(8), take(8), take(8)
        gin = cube(take(48), 3)
        lf = cube(take(36), 3)
        cum = cube(take(36), 3)
        aa = cube(take(12), 3)
        amax = cube(take(12), 3)
        mprev = cube(take(12), 3)
        mtop = cube(take(24), 3)
        lastv = cube(take(24), 3)
        ew = cube(take(48), 3)
        dec8, small, bias16, rb36, lfn = take(32), take(96), take(16), take(36), take(64)
        mg = take(8)
        base_raw = top[0]
        raw = [take(UN) for _ in range(RAW1)]
        sgm = cube(take(KC * NT), KC)
        sga = cube(take(KC * NT), KC)
        base_gb = top[0]
        kM01 = cube(take(2 * D), 2)
        vx01 = take(2 * HM * DE).rearrange("p (t h e) -> p t h e", t=2, h=HM)
        kT = cube(take(KC * NT), KC)
        qT = cube(take(KC * NT), KC)
        kM2 = take(D)
        vx2 = cube(take(HM * DE), HM)
        base_x = top[0]
        Cx = take(HM * 2 * DE).rearrange("p (h c e) -> p h c e", h=HM, c=2)
        Cin = [cube(take(2 * DE), 2) for _ in range(3)]
        Cout = [cube(take(2 * DE), 2) for _ in range(2)]
        W = take(3 * HM * P).rearrange("p (t h s) -> p t h s", t=3, h=HM)
        base_num = top[0]
        num = cube(take(HM * DE), HM)
        qm = take(2 * BS * DIAG)
        SW = [take(128) for _ in range(2)]
        kw = [take(DM) for _ in range(2)]
        kwm = [take(DM) for _ in range(2)]
        inter = take(DE)
        hv = take(512)
        top[0] = base_x
        xt, g1row = cube(take(3 * D), 3), take(D)
        wg = take(128)
        top[0] = base_num
        dg = cube(take(3 * 512), 3)
        top[0] = base_gb
        sgb = cube(take(KC * NT), KC)
        base_att = top[0]
        fk = cube(take(3 * D), 3)
        fq = cube(take(3 * D), 3)
        fv = cube(take(3 * D), 3)
        fkT = cube(take(HF * NT), HF)
        fqT = cube(take(HF * NT), HF)
        oT = cube(take(HF * NT), HF)
        base_p = top[0]
        PTm = cube(take(3 * HF * DIAG), 3)
        Ob, lfe = take(128), cube(take(4 * 64), 4)
        lfp = cube(take(4 * 8), 4)
        gk, gq = take(128), take(128)
        top[0] = base_p
        sqt = take(D)
        top[0] = base_raw + RAW1 * UN
        KTc = cube(take(HF * KEYS), HF)
        top[0] = base_att
        Vc = [cube(take(NPAGES * D), NPAGES) for _ in range(2)]
        sS, Pp, PT, Ps, qms = take(384), take(384), take(384), take(320), take(HF * DIAG)
        assert top[0] <= base_att + 6 * D
        top[0] = base_att
        xr = cube(take(3 * D), 3)
        x1 = cube(take(3 * D), 3)
        h2 = cube(take(3 * D), 3)
        h2T = cube(take(KC * NT), KC)
        g2row = take(D)
        top[0] = base_raw
        rawm = [take(UN) for _ in range(RAWM)]
        xs = cube(take(KC * XC), KC)
        yrow = take(D)
        tmp, gu = take(512), take(512)
        top[0] -= 2 * D
        iota, wr = take(SLOTS), take(KC * 36)
        wr3 = cube(wr, KC)
        lg = cube(take(3 * 36), 3)
        base_rt = top[0]
        gl8, gtop, gidx, el8, etop, eidx = (cube(take(24), 3) for _ in range(6))
        ghot, gexp, picks = cube(take(12), 3), cube(take(12), 3), cube(take(6), 3)
        scal = [take(3) for _ in range(6)]
        esel = cube(take(96), 3)
        hot = [cube(take(96), 3) for _ in range(2)]
        chosen, rank = cube(take(96), 3), cube(take(96), 3)
        offs, cnts = take(NE), take(NE)
        assert top[0] <= FW
        blkf = cube(fm[:, base_rt:base_rt + NE * JB], NE)
        top[0] = base_raw
        xe = cube(take(3 * D), 3)
        gat = [take(D) for _ in range(6)]

        pair = [(cube(rm[:, 4096 * i:4096 * i + UN], KC), cube(rm[:, 4096 * i + UN:4096 * (i + 1)], KC))
                for i in range(2)]
        R1, R2 = 8192, 8192 + 2 * KC * NT
        r1 = [cube(rm[:, R1 + i * KC * NT:R1 + (i + 1) * KC * NT], KC) for i in range(2)]
        r2 = [cube(rm[:, R2 + i * KC * NT:R2 + (i + 1) * KC * NT], KC) for i in range(2)]
        pair3 = pair + [(cube(rm[:, R1:R1 + UN], KC), cube(rm[:, R1 + UN:R1 + 2 * UN], KC))]
        pack = [cube(rm[:, R2 + 1024 * i:R2 + 1024 * (i + 1)], KC) for i in range(2)]
        htp = cube(rm[:, R2 + 2048:R2 + 2304], 2)
        down = [rm[:, R1 + UN * i:R1 + UN * (i + 1)].rearrange("p (k n) -> p k n", k=2) for i in range(2)]
        h2s = [cube(rm[:, 3072 * i:3072 * (i + 1)], 3) for i in range(2)]
        onehot = cube(rm[:, 6144:6144 + 3 * SLOTS], 3)
        wts = cube(dec8[:, 0:6], 3)
        wgs = [cube(rm[:, R2 + 128 * i:R2 + 128 * (i + 1)], KC) for i in range(2)]

        def kM(t, h):
            return kM01[:, t, DM * h:DM * (h + 1)] if t < 2 else kM2[0:NS, DM * h:DM * (h + 1)]

        def vx(t, h, w=DE):
            return vx01[:, t, h, 0:w] if t < 2 else vx2[0:NS, h, 0:w]

        def diag(ap, n=HF):
            return ap.rearrange("p (b x) -> p b x", x=DIAG)[:, :, 0:TS]

        def units(c):
            n0 = sum(2 if SECTIONS[k // CPS] in BY_FEATURE else 3 for k in range(c))
            return n0, (2 if SECTIONS[c // CPS] in BY_FEATURE else 3)

        mxi = [im[:, 56 + 24 * i:56 + 24 * (i + 1)].bitcast(U32) for i in range(2)]

        def experts(eng, base, total, step):
            first, turns = base // EB, total // EB
            for u in range(EB):
                step(first, u, base + u, total - 1 - u)
            with eng.Fori(first + 1, first + turns - 1) as i:
                for u in range(EB):
                    step(i, u, i * EB + u, EB)
            for u in range(EB):
                step(first + turns - 1, u, base + total - EB + u, EB - 1 - u)

        def either(eng, crowd):
            eng.wait_ge(sem("m_stored_all"), 1)
            most = eng.value_load(flag_i, min_val=0, max_val=2 * NT)
            with eng.If(most > CAP):
                crowd()
            with eng.Else():
                eng.nop()
            eng.nop()

        block = ctx.enter_context(nc.Block())

        @block.sync
        def _(sp):
            def small_in(dst, src, s="small_in"):
                sp.dma_start(dst, src).then_inc(sem(s), 16)

            sp.dma_start(xt[:, 0:2, :], A["x_prompt"]).then_inc(sem("x_in"), 16)
            sp.dma_start(xt[0:NS, 2, :], A["x_sample"]).then_inc(sem("x_in"), 16)
            sp.dma_start(g1row, A["norm1_g"].partition_broadcast(P)).then_inc(sem("x_in"), 16)
            for c in range(RAW1):
                sp.dma_start(raw[c], A["w_dense"][c]).then_inc(sem(f"raw_in{c % RAW1}"), 16)
            small_in(wg, A["w_gates"])
            small_in(bias16, A["b_gates"].partition_broadcast(P))
            small_in(mg, A["mlstm_norm_g"])
            small_in(small[0:BS, 90:94], A["state_m"])
            for c in range(RAW1, NCH):
                sp.wait_ge(sem("split_done"), c - RAW1 + 1)
                sp.dma_start(raw[c % RAW1], A["w_dense"][c]).then_inc(sem(f"raw_in{c % RAW1}"), 16)
                if c == 26:
                    sp.wait_ge(sem("ha_split"), 6)
                    sp.dma_start(gk, A["k_norm_g"].partition_broadcast(P)).then_inc(sem("qk_gain_in"), 16)
                    sp.dma_start(gq, A["q_norm_g"].partition_broadcast(P)).then_inc(sem("qk_gain_in"), 16)
                if c == 42:
                    sp.wait_ge(sem("o_split"), KC)
                    sp.dma_start(xr[:, 0:2, :], A["x_prompt"]).then_inc(sem("xr_in"), 16)
                    sp.dma_start(xr[0:NS, 2, :], A["x_sample"]).then_inc(sem("xr_in"), 16)
                    sp.dma_start(g2row, A["norm2_g"].partition_broadcast(P)).then_inc(sem("xr_in"), 16)
                    sp.dma_start(wr, A["w_router"]).then_inc(sem("xr_in"), 16)
                    sp.dma_start(rb36, A["b_router"].partition_broadcast(P)).then_inc(sem("xr_in"), 16)

            def load(slot, expert, j):
                sp.dma_start(rawm[slot], A["w_moe"][bass.ds(expert * 3 + j, 1)].rearrange("a p w -> (a p) w"))\
                    .then_inc(sem(f"e_raw{slot // 3}"), 16)

            for n in range(RAWM):
                if n < RAW1:
                    sp.wait_ge(sem("split_done"), NCH - RAW1 + 1 + n)
                elif n == RAW1:
                    sp.wait_ge(sem("m_split"), KC)
                elif n == 5:
                    sp.wait_ge(sem("x1_stored"), 16)
                    sp.wait_ge(sem("router_words"), 1)
                load(n, n // 3, n % 3)
            with sp.Fori(1, NE // EB) as i:
                for n in range(RAWM):
                    sp.wait_ge(sem(f"e_split{n % 3}"), i * EB - EB + n // 3 + 1)
                    load(n, i * EB + n // 3, n % 3)

            def crowd():
                for half in range(JB // EB):
                    for n in range(RAWM):
                        if half:
                            sp.wait_ge(sem(f"e_split{n % 3}"), NE + (half - 1) * EB + n // 3 + 1)
                        load(n, 0, n % 3)
                with sp.Fori(1, NE) as e:
                    for half in range(JB // EB):
                        for n in range(RAWM):
                            sp.wait_ge(sem(f"e_split{n % 3}"), e * JB + (NE + (half - 1) * EB + n // 3 + 1))
                            load(n, e, n % 3)

            either(sp, crowd)
            sp.wait_ge(sem("experts_done"), 1)
            sp.dma_start(xe, x1_dram).then_inc(sem("xe_in"), 16)
            for t in range(3):
                sp.wait_ge(sem("y_done"), t + 1)
                if t < 2:
                    sp.dma_start(O["y_prompt"][:, t, :], xe[:, t, :]).then_inc(sem("y_out"), 16)
                else:
                    sp.dma_start(O["y_sample"], xe[0:NS, t, :]).then_inc(sem("y_out"), 16)
            sp.wait_ge(sem("y_out"), 48)

        @block.gpsimd
        def _(pool):
            g = Steps(pool, sem("pool_step"))

            def tri(dst, n, value, fillv, pattern, cm, base=0, op=ALU.is_ge):
                g(nc.gpsimd.affine_select(out=dst, in_=dst, compare_op=op, fill=fillv, base=base,
                                          pattern=pattern, channel_multiplier=cm))

            def const(dst, v):
                g(nc.gpsimd.memset(dst, v))

            const(ident, 0.0)
            tri(ident, 128, 0, 1.0, [[-1, 128]], 1, op=ALU.not_equal)
            for dst, inside, fillv, pat, cm, base in (
                    (upto, 1.0, 0.0, [[1, 128]], -1, 0),
                    (maskT, 0.0, NEG, [[1, 128]], -1, 0),
                    (mask, 0.0, NEG, [[-1, 128]], 1, 0),
                    (after, 1.0, 0.0, [[-1, 128]], 1, -1),
                    (before, 1.0, 0.0, [[1, 128]], -1, -1),
                    (last, 1.0, 0.0, [[0, 128]], 1, -127),
                    (negs[:, 0:128], -1.0, 0.0, [[1, 128]], -1, 0)):
                const(dst, inside)
                tri(dst, 128, 0, fillv, pat, cm, base)
            const(ones, 1.0)
            const(negs[:, 128:256], -1.0)

            def blocks(dst, n, fillv):
                v = dst.rearrange("p (b t) -> p b t", t=TS)
                tri(v, n, 0, fillv, [[-TS, BS], [0, TS]], 1)
                tri(v, n, 0, fillv, [[TS, BS], [0, TS]], -1, TS - 1)

            q = NS
            for dst, inside, fillv, pat, cm in ((upto8, 1.0, 0.0, [[1, 64]], -1), (maskT8, 0.0, NEG, [[1, 64]], -1),
                                                (mask8, 0.0, NEG, [[-1, 64]], 1)):
                const(dst[0:q, :], inside)
                tri(dst[0:q, :], 64, 0, fillv, pat, cm)
                blocks(dst[0:q, :], 64, fillv)
            const(last8[0:q, :], 1.0)
            v = last8[0:q, :].rearrange("p (b t) -> p b t", t=TS)
            tri(v, 64, 0, 0.0, [[-TS, BS], [0, TS]], 1, -(TS - 1), op=ALU.is_equal)
            const(e8[0:BS, :], 1.0)
            v = e8[0:BS, :].rearrange("p (b t) -> p b t", t=TS)
            tri(v, 64, 0, 0.0, [[-1, BS], [0, TS]], 1, 0, op=ALU.is_equal)
            const(blk8[0:q, :], 1.0)
            tri(blk8[0:q, :], 8, 0, 0.0, [[-TS, BS]], 1)
            tri(blk8[0:q, :], 8, 0, 0.0, [[TS, BS]], -1, TS - 1)
            const(first8[0:q, :], 1.0)
            tri(first8[0:q, :], 8, 0, 0.0, [[-TS, BS]], 1, 0, op=ALU.is_equal)
            g(nc.gpsimd.memset(vx01[:, :, :, DM:DE], 1.0))
            g(nc.gpsimd.memset(vx2[0:q, :, DM:DE], 1.0))
            const(small[:, 95:96], 0.0)
            nc.gpsimd.memset(mprev[:, 0, :], 0.0).then_inc(sem("consts"), 1)

            def state(n):
                if n >= 3:
                    pool.wait_ge(sem("cin_used"), n - 2)
                pool.dma_start(Cin[n % 3], A["state_C"][n % BS, n // BS]).then_inc(sem(f"cin_in{n % 3}"), 16)

            def pe_past(st):
                b = banks_of(st)[-1]
                pool.wait_ge(sem(f"bank_full{b}"), fill[st, b] + 1)

            def out(dst, src, name):
                pool.dma_start(dst, src).then_inc(sem(name), 16)

            pool.dma_start(pt, A["page_table"]).then_inc(sem("pt_in"), 16)
            pool.wait_ge(sem("pt_in"), 16)
            pool.wait_ge(sem("gates_out"), 1)
            out(O["lf_prompt"], lf[:, 0:2, HM:HM + HF], "stored")
            out(O["lf_sample"], lf[0:NS, 2, HM:HM + HF], "stored")
            pool.wait_ge(sem("m_last"), 1)
            out(O["m_prompt"], lastv[0:1, 1, HM:2 * HM], "stored")
            out(O["m_sample"], lastv[0:NS:TS, 2, HM:2 * HM], "stored")

            def cache(b):
                for j in range(NPAGES):
                    page = pool.value_load(pt[0:1, b * NPAGES + j:b * NPAGES + j + 1], min_val=0, max_val=NPHYS - 1)
                    if j == 0 and b >= 1:
                        pe_past(("FS1", b - 1, 0))
                    pool.dma_start(KTc[:, :, j * PAGE:(j + 1) * PAGE],
                                   A["cache_kT"][bass.ds(page, 1)].rearrange("a d h s -> (a d) h s"))\
                        .then_inc(sem("keys_in"), 16)
                    if j == 0 and b >= 2:
                        pe_past(("FS3", b - 2, 0))
                    pool.dma_start(Vc[b % 2][:, j, :], A["cache_v"][bass.ds(page, 1)].rearrange("a s f -> (a s) f"))\
                        .then_inc(sem(f"values_in{b % 2}"), 16)
                    pool.dma_start(lfp[:, 2 * (b % 2) + j, :], A["cache_lf"][bass.ds(page, 1)].rearrange("a s h -> (a s) h"))\
                        .then_inc(sem(f"values_in{b % 2}"), 16)

            for c in range(NCH):
                if c == 12:
                    for n in range(3):
                        state(n)
                if 20 <= c < 24:
                    for b in range(BS):
                        n = (c - 20) * BS + b
                        if n + 3 < HM * BS:
                            state(n + 3)
                        pool.wait_ge(sem("cout_full"), n + 1)
                        pool.dma_start(O["C_sample"][b, c - 20], Cout[n % 2]).then_inc(sem(f"cout_out{n % 2}"), 16)
                if c == 20:
                    pool.wait_ge(sem("cx_done"), HM)
                    out(O["C_prompt"], Cx, "stored")
                if c == 34:
                    pool.wait_ge(sem("k_normed"), 3)
                    out(O["k_prompt"], fk[:, 0:2, :], "k_stored")
                    out(O["k_sample"], fk[0:NS, 2, :], "k_stored")
                    pool.wait_ge(sem("k_stored"), 32)
                    pool.wait_ge(sem("t_copied"), 12)
                    g(nc.gpsimd.memset(PTm, 0.0))
                    g(nc.gpsimd.memset(qms, 0.0))
                    g(nc.gpsimd.memset(Ps[0:NS, :], 0.0), sem("att_zeroed"))
                    cache(0)
                if c == 36:
                    pool.wait_ge(sem("unit_free_a"), units(9 * CPS)[0])
                    out(O["v_prompt"], fv[:, 0:2, :], "v_stored")
                    out(O["v_sample"], fv[0:NS, 2, :], "v_stored")
                for kind, b, _ in AT[c]:
                    if kind == "FS1":
                        if b + 1 < BS:
                            cache(b + 1)
            pool.wait_ge(sem("o_split"), KC)
            g(nc.gpsimd.iota(iota, pattern=[[1, SLOTS]], base=0, channel_multiplier=0,
                             allow_small_or_imprecise_dtypes=True), sem("iota_ready"))
            pool.wait_ge(sem("x1_full"), 1)
            pool.dma_start(x1_dram, x1).then_inc(sem("x1_stored"), 16)

            def run_experts(base, total, table):
                def place(v):
                    return pool.value_load(table[:, bass.ds(v - base, 1)], min_val=0, max_val=SLOTS)

                def packed(v, u):
                    src = xs[:, :, bass.ds(place(v), CAP)]
                    dst = pack[u % 2]
                    if not (isinstance(v, int) and v < base + 2):
                        pool.wait_ge(sem("e_gu_full"), v - 1)
                    nc.gpsimd.tensor_copy(dst[:, :, 0:CAP], src).then_inc(sem("e_pack_hi"), 1)
                    pool.wait_ge(sem("e_pack_hi"), v + 1)
                    nc.gpsimd.tensor_tensor(small[0:1, 91:92], small[0:1, 93:94], small[0:1, 93:94], ALU.add)
                    nc.gpsimd.tensor_tensor(dst[:, :, CAP:2 * CAP], src, dst[:, :, 0:CAP], ALU.subtract)\
                        .then_inc(sem("e_packed"), 1)

                def step(i, u, v, left):
                    if left >= 2:
                        packed(v + 2, u)
                    row = place(v)
                    pool.wait_ge(sem("e_y_taken"), v + 1)
                    if not (isinstance(v, int) and v == 0):
                        pool.wait_ge(sem("e_y_stored"), v * 16)
                    pool.dma_start(y_slots[bass.ds(row, CAP), :], yrow[64 * (u % 2):64 * (u % 2) + CAP, :])\
                        .then_inc(sem("e_y_stored"), 16)

                for u in range(2):
                    packed(base + u, u)
                experts(pool, base, total, step)
                pool.wait_ge(sem("e_y_stored"), (base + total) * 16)

            pool.wait_ge(sem("xs_ready"), 1)
            run_experts(0, NE, off_i)
            nc.gpsimd.memset(small[0:1, 93:94], 0.0).then_inc(sem("m_stored_all"), 1)
            either(pool, lambda: run_experts(NE, NE * JB, blk_i))
            nc.gpsimd.memset(small[0:1, 92:93], 0.0).then_inc(sem("experts_done"), 1)
            pool.wait_ge(sem("experts_done"), 1)
            for t in range(3):
                for k in range(2):
                    r = ROWS[t]
                    idx = slot_i[0:r, 2 * t + k:2 * t + k + 1].bitcast(U32)
                    pool.indirect_dma_start(gat[2 * t + k][0:r, :], None, y_slots[0:SLOTS, :],
                                            bass.IndirectOffsetOnAxis(ap=idx, axis=0)).then_inc(sem(f"gathered{t}"), 16)
            pool.wait_ge(sem("stored"), 16 * 5)
            pool.wait_ge(sem("k_stored"), 16 * 2)
            pool.wait_ge(sem("v_stored"), 16 * 2)
            for i in range(2):
                pool.wait_ge(sem(f"cout_out{i}"), 16 * (HM * BS // 2))

        @block.scalar
        def _(act):
            s = Steps(act, sem("act_step"))
            A_ = nc.scalar.activation

            def got(st, b):
                act.wait_ge(sem(f"bank_full{b}"), fill[st, b] + 1)

            def pe_past(st):
                b = banks_of(st)[-1]
                act.wait_ge(sem(f"bank_full{b}"), fill[st, b] + 1)

            def done(ins, b):
                s(ins, sem(f"bank_free{b}"))

            def split_hi(c):
                act.wait_ge(sem(f"raw_in{c % RAW1}"), 16 * (c // RAW1 + 1))
                if c >= 2:
                    act.wait_ge(sem("unit_full"), units(c - 1)[0])
                s(A_(pair[c % 2][0], cube(raw[c % RAW1], KC), ACT.Copy), sem("hi_done"))

            def evac(c):
                sec, cc = SECTIONS[c // CPS], c % CPS
                n0, n = units(c)
                if sec == "fk" and cc == 0:
                    act.wait_ge(sem("stored"), 16 * 5)
                    for i in range(2):
                        act.wait_ge(sem(f"cout_out{i}"), 16 * (HM * BS // 2))
                for u in range(n):
                    if sec in ("bm", "bf", "out"):
                        continue
                    act.wait_ge(sem("unit_full"), n0 + u + 1)
                    b = (n0 + u) % NRING
                    if sec in BY_FEATURE:
                        src, j = bank[b][:, 0:NT], 2 * cc + u
                        if sec == "mk":
                            ins = A_(kT[:, j, :], src, ACT.Copy, scale=DM ** -0.5)
                        elif sec == "mq":
                            ins = A_(qT[:, j, :], src, ACT.Copy)
                        else:
                            ins = A_({"mo": sgm, "ga": sga, "gb": sgb}[sec][:, j, :], src, ACT.Sigmoid)
                    else:
                        r = ROWS[u]
                        src = bank[b][0:r, 0:CW]
                        if sec == "mv":
                            ins = A_(vx(u, cc, DM), src, ACT.Copy)
                        else:
                            ins = A_({"fk": fk, "fq": fq, "fv": fv}[sec][0:r, u, CW * cc:CW * (cc + 1)], src, ACT.Copy)
                    s(ins, sem("unit_free_a"))
                if sec == "fv":
                    pass

            act.wait_ge(sem("x_in"), 48)
            for t in range(3):
                r = ROWS[t]
                s(A_(fm[0:r, base_gb:base_gb + D], xt[0:r, t, :], ACT.Square, accum_out=small[0:r, t:t + 1]), sem("x_squared"))
            act.wait_ge(sem("x_var"), 1)
            s(A_(small[:, 6:9], small[:, 3:6], ACT.Sqrt), sem("x_rooted"))
            split_hi(0)
            for n in range(6):
                t, half = n // 2, n % 2
                act.wait_ge(sem("xT_full"), n + 1)
                r = ROWS[t]
                s(A_(r1[0][:, 4 * half:4 * half + 4, TILE0[t]:TILE0[t] + r],
                     cube(bank[3 + n % 2][:, :], 4)[:, :, 0:r], ACT.Copy), sem("xT_hi"))
            split_hi(1)

            def gate_exps():
                act.wait_ge(sem("gate_abs"), 1)
                s(A_(lf, cum, ACT.Exp, scale=-1.0))
                s(A_(lf, lf, ACT.Ln, bias=1.0), sem("gate_ln"))

            gate_exps()
            act.wait_ge(sem("consts"), 1)

            def G(st):
                if st[1] == 4:
                    act.wait_ge(sem("gate_args"), 1)
                    s(A_(ew, ew, ACT.Exp), sem("gate_exp"))
                    for t in range(3):
                        r = ROWS[t]
                        for h in range(HM):
                            ins = A_(W[0:r, t, h, 0:r], W[0:r, t, h, 0:r], ACT.Exp, bias=aa[0:r, t, h:h + 1])
                            if (t, h) == (2, HM - 1):
                                s(ins, sem("gate_W"))

            def KT(st):
                t = st[1]
                for i, b in enumerate((6, 7)):
                    got(st, b)
                    dst = kM01[:, t, 512 * i:512 * (i + 1)] if t < 2 else kM2[0:NS, 512 * i:512 * (i + 1)]
                    done(A_(dst, bank[b][0:ROWS[t], 0:512], ACT.Copy), b)

            def P1(st):
                _, c, h = st
                n = c * HM + h
                if n == 0:
                    act.wait_ge(sem("gate_exp"), 1)
                if n >= 2:
                    pe_past(("P2", (n - 2) // HM, (n - 2) % HM))
                s(A_(kw[n % 2], kM(c, h), ACT.Copy, scale=ew[:, c, 8 + h:9 + h]), sem("kw_ready"))

            def take_inter(st, c, h, n):
                got(st, 5)
                r = ROWS[c]
                if n >= 1:
                    act.wait_ge(sem("inter_used"), n)
                ins = A_(inter[0:r, :], bank[5][0:r, 0:DE], ACT.Copy, scale=ew[0:r, c, h:h + 1])
                done(ins, 5)

            def P2(st):
                _, c, h = st
                if c == 1:
                    take_inter(st, c, h, h)

            def F1(st):
                t = st[1]
                r = ROWS[t]
                act.wait_ge(sem("num_full"), HM * (t + 1))
                for h in range(HM):
                    s(A_(hv[0:r, 0:DM], num[0:r, h, 0:DM], ACT.Square, accum_out=small[0:r, 20 + h:21 + h]))
                s(A_(small[0:r, 24:28], small[0:r, 20:24], ACT.Copy), sem("num_squared"))
                act.wait_ge(sem("num_var"), t + 1)
                s(A_(small[0:r, 36:40], small[0:r, 32:36], ACT.Sqrt), sem("num_rooted"))

            def F2(st):
                t = st[1]
                r = ROWS[t]
                for i, b in enumerate((6, 7)):
                    act.wait_ge(sem("hv_full"), 2 * t + i + 1)
                    s(A_(r2[0][:, 4 * i:4 * i + 4, TILE0[t]:TILE0[t] + r], cube(hv, 4)[:, :, 0:r], ACT.Copy),
                      sem("ha_hi"))

            def SA(st):
                h = st[1]
                n = 2 * HM + h
                pe_past(("P2", 1, HM - 2 + h) if h < 2 else ("SB", h - 2, BS - 1))
                s(A_(kw[n % 2][0:NS, :], kM(2, h), ACT.Copy, scale=ew[0:NS, 2, 8 + h:9 + h]), sem("kw_ready"))

            def SB(st):
                _, h, b = st
                n = h * BS + b
                if n >= 2:
                    pe_past(("SB", (n - 2) // BS, (n - 2) % BS))
                s(A_(kwm[n % 2][0:NS, :], kw[h % 2][0:NS, :], ACT.Copy, scale=blk8[0:NS, b:b + 1]), sem("kwm_ready"))
                if b == BS - 1:
                    take_inter(st, 2, h, HM + h)

            def N1(st):
                _, w, t = st
                r = ROWS[t]
                src = (fk, fq)[w]
                if w == 0 and t == 0:
                    pass
                n = 3 * w + t
                if n >= 1:
                    act.wait_ge(sem("sq_summed"), n)
                s(A_(sqt[0:r, :], src[0:r, t, :], ACT.Square), sem("squared"))
                act.wait_ge(sem("qk_var"), n + 1)
                s(A_(small[0:r, 60:68], small[0:r, 52:60], ACT.Sqrt), sem("qk_rooted"))

            def N2(st):
                _, w, t = st
                r = ROWS[t]
                for i, b in enumerate((6, 7)):
                    got(st, b)
                    ins = A_((fkT, fqT)[w][:, 4 * i:4 * i + 4, TILE0[t]:TILE0[t] + r],
                             cube(bank[b][:, :], 4)[:, :, 0:r], ACT.Copy)
                    done(ins, b)
                    s(A_(small[0:1, 95:96], small[0:1, 95:96], ACT.Copy), sem("t_copied"))

            def FP1(st):
                h = st[1]
                act.wait_ge(sem("fp_max"), h + 1)
                if h >= 1:
                    pe_past(("FP2", h - 1, 0))
                s(A_(Pp[:, 0:128], sS[:, 0:128], ACT.Exp, bias=small[:, 42:43], accum_out=small[:, 44:45]))
                s(A_(Pp[:, 128:384], sS[:, 128:384], ACT.Exp, bias=small[:, 43:44], accum_out=small[:, 45:46]),
                  sem("fp_exp"))

            def FP2(st):
                h = st[1]
                got(st, 5)
                if h >= 1:
                    pe_past(("FP3", h - 1, 0))
                ins = A_(PT, bank[5][:, 0:384], ACT.Copy)
                done(ins, 5)
                s(A_(small[0:1, 95:96], small[0:1, 95:96], ACT.Copy), sem("fp_pt"))

            def FS1(st):
                b = st[1]
                act.wait_ge(sem("fs_max"), b + 1)
                if b >= 1:
                    pe_past(("FS2", b - 1, 0))
                q = NS
                s(A_(Ps[0:q, 0:PAST], bank[3][0:q, 0:PAST], ACT.Exp, bias=small[0:q, 71:72],
                     accum_out=small[0:q, 72:73]))
                done(A_(Ps[0:q, PAST + TS * b:PAST + TS * (b + 1)], bank[3][0:q, PAST:KEYS], ACT.Exp,
                        bias=small[0:q, 71:72], accum_out=small[0:q, 73:74]), 3)
                s(A_(small[0:1, 95:96], small[0:1, 95:96], ACT.Copy), sem("fs_exp"))

            run = dict(G=G, KT=KT, P1=P1, P2=P2, F1=F1, F2=F2, SA=SA, SB=SB, N1=N1, N2=N2, FP1=FP1, FP2=FP2,
                       FS1=FS1)
            for c in range(NCH):
                evac(c)
                if c + 2 < NCH:
                    split_hi(c + 2)
                for st in AT[c]:
                    if st[0] in run:
                        run[st[0]](st)
                if c == 39:
                    act.wait_ge(sem("o_full"), HF + BS)
                    for k in range(KC):
                        s(A_(r1[0][:, k, :], oT[:, k, :], ACT.Copy), sem("o_hi"))
                if 40 <= c < 44:
                    act.wait_ge(sem("merged"), 2 * (c - 39))
                    for j in (2 * (c - 40), 2 * (c - 40) + 1):
                        s(A_(r2[0][:, j, :], sga[:, j, :], ACT.Copy), sem("m_hi"))

            act.wait_ge(sem("x1_full"), 1)
            for t in range(3):
                r = ROWS[t]
                s(A_(h2[0:r, t, :], x1[0:r, t, :], ACT.Square, accum_out=small[0:r, t:t + 1]), sem("x1_squared"))
            act.wait_ge(sem("x1_var"), 1)
            s(A_(small[:, 6:9], small[:, 3:6], ACT.Sqrt), sem("x1_rooted"))
            for n in range(6):
                t, half = n // 2, n % 2
                r = ROWS[t]
                act.wait_ge(sem("h2T_full"), n + 1)
                s(A_(h2T[:, 4 * half:4 * half + 4, TILE0[t]:TILE0[t] + r], cube(bank[3 + n % 2][:, :], 4)[:, :, 0:r],
                     ACT.Copy), sem("h2T_taken"))
            for t in range(3):
                r = ROWS[t]
                s(A_(h2s[0][0:r, t, :], h2[0:r, t, :], ACT.Copy), sem("h2_hi"))
            act.wait_ge(sem("router_args"), 1)
            s(A_(gexp, gexp, ACT.Exp))
            act.wait_ge(sem("router_args"), 2)
            s(A_(scal[3], scal[2], ACT.Exp), sem("router_exps"))
            act.wait_ge(sem("x1_stored"), 16)
            for n in range(0, 2 * KC, 2):
                k, half = n // 2, n % 2
                act.wait_ge(sem("sorted_full"), n + 1)
                s(A_(xs[:, k, NT * half:NT * (half + 1)], bank[n % 4][:, 0:NT], ACT.Copy), sem("sorted_free_a"))

            def run_experts(base, total):
                def hi(i, u, v, j):
                    act.wait_ge(sem(f"e_raw{u % EB}"), 48 * (i + 1))
                    A_(pair3[j][0], cube(rawm[3 * (u % EB) + j], KC), ACT.Copy).then_inc(sem(f"e_hi{j}"), 1)

                def nxt(i, u, n):
                    return (i, u + n) if u + n < EB else (i + 1, u + n - EB)

                def take_y(v, u):
                    act.wait_ge(sem("e_y_full"), v + 1)
                    if not (isinstance(v, int) and v < 2):
                        act.wait_ge(sem("e_y_stored"), (v - 1) * 16)
                    rows = slice(64 * (u % 2), 64 * (u % 2) + CAP)
                    for j in range(2):
                        ins = A_(yrow[rows, 512 * j:512 * (j + 1)], bank[4 + 2 * (u % 2) + j][0:CAP, :], ACT.Copy)
                    ins.then_inc(sem("e_y_taken"), 1)

                def step(i, u, v, left):
                    act.wait_ge(sem("e_gu_full"), v + 1)
                    A_(tmp[0:CAP, :], bank[u % 2][CAP:2 * CAP, :], ACT.Copy).then_inc(sem("e_low_taken"), 1)
                    act.wait_ge(sem("e_gu"), v + 1)
                    A_(tmp[0:CAP, 0:FE], gu[0:CAP, 0:FE], ACT.Silu).then_inc(sem("e_silu"), 1)
                    if left >= 1:
                        hi(*nxt(i, u, 1), v + 1, 1)
                    if not (isinstance(v, int) and v == base):
                        take_y(v - 1, u + 1)
                    hi(i, u, v, 2)
                    act.wait_ge(sem("e_hT_full"), v + 1)
                    A_(htp[:, :, 0:CAP], cube(bank[2][:, 0:2 * CAP], 2), ACT.Copy).then_inc(sem("e_hT_hi"), 1)
                    if left >= 2:
                        act.wait_ge(sem("e_gate_used"), v + 2)
                        hi(*nxt(i, u, 2), v + 2, 0)

                hi(base // EB, 0, base, 0)
                hi(base // EB, 0, base, 1)
                act.wait_ge(sem("e_gate_used"), base + 1)
                hi(base // EB, 1, base + 1, 0)
                experts(act, base, total, step)
                take_y(base + total - 1, total - 1)

            act.wait_ge(sem("sorted_full"), 2 * KC)
            run_experts(0, NE)
            either(act, lambda: run_experts(NE, NE * JB))

        @block.vector
        def _(dve):
            s = Steps(dve, sem("dve_step"))
            v = nc.vector
            TT, TSC, STT, CP = v.tensor_tensor, v.tensor_scalar, v.scalar_tensor_tensor, v.tensor_copy

            def got(st, b):
                dve.wait_ge(sem(f"bank_full{b}"), fill[st, b] + 1)

            def pe_past(st):
                b = banks_of(st)[-1]
                dve.wait_ge(sem(f"bank_full{b}"), fill[st, b] + 1)

            def done(ins, b):
                s(ins, sem(f"bank_free{b}"))

            def split_lo(c):
                dve.wait_ge(sem("hi_done"), c + 1)
                s(TT(pair[c % 2][1], cube(raw[c % RAW1], KC), pair[c % 2][0], ALU.subtract), sem("split_done"))

            dve.wait_ge(sem("x_squared"), 3)
            s(TSC(small[:, 3:5], small[:, 0:2], 1.0 / D, EPS, ALU.mult, ALU.add))
            s(v.memset(small[:, 5:6], 1.0))
            s(TSC(small[0:NS, 5:6], small[0:NS, 2:3], 1.0 / D, EPS, ALU.mult, ALU.add), sem("x_var"))
            dve.wait_ge(sem("x_rooted"), 1)
            s(v.reciprocal(small[:, 9:12], small[:, 6:9]))
            for t in range(3):
                r = ROWS[t]
                s(STT(xt[0:r, t, :], xt[0:r, t, :], small[0:r, 9 + t:10 + t], g1row[0:r, :], ALU.mult, ALU.mult),
                  sem("xn"))
            dve.wait_ge(sem("small_in"), 64)
            s(CP(wgs[0], cube(wg, KC)))
            s(TT(wgs[1], cube(wg, KC), wgs[0], ALU.subtract), sem("wg_split"))
            split_lo(0)
            for n in range(6):
                t, half = n // 2, n % 2
                dve.wait_ge(sem("xT_hi"), n + 1)
                r = ROWS[t]
                w = (slice(None), slice(4 * half, 4 * half + 4), slice(TILE0[t], TILE0[t] + r))
                s(TT(r1[1][w], cube(bank[3 + n % 2][:, :], 4)[:, :, 0:r], r1[0][w], ALU.subtract), sem("xT_free"))
            split_lo(1)

            dve.wait_ge(sem("gates_full"), 1)
            dve.wait_ge(sem("consts"), 1)
            s(v.memset(gin, 0.0))
            s(TT(gin[:, 0:2, :], cube(bank[7][:, 0:32], 2), bias16.unsqueeze(1).broadcast_to([P, 2, 16]), ALU.add))
            s(TT(gin[0:NS, 2, :], bank[7][0:NS, 32:48], bias16[0:NS, :], ALU.add))
            s(TSC(cum, gin[:, :, 4:16], -1.0, None, ALU.mult))
            s(TT(cum, cum, gin[:, :, 4:16], ALU.max), sem("gate_abs"))
            dve.wait_ge(sem("gate_ln"), 1)
            s(TSC(cum, gin[:, :, 4:16], 0.0, None, ALU.min))
            s(TT(lf, cum, lf, ALU.subtract), sem("gates_out"))
            s(TSC(lfn[0:NS, :].rearrange("p (h t) -> p h t", t=TS),
                  lf[0:NS, 2, HM:HM + HF].unsqueeze(2).broadcast_to([NS, HF, TS]), -1.0, None, ALU.mult))
            s(v.tensor_reduce(maskHT[0:NS, :], mask8[0:NS, :].rearrange("p (b t) -> p t b", t=TS), AX_X, ALU.max),
              sem("lfn_ready"))

            def ident_bc(r):
                return ident[0:r, 0:r].unsqueeze(1).broadcast_to([r, HM, r])

            def diagonals(t, vals):
                r = ROWS[t]
                s(TT(dg[0:r, t, 0:HM * r].rearrange("p (h s) -> p h s", h=HM), ident_bc(r),
                     vals.unsqueeze(2).broadcast_to([r, HM, r]), ALU.mult))

            def gate_tops(t, r):
                s(TT(mtop[0:r, t, 0:HM], amax[0:r, t, :], mprev[0:r, t, :], ALU.max))
                s(TT(mtop[0:r, t, HM:8], mtop[0:r, t, 0:HM], cum[0:r, t, 0:HM], ALU.add))

            def minus_diagonals(t):
                r = ROWS[t]
                s(TSC(small[0:r, 12:16], mtop[0:r, t, 0:HM], -1.0, None, ALU.mult))
                diagonals(t, small[0:r, 12:16])

            def G(st):
                n = st[1]
                if n == 1:
                    got(st, 3)
                    s(CP(cum[:, 0:2, :], cube(bank[3][:, 0:24], 2)))
                    done(CP(cum[0:NS, 2, :], bank[3][0:NS, 24:36]), 3)
                    s(TT(aa, gin[:, :, 0:HM], cum[:, :, 0:HM], ALU.subtract))
                    for t in range(3):
                        diagonals(t, aa[0:ROWS[t], t, :])
                    s(v.memset(small[:, 14:16], 0.0), sem("gate_diag"))
                if n == 2:
                    for t, b in enumerate((4, 5, 6)):
                        r = ROWS[t]
                        got(st, b)
                        p = bank[b][0:r, 0:HM * r].rearrange("p (h s) -> p h s", h=HM)
                        m = (mask if t < 2 else mask8)[0:r, 0:r].unsqueeze(1).broadcast_to([r, HM, r])
                        s(TT(p, p, m, ALU.add))
                        done(v.tensor_reduce(amax[0:r, t, :], p, AX_X, ALU.max), b)
                    gate_tops(0, P)
                    s(v.memset(small[:, 14:16], 0.0), sem("gate_top0"))
                if n == 3:
                    got(st, 3)
                    s(CP(mprev[:, 1, :], bank[3][:, HM:8]))
                    done(CP(lastv[:, 0, :], bank[3][:, 0:8]), 3)
                    got(st, 7)
                    done(CP(mprev[0:NS, 2, :], bank[7][0:NS, 0:HM]), 7)
                    gate_tops(1, P)
                    gate_tops(2, NS)
                    for t in range(3):
                        minus_diagonals(t)
                    s(v.memset(small[:, 14:16], 0.0), sem("gate_tops"))
                if n == 4:
                    got(st, 3)
                    done(CP(lastv[:, 1, :], bank[3][:, 0:8]), 3)
                    got(st, 7)
                    done(CP(lastv[0:NS, 2, :], bank[7][0:NS, 0:8]), 7)
                    s(v.memset(small[:, 14:16], 0.0), sem("m_last"))
                    s(v.memset(ew[NS:P, 2, :], 0.0))
                    for t in range(3):
                        r = ROWS[t]
                        s(TT(ew[0:r, t, 0:4], mprev[0:r, t, :], mtop[0:r, t, 0:HM], ALU.subtract))
                        s(TSC(ew[0:r, t, 4:8], mtop[0:r, t, HM:8], -1.0, None, ALU.mult))
                        s(TT(ew[0:r, t, 8:12], aa[0:r, t, :], lastv[0:r, t, 0:HM], ALU.subtract))
                        s(TT(ew[0:r, t, 12:16], mprev[0:r, t, :], lastv[0:r, t, 0:HM], ALU.subtract))
                    for t, b in enumerate((4, 5, 6)):
                        r = ROWS[t]
                        got(st, b)
                        p = bank[b][0:r, 0:HM * r].rearrange("p (h s) -> p h s", h=HM)
                        m = (maskT if t < 2 else maskT8)[0:r, 0:r].unsqueeze(1).broadcast_to([r, HM, r])
                        done(TT(W[0:r, t, :, 0:r], p, m, ALU.add), b)
                    s(v.memset(small[:, 14:16], 0.0), sem("gate_args"))
                    dve.wait_ge(sem("gate_exp"), 1)
                    s(TT(small[0:NS, 52:84].rearrange("p (b h) -> p b h", b=BS),
                         first8[0:NS, :].unsqueeze(2).broadcast_to([NS, BS, HM]),
                         ew[0:NS, 2, 12:16].unsqueeze(1).broadcast_to([NS, BS, HM]), ALU.mult), sem("decay_rows"))
                if n == 5:
                    got(st, 3)
                    done(CP(dec8, bank[3][:, 0:32]), 3)

            def P1(st):
                _, c, h = st
                n = c * HM + h
                got(st, 3)
                if n == 0:
                    dve.wait_ge(sem("gate_W"), 1)
                if n >= 2:
                    pe_past(("P2", (n - 2) // HM, (n - 2) % HM))
                done(TT(SW[n % 2], bank[3][:, 0:128], W[:, c, h, :], ALU.mult), 3)

            def P2(st):
                _, c, h = st
                got(st, 4)
                if c == 0:
                    done(CP(num[:, h, :], bank[4][:, 0:DE]), 4)
                    s(v.memset(small[0:1, 94:95], 0.0), sem("num_full"))
                else:
                    dve.wait_ge(sem("bank_free5"), fill[st, 5] + 1)
                    done(TT(num[:, h, :], bank[4][:, 0:DE], inter, ALU.add), 4)
                    s(v.memset(small[0:1, 94:95], 0.0), sem("num_full"))
                    s(v.memset(small[0:1, 94:95], 0.0), sem("inter_used"))
                for k, b in enumerate((6, 7)):
                    got(st, b)
                    if c == 0:
                        done(CP(Cx[:, h, k, :], bank[b][:, 0:DE]), b)
                    else:
                        done(STT(Cx[:, h, k, :], Cx[:, h, k, :], ew[:, 1, 12 + h:13 + h], bank[b][:, 0:DE],
                                 ALU.mult, ALU.add), b)
                s(v.memset(small[0:1, 94:95], 0.0), sem("cx_first" if c == 0 else "cx_done"))

            def F1(st):
                t = st[1]
                r = ROWS[t]
                dve.wait_ge(sem("num_squared"), t + 1)
                d = num[0:r, :, DM]
                s(TSC(small[0:r, 28:32], d, -1.0, None, ALU.mult))
                s(TT(small[0:r, 28:32], small[0:r, 28:32], d, ALU.max))
                s(TT(small[0:r, 28:32], small[0:r, 28:32], ew[0:r, t, 4:8], ALU.max))
                s(v.reciprocal(small[0:r, 40:44], small[0:r, 28:32]))
                s(TT(small[0:r, 32:36], small[0:r, 40:44], small[0:r, 40:44], ALU.mult))
                s(TT(small[0:r, 32:36], small[0:r, 32:36], small[0:r, 24:28], ALU.mult))
                s(TSC(small[0:r, 32:36], small[0:r, 32:36], 1.0 / DM, EPS, ALU.mult, ALU.add), sem("num_var"))
                dve.wait_ge(sem("num_rooted"), t + 1)
                s(v.reciprocal(small[0:r, 44:48], small[0:r, 36:40]))
                s(TT(small[0:r, 44:48], small[0:r, 44:48], small[0:r, 40:44], ALU.mult))
                for h in range(HM):
                    s(TSC(num[0:r, h, 0:DM], num[0:r, h, 0:DM], small[0:r, 44 + h:45 + h], None, ALU.mult),
                      sem("num_normed"))

            def F2(st):
                t = st[1]
                r = ROWS[t]
                for i, b in enumerate((6, 7)):
                    got(st, b)
                    w = (slice(None), slice(4 * i, 4 * i + 4), slice(TILE0[t], TILE0[t] + r))
                    done(TT(cube(hv, 4)[:, :, 0:r], cube(bank[b][:, :], 4)[:, :, 0:r], sgm[w], ALU.mult), b)
                    s(v.memset(small[0:1, 94:95], 0.0), sem("hv_full"))
                    dve.wait_ge(sem("ha_hi"), 2 * t + i + 1)
                    s(TT(r2[1][w], cube(hv, 4)[:, :, 0:r], r2[0][w], ALU.subtract), sem("ha_split"))

            def SA(st):
                h = st[1]
                got(st, 3)
                n = 2 * HM + h
                pe_past(("P2", 1, HM - 2 + h) if h < 2 else ("SB", h - 2, BS - 1))
                done(TT(SW[n % 2][0:NS, 0:64], bank[3][0:NS, 0:64], W[0:NS, 2, h, 0:64], ALU.mult), 3)
                if h == 0:
                    s(v.memset(qm, 0.0))
                else:
                    pe_past(("SB", h - 1, BS - 1))
                for k in range(2):
                    s(CP(diag(qm[:, 576 * k:576 * (k + 1)]), qT[:, 2 * h + k, TP:NT].rearrange("p (b t) -> p b t", t=TS)),
                      sem("qm_full"))

            def SB(st):
                _, h, b = st
                n = h * BS + b
                if n >= 2:
                    dve.wait_ge(sem(f"cout_out{n % 2}"), 16 * (n // 2))
                for k, bk in enumerate((6, 7)):
                    got(st, bk)
                    done(STT(Cout[n % 2][:, k, :], Cin[n % 3][:, k, :], dec8[:, HM * b + h:HM * b + h + 1],
                             bank[bk][:, 0:DE], ALU.mult, ALU.add), bk)
                s(v.memset(small[0:1, 94:95], 0.0), sem("cout_full"))
                s(v.memset(small[0:1, 94:95], 0.0), sem("cin_used"))
                if b == BS - 1:
                    got(st, 4)
                    dve.wait_ge(sem("bank_free5"), fill[st, 5] + 1)
                    done(TT(num[0:NS, h, :], bank[4][0:NS, 0:DE], inter[0:NS, :], ALU.add), 4)
                    s(v.memset(small[0:1, 94:95], 0.0), sem("num_full"))
                    s(v.memset(small[0:1, 94:95], 0.0), sem("inter_used"))

            def N1(st):
                _, w, t = st
                r = ROWS[t]
                src = (fk, fq)[w]
                n = 3 * w + t
                dve.wait_ge(sem("squared"), n + 1)
                s(v.tensor_reduce(small[0:r, 52:60], cube(sqt[0:r, :], HF), AX_X, ALU.add), sem("sq_summed"))
                s(TSC(small[0:r, 52:60], small[0:r, 52:60], 1.0 / DF, EPS, ALU.mult, ALU.add), sem("qk_var"))
                dve.wait_ge(sem("qk_rooted"), n + 1)
                s(v.reciprocal(small[0:r, 68:76], small[0:r, 60:68]))
                x3 = cube(src[0:r, t, :], HF)
                s(TT(x3, x3, small[0:r, 68:76].unsqueeze(2).broadcast_to([r, HF, DF]), ALU.mult))
                if n == 0:
                    dve.wait_ge(sem("qk_gain_in"), 32)
                    s(TSC(gq, gq, DF ** -0.5, None, ALU.mult))
                g = (gk, gq)[w][0:r, :].unsqueeze(1).broadcast_to([r, HF, DF])
                s(TT(x3, x3, g, ALU.mult), sem("k_normed" if w == 0 else "q_normed"))

            def FP1(st):
                h = st[1]
                got(st, 3)
                if h >= 1:
                    dve.wait_ge(sem("fp_exp"), h)
                done(TT(sS[:, 0:128], bank[3][:, 0:128], mask, ALU.add), 3)
                got(st, 4)
                s(CP(sS[:, 128:256], bank[4][:, 0:128]))
                done(TT(sS[:, 256:384], bank[4][:, 128:256], mask, ALU.add), 4)
                s(v.tensor_reduce(small[:, 40:41], sS[:, 0:128], AX_X, ALU.max))
                s(v.tensor_reduce(small[:, 41:42], sS[:, 128:384], AX_X, ALU.max))
                s(TSC(small[:, 42:44], small[:, 40:42], -1.0, None, ALU.mult), sem("fp_max"))
                dve.wait_ge(sem("fp_exp"), h + 1)
                s(v.reciprocal(small[:, 46:48], small[:, 44:46]))
                s(TSC(Pp[:, 0:128], Pp[:, 0:128], small[:, 46:47], None, ALU.mult))
                s(TSC(Pp[:, 128:384], Pp[:, 128:384], small[:, 47:48], None, ALU.mult), sem("fp_prob"))

            def FP3(st):
                h = st[1]
                got(st, 6)
                done(CP(oT[:, h, 0:TP], bank[6][:, 0:TP]), 6)
                s(v.memset(small[0:1, 94:95], 0.0), sem("o_full"))

            def FS1(st):
                b = st[1]
                q = NS
                if b == 0:
                    dve.wait_ge(sem("att_zeroed"), 1)
                else:
                    pe_past(("FS1", b - 1, 0))
                new = slice(TP + TS * b, TP + TS * (b + 1))
                s(CP(KTc[:, :, PAST:KEYS], fkT[:, :, new]))
                s(CP(diag(qms), fqT[:, :, new]))
                dve.wait_ge(sem(f"values_in{b % 2}"), 16 * 2 * NPAGES * (b // 2 + 1))
                w = slice(2 * (b % 2), 2 * (b % 2) + 2)
                s(CP(lfe[:, w, :].rearrange("p j (h t) -> p j h t", t=TS),
                     lfp[:, w, :].unsqueeze(3).broadcast_to([P, 2, HF, TS])), sem("fs_ready"))
                got(st, 3)
                s(TT(bank[3][0:q, PAST:KEYS], bank[3][0:q, PAST:KEYS], maskHT[0:q, :], ALU.add))
                s(v.tensor_reduce(small[0:q, 70:71], bank[3][0:q, 0:KEYS], AX_X, ALU.max))
                s(TSC(small[0:q, 71:72], small[0:q, 70:71], -1.0, None, ALU.mult))
                if b >= 1:
                    pe_past(("FS2", b - 1, 0))
                    s(v.memset(Ps[0:q, PAST + TS * (b - 1):PAST + TS * b], 0.0))
                s(v.memset(small[0:1, 94:95], 0.0), sem("fs_max"))
                dve.wait_ge(sem("fs_exp"), b + 1)
                s(TT(small[0:q, 74:75], small[0:q, 72:73], small[0:q, 73:74], ALU.add))
                s(v.reciprocal(small[0:q, 75:76], small[0:q, 74:75]))
                s(TSC(Ps[0:q, :], Ps[0:q, :], small[0:q, 75:76], None, ALU.mult), sem("fs_prob"))

            def FS2(st):
                b = st[1]
                got(st, 5)
                if b >= 1:
                    pe_past(("FS3", b - 1, 0))
                for j in range(2):
                    s(CP(diag(PTm[:, j, :]), bank[5][:, 64 * j:64 * (j + 1)].rearrange("p (h t) -> p h t", t=TS)))
                done(CP(diag(PTm[0:NS, 2, :]), bank[5][0:NS, 128:192].rearrange("p (h t) -> p h t", t=TS)), 5)
                s(v.memset(small[0:1, 94:95], 0.0), sem("fs_pt"))

            def FS3(st):
                b = st[1]
                got(st, 4)
                if b >= 1:
                    dve.wait_ge(sem("bank_full7"), fill[("FS4", b - 1, 0), 7] + 1)
                done(CP(Ob[0:NS, :], bank[4][0:NS, 0:DF]), 4)
                s(v.memset(small[0:1, 94:95], 0.0), sem("fs_o"))

            def FS4(st):
                b = st[1]
                got(st, 7)
                done(CP(oT[:, :, TP + TS * b:TP + TS * (b + 1)],
                        bank[7][:, 0:64].rearrange("p (h t) -> p h t", t=TS)), 7)
                s(v.memset(small[0:1, 94:95], 0.0), sem("o_full"))

            run = dict(G=G, P1=P1, P2=P2, F1=F1, F2=F2, SA=SA, SB=SB, N1=N1, FP1=FP1, FP3=FP3,
                       FS1=FS1, FS2=FS2, FS3=FS3, FS4=FS4)

            def evac(c):
                sec, cc = SECTIONS[c // CPS], c % CPS
                n0, n = units(c)
                if sec == "mo":
                    dve.wait_ge(sem("unit_free_a"), n0 + 2)
                    for j in (2 * cc, 2 * cc + 1):
                        s(TSC(sgm[:, j, :], sgm[:, j, :], mg[:, j:j + 1], None, ALU.mult))
                if sec not in ("bm", "bf", "out"):
                    return
                for u in range(n):
                    dve.wait_ge(sem("unit_full"), n0 + u + 1)
                    b = (n0 + u) % NRING
                    j = 2 * cc + u
                    if sec == "bm":
                        s(TT(sga[:, j, :], bank[b][:, 0:NT], sga[:, j, :], ALU.mult), sem("unit_free_v"))
                    elif sec == "bf":
                        s(TT(sgb[:, j, :], bank[b][:, 0:NT], sgb[:, j, :], ALU.mult), sem("unit_free_v"))
                        s(TT(sga[:, j, :], sga[:, j, :], sgb[:, j, :], ALU.add), sem("merged"))
                    else:
                        r = ROWS[u]
                        if c == 44 and u == 0:
                            dve.wait_ge(sem("xr_in"), 16 * 5)
                            dve.wait_ge(sem("v_stored"), 32)
                            s(v.memset(x1[NS:P, 2, :], 0.0))
                        w = slice(CW * cc, CW * (cc + 1))
                        s(TT(x1[0:r, u, w], bank[b][0:r, 0:CW], xr[0:r, u, w], ALU.add),
                          sem("x1_full" if (c, u) == (NCH - 1, 2) else "unit_free_v"))

            for c in range(NCH):
                evac(c)
                if c + 2 < NCH:
                    split_lo(c + 2)
                for st in AT[c]:
                    if st[0] in run:
                        run[st[0]](st)
                if c == 39:
                    for k in range(KC):
                        dve.wait_ge(sem("o_hi"), k + 1)
                        s(TT(r1[1][:, k, :], oT[:, k, :], r1[0][:, k, :], ALU.subtract), sem("o_split"))
                    
                if 40 <= c < 44:
                    for j in (2 * (c - 40), 2 * (c - 40) + 1):
                        dve.wait_ge(sem("m_hi"), j + 1)
                        s(TT(r2[1][:, j, :], sga[:, j, :], r2[0][:, j, :], ALU.subtract), sem("m_split"))

            dve.wait_ge(sem("x1_squared"), 3)
            s(TSC(small[:, 3:5], small[:, 0:2], 1.0 / D, EPS, ALU.mult, ALU.add))
            s(v.memset(small[:, 5:6], 1.0))
            s(TSC(small[0:NS, 5:6], small[0:NS, 2:3], 1.0 / D, EPS, ALU.mult, ALU.add), sem("x1_var"))
            dve.wait_ge(sem("x1_rooted"), 1)
            s(v.reciprocal(small[:, 9:12], small[:, 6:9]))
            for t in range(3):
                r = ROWS[t]
                s(STT(h2[0:r, t, :], x1[0:r, t, :], small[0:r, 9 + t:10 + t], g2row[0:r, :], ALU.mult, ALU.mult),
                  sem("h2_full"))
            s(v.memset(gl8, NEG))
            s(v.memset(lg[NS:P, 2, :], 0.0))
            for t in range(3):
                r = ROWS[t]
                dve.wait_ge(sem("h2_hi"), t + 1)
                s(TT(h2s[1][0:r, t, :], h2[0:r, t, :], h2s[0][0:r, t, :], ALU.subtract), sem("h2_split"))
            dve.wait_ge(sem("logits_full"), 1)
            s(TT(lg[:, 0:2, :], cube(bank[5][:, 0:72], 2), rb36.unsqueeze(1).broadcast_to([P, 2, 36]), ALU.add))
            s(TT(lg[0:NS, 2, :], bank[5][0:NS, 72:108], rb36[0:NS, :], ALU.add), sem("router_words"))
            s(CP(gl8[:, :, 0:NG], lg[:, :, 0:NG]))
            gi, ei = (m.rearrange("p (t e) -> p t e", t=3) for m in mxi)
            for t in range(3):
                s(v.max(gtop[:, t, :], gl8[:, t, :]))
                s(v.max_index(gi[:, t, :], gtop[:, t, :], gl8[:, t, :]))
            s(CP(gidx, gi))
            s(TT(gexp, lg[:, :, 0:NG], gtop[:, :, 0:1].broadcast_to([P, 3, NG]), ALU.subtract), sem("router_args"))
            dve.wait_ge(sem("iota_ready"), 1)
            s(TT(ghot, iota[:, 0:NG].unsqueeze(1).broadcast_to([P, 3, NG]), gidx[:, :, 0:1].broadcast_to([P, 3, NG]),
                 ALU.is_equal))
            for t in range(3):
                s(TT(esel[:, t, :].rearrange("p (g e) -> p g e", g=NG),
                     lg[:, t, NG:36].rearrange("p (g e) -> p g e", g=NG),
                     ghot[:, t, :].unsqueeze(2).broadcast_to([P, NG, EPG]), ALU.mult))
                s(v.tensor_reduce(el8[:, t, :], esel[:, t, :].rearrange("p (g e) -> p e g", g=NG), AX_X, ALU.add))
                s(v.max(etop[:, t, :], el8[:, t, :]))
                s(v.max_index(ei[:, t, :], etop[:, t, :], el8[:, t, :]))
            s(CP(eidx, ei))
            s(TT(scal[2], etop[:, :, 1], etop[:, :, 0], ALU.subtract), sem("router_args"))
            for k in range(2):
                s(STT(picks[:, :, k], gidx[:, :, 0], float(EPG), eidx[:, :, k], ALU.mult, ALU.add))
                s(TT(hot[k], iota[:, 0:NE].unsqueeze(1).broadcast_to([P, 3, NE]),
                     picks[:, :, k:k + 1].broadcast_to([P, 3, NE]), ALU.is_equal))
            s(TT(chosen, hot[0], hot[1], ALU.add), sem("chosen"))
            dve.wait_ge(sem("router_exps"), 1)
            s(v.tensor_reduce(scal[0], gexp, AX_X, ALU.add))
            s(TSC(scal[1], scal[3], 1.0, None, ALU.add))
            s(TT(scal[0], scal[0], scal[1], ALU.mult))
            s(v.reciprocal(wts[:, :, 0], scal[0]))
            s(TT(wts[:, :, 1], wts[:, :, 0], scal[3], ALU.mult))
            dve.wait_ge(sem("counted"), 1)
            s(CP(cnts[0:NE, 0:1], bank[7][0:NE, 0:1]), sem("counts_out"))
            s(v.memset(rank[NS:P, 2, :], 0.0))
            dve.wait_ge(sem("offsets_full"), 1)
            s(CP(offs, bank[6][:, 96:96 + NE]))
            s(v.tensor_reduce(scal[5][:, 0:1], bank[6][:, 96 + NE:96 + 2 * NE], AX_X, ALU.max))
            offs3 = offs.unsqueeze(1)
            s(TT(rank[:, 0:2, :], cube(bank[6][:, 0:2 * NE], 2), offs3.broadcast_to([P, 2, NE]), ALU.add))
            s(TT(rank[0:NS, 2, :], bank[6][0:NS, 2 * NE:3 * NE], offs[0:NS, :], ALU.add))
            for k in range(2):
                s(TT(esel, hot[k], rank, ALU.mult))
                s(v.tensor_reduce(picks[:, :, k], esel, AX_X, ALU.add))
            for t in range(3):
                r = ROWS[t]
                s(TSC(onehot[0:r, t, :], iota[0:r, :], picks[0:r, t, 0:1], None, ALU.is_equal))
                s(STT(onehot[0:r, t, :], iota[0:r, :], picks[0:r, t, 1:2], onehot[0:r, t, :], ALU.is_equal, ALU.add),
                  sem("onehot"))
            s(CP(slot_i.rearrange("p (t k) -> p t k", t=3), picks))
            s(CP(flag_i, scal[5][0:1, 0:1]))
            s(CP(off_i, offs[0:1, :]))
            for j in range(JB):
                s(TSC(blkf[0:1, :, j], offs[0:1, :], float(CAP * j), float(SLOTS), ALU.add, ALU.min))
            s(CP(blk_i, blkf[0:1, :, :].rearrange("p e j -> p (e j)")))
            dve.wait_ge(sem("x1_stored"), 16)
            s(v.memset(xs[:, :, SLOTS:XC], 0.0))
            for n in range(1, 2 * KC, 2):
                k, half = n // 2, n % 2
                dve.wait_ge(sem("sorted_full"), n + 1)
                s(CP(xs[:, k, NT * half:NT * (half + 1)], bank[n % 4][:, 0:NT]), sem("sorted_free_v"))
            dve.wait_ge(sem("sorted_free_a"), KC)
            s(v.memset(small[0:1, 94:95], 0.0), sem("xs_ready"))

            def run_experts(base, total):
                def split(u, v, j):
                    dve.wait_ge(sem(f"e_hi{j}"), v + 1)
                    TT(pair3[j][1], cube(rawm[3 * (u % EB) + j], KC), pair3[j][0], ALU.subtract)\
                        .then_inc(sem(f"e_split{j}"), 1)

                def step(i, u, v, left):
                    dve.wait_ge(sem("e_low_taken"), v + 1)
                    TT(gu[0:CAP, :], bank[u % 2][0:CAP, :], tmp[0:CAP, :], ALU.add).then_inc(sem("e_gu"), 1)
                    dve.wait_ge(sem("e_silu"), v + 1)
                    TT(tmp[0:CAP, FE:2 * FE], tmp[0:CAP, 0:FE], gu[0:CAP, FE:2 * FE], ALU.mult).then_inc(sem("e_hact"), 1)
                    if left >= 1:
                        split(u + 1, v + 1, 1)
                    split(u, v, 2)
                    dve.wait_ge(sem("e_hT_hi"), v + 1)
                    TT(htp[:, :, CAP:2 * CAP], cube(bank[2][:, 0:2 * CAP], 2), htp[:, :, 0:CAP], ALU.subtract)\
                        .then_inc(sem("e_hT_split"), 1)
                    if left >= 2:
                        split(u + 2, v + 2, 0)

                split(0, base, 0)
                split(0, base, 1)
                split(1, base + 1, 0)
                experts(dve, base, total, step)

            run_experts(0, NE)
            either(dve, lambda: run_experts(NE, NE * JB))
            dve.wait_ge(sem("xe_in"), 16)
            for t in range(3):
                r = ROWS[t]
                dve.wait_ge(sem(f"gathered{t}"), 32)
                for k in range(2):
                    s(STT(xe[0:r, t, :], gat[2 * t + k][0:r, :], wts[0:r, t, k:k + 1], xe[0:r, t, :], ALU.mult, ALU.add),
                      sem("y_done") if k else None)

        @block.tensor
        def _(pe):
            mm = nc.tensor.matmul
            n_act = units(SECTIONS.index("bm") * CPS)[0]

            def claim(st, b):
                if fill[st, b]:
                    pe.wait_ge(sem(f"bank_free{b}"), fill[st, b])

            def full(ins, b):
                ins.then_inc(sem(f"bank_full{b}"), 1)

            def dense(c):
                sec, cc = SECTIONS[c // CPS], c % CPS
                pe.wait_ge(sem("split_done"), c + 1)
                hi, lo = pair[c % 2]
                x = r1 if sec not in ("bm", "out") else r2
                if c == 0:
                    pe.wait_ge(sem("xT_free"), 6)
                if sec == "bm" and cc == 0:
                    pe.wait_ge(sem("ha_split"), 6)
                if sec == "bf" and cc == 0:
                    pe.wait_ge(sem("o_split"), KC)
                if sec == "out" and cc == 0:
                    pe.wait_ge(sem("m_split"), KC)
                n0, n = units(c)
                for u in range(n):
                    m = n0 + u - NRING
                    if m >= n_act:
                        pe.wait_ge(sem("unit_free_v"), m - n_act + 1)
                    elif m >= 0:
                        pe.wait_ge(sem("unit_free_a"), m + 1)
                    b = (n0 + u) % NRING
                    for k in range(KC):
                        for i, (w, a) in enumerate(((hi, x[0]), (hi, x[1]), (lo, x[0]))):
                            first, final = k == 0 and i == 0, k == KC - 1 and i == 2
                            if sec in BY_FEATURE:
                                ins = mm(bank[b][:, 0:NT], w[:, k, P * u:P * (u + 1)], a[:, k, :],
                                         start=first, stop=final)
                            else:
                                r = ROWS[u]
                                ins = mm(bank[b][0:r, 0:CW], a[:, k, TILE0[u]:TILE0[u] + r], w[:, k, :],
                                         start=first, stop=final)
                    ins.then_inc(sem("unit_full"), 1)

            pe.wait_ge(sem("consts"), 1)
            for n in range(6):
                t, half = n // 2, n % 2
                r = ROWS[t]
                pe.wait_ge(sem("xn"), t + 1)
                if n >= 2:
                    pe.wait_ge(sem("xT_free"), n - 1)
                for i in range(4):
                    k = 4 * half + i
                    ins = nc.tensor.transpose(bank[3 + n % 2][:, P * i:P * i + r], xt[0:r, t, P * k:P * (k + 1)],
                                              ident[0:r, 0:r])
                ins.then_inc(sem("xT_full"), 1)
            pe.wait_ge(sem("xT_free"), 6)
            pe.wait_ge(sem("wg_split"), 1)
            for t in range(3):
                r = ROWS[t]
                for k in range(KC):
                    for i, (w, a) in enumerate(((0, 0), (0, 1), (1, 0))):
                        ins = mm(bank[7][0:r, 16 * t:16 * t + 16], r1[a][:, k, TILE0[t]:TILE0[t] + r], wgs[w][:, k, :],
                                 start=(k == 0 and i == 0), stop=(k == KC - 1 and i == 2), skip_group_check=True)
            ins.then_inc(sem("gates_full"), 1)

            def G(st):
                n = st[1]
                if n == 1:
                    pe.wait_ge(sem("gates_out"), 1)
                    for t in range(3):
                        r = ROWS[t]
                        ins = mm(bank[3][0:r, 12 * t:12 * t + 12], (upto if t < 2 else upto8)[0:r, 0:r], lf[0:r, t, :],
                                 start=True, stop=True, skip_group_check=True)
                    full(ins, 3)
                if n == 2:
                    pe.wait_ge(sem("gate_diag"), 1)
                    for t, b in enumerate((4, 5, 6)):
                        r = ROWS[t]
                        full(mm(bank[b][0:r, 0:HM * r], ones[0:r, 0:r], dg[0:r, t, 0:HM * r], start=True, stop=True), b)
                if n == 3:
                    pe.wait_ge(sem("gate_top0"), 1)
                    claim(st, 3)
                    full(mm(bank[3][:, 0:8], last, mtop[:, 0, :], start=True, stop=True), 3)
                    claim(st, 7)
                    full(mm(bank[7][0:NS, 0:HM], e8[0:BS, :], small[0:BS, 90:94], start=True, stop=True), 7)
                if n == 4:
                    pe.wait_ge(sem("gate_tops"), 1)
                    claim(st, 3)
                    full(mm(bank[3][:, 0:8], last, mtop[:, 1, :], start=True, stop=True), 3)
                    claim(st, 7)
                    full(mm(bank[7][0:NS, 0:8], last8[0:NS, :], mtop[0:NS, 2, :], start=True, stop=True), 7)
                    for t, b in enumerate((4, 5, 6)):
                        r = ROWS[t]
                        claim(st, b)
                        full(mm(bank[b][0:r, 0:HM * r], ones[0:r, 0:r], dg[0:r, t, 0:HM * r], start=True, stop=True), b)
                if n == 5:
                    pe.wait_ge(sem("decay_rows"), 1)
                    claim(st, 3)
                    full(mm(bank[3][:, 0:32], ones[0:NS, :], small[0:NS, 52:84], start=True, stop=True), 3)

            def KT(st):
                t = st[1]
                r = ROWS[t]
                if t == 0:
                    pe.wait_ge(sem("unit_free_a"), 2 * CPS)
                for i, b in enumerate((6, 7)):
                    claim(st, b)
                    for j in range(4):
                        ins = nc.tensor.transpose(bank[b][0:r, P * j:P * (j + 1)],
                                                  kT[:, 4 * i + j, TILE0[t]:TILE0[t] + r], ident)
                    full(ins, b)

            def scores(b, c, h):
                r, w = ROWS[c], slice(TILE0[c], TILE0[c] + ROWS[c])
                for k in range(2):
                    ins = mm(bank[b][0:r, 0:r], kT[:, 2 * h + k, w], qT[:, 2 * h + k, w], start=(k == 0), stop=(k == 1))
                full(ins, b)

            def P1(st):
                _, c, h = st
                if c == 0:
                    pe.wait_ge(sem("unit_free_a"), 2 * 2 * CPS + 3 * (h + 1))
                claim(st, 3)
                scores(3, c, h)

            def P2(st):
                _, c, h = st
                n = c * HM + h
                if c == 1:
                    pe.wait_ge(sem("cx_first"), h + 1)
                    claim(st, 5)
                    for k in range(2):
                        ins = mm(bank[5][:, 0:DE], qT[:, 2 * h + k, P:2 * P], Cx[:, h, k, :], start=(k == 0), stop=(k == 1))
                    full(ins, 5)
                pe.wait_ge(sem("bank_free3"), fill[("P1", c, h), 3] + 1)
                claim(st, 4)
                full(mm(bank[4][:, 0:DE], SW[n % 2], vx(c, h), start=True, stop=True), 4)
                pe.wait_ge(sem("kw_ready"), n + 1)
                for k, b in enumerate((6, 7)):
                    claim(st, b)
                    full(mm(bank[b][:, 0:DE], kw[n % 2][:, P * k:P * (k + 1)], vx(c, h), start=True, stop=True), b)

            def F2(st):
                t = st[1]
                r = ROWS[t]
                for i, b in enumerate((6, 7)):
                    claim(st, b)
                    for j in range(4):
                        k = 4 * i + j
                        if j % 2 == 0:
                            pe.wait_ge(sem("num_normed"), HM * t + k // 2 + 1)
                        ins = nc.tensor.transpose(bank[b][:, P * j:P * j + r],
                                                  num[0:r, k // 2, P * (k % 2):P * (k % 2 + 1)], ident[0:r, 0:r])
                    full(ins, b)

            def SA(st):
                _, h, _ = st
                claim(st, 3)
                scores(3, 2, h)

            def SB(st):
                _, h, b = st
                n = h * BS + b
                if b == 0:
                    claim(("SB", h, BS - 1), 5)
                    pe.wait_ge(sem("qm_full"), 2 * (h + 1))
                pe.wait_ge(sem(f"cin_in{n % 3}"), 16 * (n // 3 + 1))
                for k in range(2):
                    ins = mm(bank[5][0:NS, 0:DE], qm[:, 576 * k + 64 * b:576 * k + 64 * (b + 1)], Cin[n % 3][:, k, :],
                             start=(b == 0 and k == 0), stop=(b == BS - 1 and k == 1))
                if b == BS - 1:
                    full(ins, 5)
                    pe.wait_ge(sem("bank_free3"), fill[("SA", h, 0), 3] + 1)
                    claim(st, 4)
                    full(mm(bank[4][0:NS, 0:DE], SW[(2 * HM + h) % 2][0:NS, 0:64], vx(2, h), start=True, stop=True), 4)
                pe.wait_ge(sem("kwm_ready"), n + 1)
                for k, bk in enumerate((6, 7)):
                    claim(st, bk)
                    ins = mm(bank[bk][:, 0:DE], kwm[n % 2][0:NS, P * k:P * (k + 1)], vx(2, h), start=True, stop=True)
                    full(ins, bk)

            def N2(st):
                _, w, t = st
                r = ROWS[t]
                pe.wait_ge(sem(("k_normed", "q_normed")[w]), t + 1)
                for i, b in enumerate((6, 7)):
                    claim(st, b)
                    for j in range(4):
                        ins = nc.tensor.transpose(bank[b][:, P * j:P * j + r],
                                                  (fk, fq)[w][0:r, t, P * (4 * i + j):P * (4 * i + j + 1)],
                                                  ident[0:r, 0:r])
                    full(ins, b)

            def FP1(st):
                h = st[1]
                col = [lf[:, t, HM + h:HM + h + 1].broadcast_to([P, P]) for t in range(2)]
                claim(st, 3)
                mm(bank[3][:, 0:P], fqT[:, h, 0:P], fkT[:, h, 0:P], start=True, stop=False)
                full(mm(bank[3][:, 0:P], col[0], negs[:, 0:P], start=False, stop=True), 3)
                claim(st, 4)
                mm(bank[4][:, 0:TP], fqT[:, h, P:TP], fkT[:, h, 0:TP], start=True, stop=False)
                mm(bank[4][:, 0:TP], col[0], negs, start=False, stop=False)
                full(mm(bank[4][:, P:TP], col[1], negs[:, 0:P], start=False, stop=True), 4)

            def FP2(st):
                h = st[1]
                pe.wait_ge(sem("fp_prob"), h + 1)
                claim(st, 5)
                for j in range(3):
                    ins = nc.tensor.transpose(bank[5][:, P * j:P * (j + 1)], Pp[:, P * j:P * (j + 1)], ident)
                full(ins, 5)

            def FP3(st):
                h = st[1]
                pe.wait_ge(sem("fp_pt"), h + 1)
                claim(st, 6)
                mm(bank[6][:, 0:TP], fv[:, 0, DF * h:DF * (h + 1)], PT[:, 0:TP], start=True, stop=False)
                full(mm(bank[6][:, P:TP], fv[:, 1, DF * h:DF * (h + 1)], PT[:, TP:TP + P], start=False, stop=True), 6)

            def FS1(st):
                b = st[1]
                q = NS
                pe.wait_ge(sem("fs_ready"), b + 1)
                pe.wait_ge(sem("keys_in"), 16 * NPAGES * (b + 1))
                claim(st, 3)
                for h in range(HF):
                    mm(bank[3][0:q, 0:KEYS], qms[:, 64 * h:64 * (h + 1)], KTc[:, h, :], start=(h == 0), stop=False)
                l0, l1 = lfe[:, 2 * (b % 2), :], lfe[:, 2 * (b % 2) + 1, :]
                mm(bank[3][0:q, 0:P], l0, after, start=False, stop=False)
                mm(bank[3][0:q, 0:P], l1, ones, start=False, stop=False)
                mm(bank[3][0:q, P:2 * P], l1, after, start=False, stop=False)
                full(mm(bank[3][0:q, PAST:KEYS], lfn[0:q, :], upto8[0:q, TS * b:TS * (b + 1)],
                        start=False, stop=True), 3)

            def FS2(st):
                b = st[1]
                pe.wait_ge(sem("fs_prob"), b + 1)
                claim(st, 5)
                for j, w in enumerate((P, P, NS)):
                    ins = nc.tensor.transpose(bank[5][0:w, 64 * j:64 * (j + 1)], Ps[0:NS, P * j:P * j + w],
                                              ident[0:NS, 0:NS])
                full(ins, 5)

            def FS3(st):
                b = st[1]
                pe.wait_ge(sem("fs_pt"), b + 1)
                claim(st, 4)
                for h in range(HF):
                    for j in range(3):
                        r = P if j < 2 else NS
                        rhs = (Vc[b % 2][:, j, DF * h:DF * (h + 1)] if j < 2 else fv[0:NS, 2, DF * h:DF * (h + 1)])
                        ins = mm(bank[4][0:NS, 0:DF], PTm[0:r, j, 64 * h:64 * (h + 1)], rhs,
                                 start=(h == 0 and j == 0), stop=(h == HF - 1 and j == 2))
                full(ins, 4)

            def FS4(st):
                b = st[1]
                pe.wait_ge(sem("fs_o"), b + 1)
                claim(st, 7)
                full(nc.tensor.transpose(bank[7][:, 0:64], Ob[0:NS, :], ident[0:NS, 0:NS]), 7)

            run = dict(G=G, KT=KT, P1=P1, P2=P2, F2=F2, SA=SA, SB=SB, N2=N2, FP1=FP1, FP2=FP2, FP3=FP3,
                       FS1=FS1, FS2=FS2, FS3=FS3, FS4=FS4)
            for c in range(NCH):
                dense(c)
                for st in AT[c]:
                    if st[0] in run:
                        run[st[0]](st)

            for n in range(6):
                t, half = n // 2, n % 2
                r = ROWS[t]
                pe.wait_ge(sem("h2_full"), t + 1)
                if n >= 2:
                    pe.wait_ge(sem("h2T_taken"), n - 1)
                for i in range(4):
                    k = 4 * half + i
                    ins = nc.tensor.transpose(bank[3 + n % 2][:, P * i:P * i + r], h2[0:r, t, P * k:P * (k + 1)],
                                              ident[0:r, 0:r])
                ins.then_inc(sem("h2T_full"), 1)
            pe.wait_ge(sem("h2T_taken"), 6)
            for t in range(3):
                r = ROWS[t]
                for k in range(KC):
                    ins = mm(bank[5][0:r, 36 * t:36 * (t + 1)], h2T[:, k, TILE0[t]:TILE0[t] + r], wr3[:, k, :],
                             start=(k == 0), stop=(k == KC - 1), skip_group_check=True)
            ins.then_inc(sem("logits_full"), 1)
            pe.wait_ge(sem("chosen"), 1)
            for t in range(3):
                r = ROWS[t]
                ins = mm(bank[7][0:NE, 0:1], chosen[0:r, t, :], ones[0:r, 0:1], start=(t == 0), stop=(t == 2))
            ins.then_inc(sem("counted"), 1)
            for t in range(3):
                r = ROWS[t]
                for e in range(t):
                    mm(bank[6][0:r, NE * t:NE * (t + 1)], ones[:, 0:r], chosen[:, e, :], start=(e == 0), stop=False,
                       skip_group_check=True)
                mm(bank[6][0:r, NE * t:NE * (t + 1)], before[0:r, 0:r], chosen[0:r, t, :], start=(t == 0), stop=True,
                   skip_group_check=True)
            for t in range(3):
                r = ROWS[t]
                mm(bank[6][:, 128:160], ones[0:r, :], chosen[0:r, t, :], start=(t == 0), stop=(t == 2),
                   skip_group_check=True)
            pe.wait_ge(sem("counts_out"), 1)
            mm(bank[6][:, 96:96 + NE], cnts[0:NE, 0:1].broadcast_to([NE, P]), before[0:NE, 0:NE], start=True, stop=True,
               skip_group_check=True).then_inc(sem("offsets_full"), 1)
            pe.wait_ge(sem("h2_split"), 3)
            pe.wait_ge(sem("onehot"), 3)
            for n in range(2 * KC):
                k, half = n // 2, n % 2
                if n >= 4:
                    pe.wait_ge(sem(("sorted_free_a", "sorted_free_v")[half]), n // 2 - 1)
                for t in range(3):
                    r = ROWS[t]
                    for i in range(2):
                        ins = mm(bank[n % 4][:, 0:NT], h2s[i][0:r, t, P * k:P * (k + 1)],
                                 onehot[0:r, t, NT * half:NT * (half + 1)], start=(t == 0 and i == 0),
                                 stop=(t == 2 and i == 1))
                ins.then_inc(sem("sorted_full"), 1)

            def run_experts(base, total):
                def gate_up(v, u, j, between=None):
                    if j == 0:
                        pe.wait_ge(sem("e_packed"), v + 1)
                        if not (isinstance(v, int) and v < 2):
                            pe.wait_ge(sem("e_gu"), v - 1)
                    pe.wait_ge(sem(f"e_split{j}"), v + 1)
                    for k in range(KC):
                        for i in range(2):
                            ins = mm(bank[u % 2][:, FE * j:FE * (j + 1)], pack[u % 2][:, k, :], pair3[j][i][:, k, :],
                                     start=(k == 0 and i == 0), stop=(k == KC - 1 and i == 1), skip_group_check=True)
                        if k == 0 and between:
                            between()
                    ins.then_inc(sem("e_gu_full" if j else "e_gate_used"), 1)

                def step(i, u, v, left):
                    def transposes():
                        for j in range(2):
                            ins = nc.tensor.transpose(bank[2][:, CAP * j:CAP * (j + 1)],
                                                      tmp[0:CAP, FE + P * j:FE + P * (j + 1)], ident[0:CAP, 0:CAP])
                        ins.then_inc(sem("e_hT_full"), 1)

                    if left >= 1:
                        gate_up(v + 1, u + 1, 0)
                        pe.wait_ge(sem("e_hact"), v + 1)
                        gate_up(v + 1, u + 1, 1, transposes)
                    else:
                        pe.wait_ge(sem("e_hact"), v + 1)
                        transposes()
                    pe.wait_ge(sem("e_split2"), v + 1)
                    pe.wait_ge(sem("e_hT_split"), v + 1)
                    if not (isinstance(v, int) and v < 2):
                        pe.wait_ge(sem("e_y_taken"), v - 1)
                    for j in range(2):
                        for k in range(2):
                            for n, (a, w) in enumerate(((0, 0), (0, 1), (1, 0))):
                                ins = mm(bank[4 + 2 * (u % 2) + j][0:CAP, :], htp[:, k, CAP * a:CAP * (a + 1)],
                                         down[w][:, k, 512 * j:512 * (j + 1)], start=(k == 0 and n == 0),
                                         stop=(k == 1 and n == 2))
                    ins.then_inc(sem("e_y_full"), 1)

                gate_up(base, 0, 0)
                gate_up(base, 0, 1)
                experts(pe, base, total, step)

            run_experts(0, NE)
            either(pe, lambda: run_experts(NE, NE * JB))


def kernel(**inputs):
    import numpy as np
    import concourse.bacc as bacc
    from concourse.bass_utils import run_bass_kernel_spmd

    x = {k: np.ascontiguousarray(v) for k, v in inputs.items()}
    w_in = x["w_in"][0]
    widths = (1024, 1024, 1024, 1024, HM, HM, 1024, 1024, 1024, HF, 1024, 1024)
    cuts = np.cumsum((0,) + widths)
    part = dict(zip(("mq", "mk", "mv", "mo", "mi", "mf", "fq", "fk", "fv", "ff", "ga", "gb"),
                    (w_in[:, a:b] for a, b in zip(cuts[:-1], cuts[1:]))))
    part |= {"bm": x["w_branch_mlstm"][0], "bf": x["w_branch_fox"][0], "out": x["w_out"][0]}

    def by_partition(w):
        return np.ascontiguousarray(w.reshape(-1, P, w.shape[-1]).transpose(1, 0, 2))

    dense = np.stack([by_partition(part[s][:, CW * c:CW * (c + 1)]).reshape(P, UN) for s in SECTIONS for c in range(CPS)])
    moe = np.stack([by_partition(x[w][0, e]).reshape(P, UN) for e in range(NE) for w in ("w_gate", "w_up", "w_down")])
    xp = x["x_prompt"][0]
    state = np.concatenate([x["state_C"][0], x["state_n"][0][..., None]], axis=-1)
    arrays = {
        "x_prompt": by_partition(xp), "x_sample": x["x_sample"].reshape(NS, D),
        "norm1_g": x["norm1_g"][0], "norm2_g": x["norm2_g"][0],
        "w_dense": dense, "w_moe": moe,
        "w_gates": by_partition(np.concatenate([part["mi"], part["mf"], part["ff"]], axis=1)).reshape(P, 128),
        "b_gates": np.concatenate([x["b_igate"][0], x["b_fgate_mlstm"][0], x["b_fgate_fox"][0]]),
        "mlstm_norm_g": np.ascontiguousarray(x["mlstm_norm_g"][0].reshape(KC, P).T),
        "q_norm_g": x["q_norm_g"][0], "k_norm_g": x["k_norm_g"][0],
        "state_C": np.ascontiguousarray(state.reshape(BS, HM, 2, P, DE).transpose(0, 1, 3, 2, 4)),
        "state_m": x["state_m"][0],
        "cache_kT": np.ascontiguousarray(x["cache_k"][0].transpose(0, 3, 2, 1)),
        "cache_v": x["cache_v"][0].reshape(NPHYS, PAGE, D),
        "cache_lf": x["cache_lf"][0],
        "page_table": x["page_table"].reshape(1, BS * NPAGES).astype(np.int32),
        "w_router": by_partition(np.concatenate([x["w_router_group"][0], x["w_router_expert"][0]], axis=1)).reshape(P, KC * 36),
        "b_router": np.concatenate([x["b_router_group"][0], x["b_router_expert"][0]]),
    }
    outs = {
        "y_prompt": (P, 2, D), "y_sample": (NS, D), "k_prompt": (P, 2, D), "v_prompt": (P, 2, D),
        "lf_prompt": (P, 2, HF), "k_sample": (NS, D), "v_sample": (NS, D), "lf_sample": (NS, HF),
        "C_prompt": (P, HM, 2, DE), "m_prompt": (1, HM), "C_sample": (BS, HM, P, 2, DE), "m_sample": (BS, HM),
    }
    nc = bacc.Bacc("TRN2", target_bir_lowering=False, num_devices=1)
    A = {k: nc.dram_tensor(f"in_{k}", v.shape, mybir.dt.from_np(v.dtype), kind="ExternalInput").ap()
         for k, v in arrays.items()}
    O = {k: nc.dram_tensor(f"out_{k}", s, F32, kind="ExternalOutput").ap() for k, s in outs.items()}
    hybrid_step(nc, A, O)
    r = run_bass_kernel_spmd(nc, [{f"in_{k}": v for k, v in arrays.items()}], core_ids=[0])
    o = {k: r.results[0][f"out_{k}"] for k in outs}

    def rows(a, *shape):
        return np.ascontiguousarray(a.transpose(1, 0, 2)).reshape(shape)

    Cp = np.ascontiguousarray(o["C_prompt"].transpose(1, 2, 0, 3)).reshape(1, 1, HM, DM, DE)
    Cs = np.ascontiguousarray(o["C_sample"].transpose(0, 1, 3, 2, 4)).reshape(1, BS, HM, DM, DE)
    return (rows(o["y_prompt"], 1, TP, D), o["y_sample"].reshape(BS, TS, D),
            rows(o["k_prompt"], 1, 1, TP, HF, DF), rows(o["v_prompt"], 1, 1, TP, HF, DF),
            rows(o["lf_prompt"], 1, 1, TP, HF),
            o["k_sample"].reshape(1, BS, TS, HF, DF), o["v_sample"].reshape(1, BS, TS, HF, DF),
            o["lf_sample"].reshape(1, BS, TS, HF),
            np.ascontiguousarray(Cp[..., :DM]), np.ascontiguousarray(Cp[..., DM]), o["m_prompt"].reshape(1, 1, HM),
            np.ascontiguousarray(Cs[..., :DM]), np.ascontiguousarray(Cs[..., DM]), o["m_sample"].reshape(1, BS, HM))
```

```python
from contextlib import ExitStack

import concourse.bass as bass
from concourse import mybir

ALU = mybir.AluOpType
ACT = mybir.ActivationFunctionType
AX_X = mybir.AxisListType.X
F32 = mybir.dt.float32
F32R = mybir.dt.float32r
I32 = mybir.dt.int32
U32 = mybir.dt.uint32

P = 128
D = 1024
KC = D // P
TP, BS, TS = 256, 8, 8
NS = BS * TS
NT = TP + NS
TILE0 = (0, 128, 256)
ROWS = (128, 128, NS)
HM, DM = 4, 256
DE = DM + 1
HF, DF = 8, 128
PAST, PAGE = 256, 128
KEYS = PAST + TS
NPAGES = PAST // PAGE
NPHYS = BS * NPAGES * 5 // 4
NE, EPG, NG, FE = 32, 8, 4, 256
EPS = 1e-6
NEG = -1e30
CW = 256
UN = KC * CW
SECTIONS = ("mo", "mk", "mq", "mv", "ga", "gb", "fk", "fq", "fv", "bm", "bf", "out")
CPS = D // CW
LAST_ATT = (SECTIONS.index("bm") * CPS + CPS - 1, 0)
LATE = ("SB", "FP3", "FS1", "P1", "P2", "N2")
NCH = len(SECTIONS) * CPS
BY_FEATURE = ("mk", "mq", "mo", "ga", "gb", "bm", "bf")
NRING = 3
CAP = 64
SLOTS = 2 * NT
XC = SLOTS + CAP
RAW1, RAWM = 2, 12
NCOUT = 4
NSPLIT = 4
EB = RAWM // 3
JB = 8
DIAG = TS * HF + TS


def units_of(c):
    return 2 if SECTIONS[c // CPS] in BY_FEATURE else 3


def stages():
    order = [(c, u) for c in range(NCH) for u in range(units_of(c))]
    at = {cu: [] for cu in order}

    def after(section, chunk, unit, n=0):
        return at[order[order.index((CPS * SECTIONS.index(section) + chunk, unit)) + n]]

    for n in range(1, 6):
        after("mo", 0, 1, 2 * (n - 1)).append(("G", n, 0))
    for t in range(3):
        after("mq", 1 + t, 1).append(("KT", t, 0))
    for h in range(HM):
        after("mv", h, 2, 2 if h < HM - 1 else 1).append(("P2", 0, h))
        after("mv", h, 2).append(("P1", 0, h))
    after("ga", 0, 0).append(("F1", 0, 0))
    after("ga", 1, 0).append(("F2", 0, 0))
    for h in range(HM):
        after("ga", 1, 0, h).append(("P2", 1, h))
        after("ga", 0, 1, h).append(("P1", 1, h))
    after("ga", 2, 1).append(("F1", 1, 0))
    after("ga", 3, 0).append(("SA", 0, 0))
    after("ga", 3, 1).append(("F2", 1, 0))
    for h in range(HM):
        for b in range(BS):
            after("ga", 3, 1, 2 * h + b // 4).append(("SB", h, b))
        if h < HM - 1:
            after("gb", 0, 0, 2 * h).append(("SA", h + 1, 0))
    after("gb", 3, 0).append(("F1", 2, 0))
    after("fk", 0, 0).append(("F2", 2, 0))
    for w, section in enumerate(("fk", "fq")):
        for t in range(3):
            after(section, 3, 2, 2 * t).append(("N1", w, t))
            after(section, 3, 2, 2 * t + 4).append(("N2", w, t))
    line = []
    for n in range(HF + 3):
        line.append([(k, n - s, 0) for s, k in ((0, "FS0"), (3, "FS4"), (2, "FS3"), (1, "FS2"), (0, "FS1")) if 0 <= n - s < BS])
        line.append([(k, n - s, 0) for s, k in ((2, "FP3"), (1, "FP2"), (0, "FP1")) if 0 <= n - s < HF])
    room = 2 * CPS - 2
    for n, sts in enumerate(line):
        after("fv", 3, 0, n if n < 4 else 4 + (n - 4) * room // (len(line) - 4)).extend(sts)
    return at


def banks_of(st):
    kind, x, y = st
    if kind == "G":
        return {1: (3,), 2: (4, 5, 6), 3: (3, 7), 4: (3, 7, 4, 5, 6), 5: (3,)}[x]
    if kind == "P2":
        return (4, 6, 7) if x == 0 else (5, 4, 6, 7)
    if kind == "SB":
        return ((5, 4) if y == BS - 1 else ()) + (6, 7)
    return {"KT": (6, 7), "P1": (3,), "F1": (), "F2": (6, 7), "SA": (3,), "N1": (), "N2": (6, 7),
            "FP1": (7, 4), "FP2": (5,), "FP3": (6,), "FS1": (3,), "FS2": (5,), "FS3": (4,), "FS4": (6,), "FS0": ()}[kind]


class Steps:

    def __init__(self, eng, step):
        self.eng, self.step, self.seen = eng, step, {}

    def __call__(self, ins, event=None):
        s = event if event is not None else self.step
        self.seen[s.name] = self.seen.get(s.name, 0) + 1
        ins.then_inc(s, 1)
        self.eng.wait_ge(s, self.seen[s.name])


def hybrid_step(nc, A, O):
    AT = stages()
    fill, count = {}, {b: 0 for b in range(8)}
    for c in range(NCH):
        for u in range(units_of(c)):
            for st in AT[c, u]:
                for b in banks_of(st):
                    fill[st, b] = count[b]
                    count[b] += 1
    ctx = ExitStack()
    with ctx:
        handles = {}

        def sem(name):
            if name not in handles:
                
                handles[name] = ctx.enter_context(nc.semaphore(name))
            return handles[name]

        FW, RW = 33360, 19456
        fm = ctx.enter_context(nc.sbuf_tensor("fm", [P, FW], F32))
        rm = ctx.enter_context(nc.sbuf_tensor("rm", [P, RW], F32R))
        im = ctx.enter_context(nc.sbuf_tensor("im", [P, 56 + NE * JB], I32))
        pt = im[0:1, 0:BS * NPAGES]
        slot_i = im[:, 16:22]
        crowd_i = im[:, 0:6]
        flag_i = im[0:1, 22:23]
        off_i = im[0:1, 24:24 + NE]
        blk_i = im[0:1, 56:56 + NE * JB]
        bank = [ctx.enter_context(nc.psum_tensor(f"bank{b}", [P, 512], F32)) for b in range(8)]
        y_rows = nc.dram_tensor("y_rows", [NE * CAP, D], F32).ap()
        y_crowd = nc.dram_tensor("y_crowd", [NE * JB * CAP, D], F32).ap()
        x1_dram = nc.dram_tensor("x1_rows", [P, 3, D], F32).ap()
        top = [0]

        def take(n):
            top[0] += n
            assert top[0] <= FW, top[0]
            return fm[:, top[0] - n:top[0]]

        def cube(ap, a):
            return ap.rearrange("p (a b) -> p a b", a=a)

        ident, ones, before = take(128), take(128), take(128)
        base_masks = top[0]
        low = fm[:, base_masks:base_masks + CW]
        upto, last, maskT, mask, after = take(128), take(128), take(128), take(128), take(128)
        negs = take(256)
        upto8, maskT8, mask8, last8 = take(64), take(64), take(64), take(64)
        e8, blk8, first8, maskHT = take(64), take(8), take(8), take(8)
        gin = cube(take(48), 3)
        lf = cube(take(36), 3)
        cum = cube(take(36), 3)
        aa = cube(take(12), 3)
        amax = cube(take(12), 3)
        mprev = cube(take(12), 3)
        mtop = cube(take(24), 3)
        lastv = cube(take(24), 3)
        ew = cube(take(48), 3)
        dec8, small, bias16, rb36, lfn = take(32), take(96), take(16), take(36), take(64)
        mg = take(8)
        base_raw = top[0]
        raw = [take(UN) for _ in range(RAW1)]
        sgm = cube(take(KC * NT), KC)
        sga = cube(take(KC * NT), KC)
        base_gb = top[0]
        kM01 = cube(take(2 * D), 2)
        vx01 = take(2 * HM * DE).rearrange("p (t h e) -> p t h e", t=2, h=HM)
        kT = cube(take(KC * NT), KC)
        qT = cube(take(KC * NT), KC)
        kM2 = take(D)
        vx2 = cube(take(HM * DE), HM)
        base_x = top[0]
        Cx = take(HM * 2 * DE).rearrange("p (h c e) -> p h c e", h=HM, c=2)
        Cin = [cube(take(2 * DE), 2) for _ in range(3)]
        Cout = [cube(take(2 * DE), 2) for _ in range(2)] + \
            [cube(fm[:, base_gb + KC * NT + 2 * DE * i:base_gb + KC * NT + 2 * DE * (i + 1)], 2) for i in range(NCOUT - 2)]
        W = take(3 * HM * P).rearrange("p (t h s) -> p t h s", t=3, h=HM)
        base_num = top[0]
        num = cube(take(HM * DE), HM)
        qm = take(2 * BS * DIAG)
        SW = [take(128) for _ in range(2)]
        kw = [take(DM) for _ in range(2)]
        kwm = [take(DM) for _ in range(2)]
        inter = take(DE)
        hv = take(512)
        top[0] = base_x
        xt, g1row = cube(take(3 * D), 3), take(D)
        wg = take(128)
        top[0] = base_num
        dg = cube(take(3 * 512), 3)
        top[0] = base_gb
        sgb = cube(take(KC * NT), KC)
        base_att = top[0]
        fk = cube(take(3 * D), 3)
        fq = cube(take(3 * D), 3)
        fv = cube(take(3 * D), 3)
        fkT = cube(take(HF * NT), HF)
        fqT = cube(take(HF * NT), HF)
        oT = cube(take(HF * NT), HF)
        base_p = top[0]
        PTm = cube(take(3 * HF * DIAG), 3)
        Ob, lfe = take(128), cube(take(4 * 64), 4)
        lfp = cube(take(4 * 8), 4)
        gk, gq = take(128), take(128)
        top[0] = base_p
        sqt = take(D)
        top[0] = base_raw + RAW1 * UN
        KTc = cube(take(HF * KEYS), HF)
        top[0] = base_att
        Vc = [cube(take(NPAGES * D), NPAGES) for _ in range(2)]
        sS, Pp, PT, Ps, qms = take(384), take(384), take(384), take(320), take(HF * DIAG)
        assert top[0] <= base_att + 6 * D
        top[0] = base_att
        xr = cube(take(3 * D), 3)
        x1 = cube(take(3 * D), 3)
        h2 = cube(take(3 * D), 3)
        h2T = cube(take(KC * NT), KC)
        g2row = take(D)
        top[0] = base_raw
        rawm = [take(UN) for _ in range(RAWM)]
        xs = cube(take(KC * XC), KC)
        base_yrow = top[0]
        yrow = take(D)
        top[0] = base_masks
        tmp, gu = take(512), take(512)
        top[0] = base_masks + CW
        iota, wr = take(SLOTS), take(KC * 36)
        top[0] = base_yrow
        squares = fm[:, base_yrow:base_yrow + D]
        wr3 = cube(wr, KC)
        lg = cube(take(3 * 36), 3)
        base_rt = top[0]
        gl8, gtop, gidx, el8, etop, eidx = (cube(take(24), 3) for _ in range(6))
        ghot, gexp, picks = cube(take(12), 3), cube(take(12), 3), cube(take(6), 3)
        scal, place = [take(3) for _ in range(6)], cube(take(6), 3)
        gap, second, wsum, wden, most = (take(3) for _ in range(5))
        esel = cube(take(96), 3)
        hot = [cube(take(96), 3) for _ in range(2)]
        chosen, rank = cube(take(96), 3), cube(take(96), 3)
        offs, cnts = take(NE), take(NE)
        assert top[0] <= FW
        blkf = cube(fm[:, base_rt:base_rt + NE * JB], NE)
        top[0] = base_raw
        xe = cube(take(3 * D), 3)
        gat = [take(D) for _ in range(6)]

        pair = [(cube(rm[:, 4096 * i:4096 * i + UN], KC), cube(rm[:, 4096 * i + UN:4096 * (i + 1)], KC))
                for i in range(2)]
        R1, R2 = 8192, 8192 + 2 * KC * NT
        r1 = [cube(rm[:, R1 + i * KC * NT:R1 + (i + 1) * KC * NT], KC) for i in range(2)]
        r2 = [cube(rm[:, R2 + i * KC * NT:R2 + (i + 1) * KC * NT], KC) for i in range(2)]
        samp = cube(rm[:, R2 + 2 * KC * NT:R2 + 2 * KC * NT + KC * P], KC)
        e_half = [(rm[:, 4096 * i:4096 * i + UN], rm[:, 4096 * i + UN:4096 * (i + 1)]) for i in (2, 3, 0, 1)]
        R3 = 4096 * NSPLIT
        pack = [cube(rm[:, R3 + 1024 * i:R3 + 1024 * (i + 1)], KC) for i in range(2)]
        htp = cube(rm[:, R3 + 2048:R3 + 2304], 2)
        h2s = [cube(rm[:, 3072 * i:3072 * (i + 1)], 3) for i in range(2)]
        onehot = cube(rm[:, 6144:6144 + 3 * SLOTS], 3)
        wts = cube(dec8[:, 0:6], 3)
        wgs = [cube(rm[:, R2 + 128 * i:R2 + 128 * (i + 1)], KC) for i in range(2)]

        def kM(t, h):
            return kM01[:, t, DM * h:DM * (h + 1)] if t < 2 else kM2[0:NS, DM * h:DM * (h + 1)]

        def vx(t, h, w=DE):
            return vx01[:, t, h, 0:w] if t < 2 else vx2[0:NS, h, 0:w]

        def diag(ap, n=HF):
            return ap.rearrange("p (b x) -> p b x", x=DIAG)[:, :, 0:TS]

        def units(c):
            return sum(units_of(k) for k in range(c)), units_of(c)

        def n_low(c):
            return sum(units_of(k) == 3 for k in range(c))

        def first(section):
            return CPS * SECTIONS.index(section)

        mxi = [im[:, 56 + 24 * i:56 + 24 * (i + 1)].bitcast(U32) for i in range(2)]

        def experts(eng, base, total, step):
            first, turns = base // EB, total // EB
            for u in range(EB):
                step(first, u, base + u, total - 1 - u)
            with eng.Fori(first + 1, first + turns - 1) as i:
                for u in range(EB):
                    step(i, u, i * EB + u, EB)
            for u in range(EB):
                step(first + turns - 1, u, base + total - EB + u, EB - 1 - u)

        def nth_unit(v, u, j, to_come=EB):
            if isinstance(v, int) and v in (0, NE) and u == 0 and j < 2:
                return 3 * v + j, j
            d = (-1, 0, 4)[j] if not (j == 2 and to_come == 0) else 2
            return v * 3 + d, 3 * u + d

        def either(eng, crowd, calm):
            eng.wait_ge(sem("blocks_stored"), 1)
            most = eng.value_load(flag_i, min_val=0, max_val=2 * NT)
            with eng.If(most > CAP):
                crowd()
            with eng.Else():
                calm()
            eng.nop()

        block = ctx.enter_context(nc.Block())

        @block.sync
        def _(sp):
            def small_in(dst, src, s="small_in"):
                sp.dma_start(dst, src).then_inc(sem(s), 16)

            for t in range(2):
                sp.dma_start(xt[:, t, :], A["x_prompt"][:, t, :]).then_inc(sem(f"x_in{t}"), 16)
            sp.dma_start(xt[0:NS, 2, :], A["x_sample"]).then_inc(sem("x_in2"), 16)
            sp.dma_start(g1row, A["norm1_g"].partition_broadcast(P)).then_inc(sem("small_in"), 16)
            small_in(wg, A["w_gates"])
            small_in(bias16, A["b_gates"].partition_broadcast(P))
            small_in(mg, A["mlstm_norm_g"])
            small_in(small[0:BS, 90:94], A["state_m"])
            for c in range(RAW1):
                sp.dma_start(raw[c], A["w_dense"][c]).then_inc(sem(f"raw_in{c % RAW1}"), 16)
            for c in range(RAW1, NCH):
                sp.wait_ge(sem("split_done"), c - RAW1 + 1)
                sp.dma_start(raw[c % RAW1], A["w_dense"][c]).then_inc(sem(f"raw_in{c % RAW1}"), 16)
                for u in range(units_of(c - 2)):
                    for kind, h, b in AT[c - 2, u]:
                        if kind == "SB":
                            n = h * BS + b
                            if n >= 3:
                                sp.wait_ge(sem("cin_used"), n - 2)
                            sp.dma_start(Cin[n % 3], A["state_C"][b, h]).then_inc(sem(f"cin_in{n % 3}"), 16)
                if c == first("fk") + 1:
                    sp.wait_ge(sem("ha_split"), 6)
                    sp.dma_start(gk, A["k_norm_g"].partition_broadcast(P)).then_inc(sem("qk_gain_in"), 16)
                    sp.dma_start(gq, A["q_norm_g"].partition_broadcast(P)).then_inc(sem("qk_gain_in"), 16)
                if c == first("bf") + 2:
                    sp.wait_ge(sem("o_split"), KC)
                    sp.dma_start(xr[:, 0:2, :], A["x_prompt"]).then_inc(sem("xr_in"), 16)
                    sp.dma_start(xr[0:NS, 2, :], A["x_sample"]).then_inc(sem("xr_in"), 16)
                    sp.dma_start(g2row, A["norm2_g"].partition_broadcast(P)).then_inc(sem("xr_in"), 16)
                    sp.dma_start(wr, A["w_router"]).then_inc(sem("xr_in"), 16)
                    sp.dma_start(rb36, A["b_router"].partition_broadcast(P)).then_inc(sem("xr_in"), 16)

            def load(turn_expert, q, kind=None):
                j, blk = ((1, q // 3), (2, q // 3 - 1), (0, q // 3 + 1))[q % 3] if kind is None else kind
                sp.dma_start(rawm[q], A["w_moe"][bass.ds(turn_expert(blk) * 3 + j, 1)].rearrange("a p w -> (a p) w"))\
                    .then_inc(sem(f"e_raw{q // 3}"), 16)

            def odd(q, start, end):
                return {0: (0, 0), 1: (1, 0)}.get(q) if start else (2, EB - 1) if end and q == RAWM - 1 else None

            for q in range(RAWM):
                if q < RAW1:
                    sp.wait_ge(sem("split_done"), NCH - RAW1 + 1 + q)
                elif q == RAW1:
                    sp.wait_ge(sem("m_split"), KC)
                elif q == 5:
                    sp.wait_ge(sem("x1_full"), 1)
                elif q == 7:
                    sp.wait_ge(sem("x1_stored"), 16)
                    sp.wait_ge(sem("x_squared"), 6)
                    sp.wait_ge(sem("h2_full"), 3)
                elif q == 8:
                    sp.wait_ge(sem("router_words"), 1)
                load(lambda blk: blk, q, odd(q, True, False))
            with sp.Fori(1, NE // EB - 1) as i:
                for q in range(RAWM):
                    sp.wait_ge(sem("e_split"), i * RAWM - RAWM + q + 1)
                    load(lambda blk: i * EB + blk, q)
            for q in range(RAWM):
                sp.wait_ge(sem("e_split"), 3 * NE - 2 * RAWM + q + 1)
                load(lambda blk: NE - EB + blk, q, odd(q, False, True))

            sp.wait_ge(sem("e_split"), 3 * NE - RAWM + 2)
            sp.dma_start(xe, x1_dram).then_inc(sem("xe_in"), 16)

            def crowd():
                sp.wait_ge(sem("xe_in"), 16)
                def turns(e, start, end):
                    for half in range(JB // EB):
                        for q in range(RAWM):
                            if not (start and half == 0):
                                sp.wait_ge(sem("e_split"), e * (3 * JB) + 3 * NE + (half - 1) * RAWM + q + 1)
                            load(lambda blk: e + (EB * half + blk) // JB, q,
                                 odd(q, start and half == 0, end and half == JB // EB - 1))

                turns(0, True, False)
                with sp.Fori(1, NE - 1) as e:
                    turns(e, False, False)
                turns(NE - 1, False, True)
                sp.wait_ge(sem("experts_done"), 1)
                sp.dma_start(xe, x1_dram).then_inc(sem("xe_in"), 16)

            either(sp, crowd, sp.nop)
            for t in range(3):
                sp.wait_ge(sem("y_done"), t + 1)
                if t < 2:
                    sp.dma_start(O["y_prompt"][:, t, :], xe[:, t, :]).then_inc(sem("y_out"), 16)
                else:
                    sp.dma_start(O["y_sample"], xe[0:NS, t, :]).then_inc(sem("y_out"), 16)
            sp.wait_ge(sem("y_out"), 48)

        @block.gpsimd
        def _(pool):
            g = Steps(pool, sem("pool_step"))

            def tri(dst, n, value, fillv, pattern, cm, base=0, op=ALU.is_ge):
                g(nc.gpsimd.affine_select(out=dst, in_=dst, compare_op=op, fill=fillv, base=base,
                                          pattern=pattern, channel_multiplier=cm))

            def const(dst, v):
                g(nc.gpsimd.memset(dst, v))

            const(ident, 0.0)
            tri(ident, 128, 0, 1.0, [[-1, 128]], 1, op=ALU.not_equal)
            nc.gpsimd.memset(small[:, 95:96], 0.0).then_inc(sem("ident_ready"), 1)
            for dst, inside, fillv, pat, cm, base in (
                    (upto, 1.0, 0.0, [[1, 128]], -1, 0),
                    (maskT, 0.0, NEG, [[1, 128]], -1, 0),
                    (mask, 0.0, NEG, [[-1, 128]], 1, 0),
                    (after, 1.0, 0.0, [[-1, 128]], 1, -1),
                    (before, 1.0, 0.0, [[1, 128]], -1, -1),
                    (last, 1.0, 0.0, [[0, 128]], 1, -127),
                    (negs[:, 0:128], -1.0, 0.0, [[1, 128]], -1, 0)):
                const(dst, inside)
                tri(dst, 128, 0, fillv, pat, cm, base)
            const(ones, 1.0)
            const(negs[:, 128:256], -1.0)

            def blocks(dst, n, fillv):
                v = dst.rearrange("p (b t) -> p b t", t=TS)
                tri(v, n, 0, fillv, [[-TS, BS], [0, TS]], 1)
                tri(v, n, 0, fillv, [[TS, BS], [0, TS]], -1, TS - 1)

            q = NS
            for dst, inside, fillv, pat, cm in ((upto8, 1.0, 0.0, [[1, 64]], -1), (maskT8, 0.0, NEG, [[1, 64]], -1),
                                                (mask8, 0.0, NEG, [[-1, 64]], 1)):
                const(dst[0:q, :], inside)
                tri(dst[0:q, :], 64, 0, fillv, pat, cm)
                blocks(dst[0:q, :], 64, fillv)
            const(last8[0:q, :], 1.0)
            v = last8[0:q, :].rearrange("p (b t) -> p b t", t=TS)
            tri(v, 64, 0, 0.0, [[-TS, BS], [0, TS]], 1, -(TS - 1), op=ALU.is_equal)
            const(e8[0:BS, :], 1.0)
            v = e8[0:BS, :].rearrange("p (b t) -> p b t", t=TS)
            tri(v, 64, 0, 0.0, [[-1, BS], [0, TS]], 1, 0, op=ALU.is_equal)
            const(blk8[0:q, :], 1.0)
            tri(blk8[0:q, :], 8, 0, 0.0, [[-TS, BS]], 1)
            tri(blk8[0:q, :], 8, 0, 0.0, [[TS, BS]], -1, TS - 1)
            const(first8[0:q, :], 1.0)
            tri(first8[0:q, :], 8, 0, 0.0, [[-TS, BS]], 1, 0, op=ALU.is_equal)
            g(nc.gpsimd.memset(vx01[:, :, :, DM:DE], 1.0))
            g(nc.gpsimd.memset(vx2[0:q, :, DM:DE], 1.0))
            nc.gpsimd.memset(mprev[:, 0, :], 0.0).then_inc(sem("consts"), 1)

            def pe_past(st):
                b = banks_of(st)[-1]
                pool.wait_ge(sem(f"bank_full{b}"), fill[st, b] + 1)

            def out(dst, src, name):
                pool.dma_start(dst, src).then_inc(sem(name), 16)

            pool.dma_start(pt, A["page_table"]).then_inc(sem("pt_in"), 16)
            pool.wait_ge(sem("pt_in"), 16)
            pool.wait_ge(sem("gates_out"), 1)
            out(O["lf_prompt"], lf[:, 0:2, HM:HM + HF], "stored")
            out(O["lf_sample"], lf[0:NS, 2, HM:HM + HF], "stored")
            pool.wait_ge(sem("m_last"), 1)
            out(O["m_prompt"], lastv[0:1, 1, HM:2 * HM], "stored")
            out(O["m_sample"], lastv[0:NS:TS, 2, HM:2 * HM], "stored")

            def pages(b):
                return [pool.value_load(pt[0:1, b * NPAGES + j:b * NPAGES + j + 1], min_val=0, max_val=NPHYS - 1)
                        for j in range(NPAGES)]

            def keys(b):
                if b >= 1:
                    pe_past(("FS1", b - 1, 0))
                for j, page in enumerate(pages(b)):
                    pool.dma_start(KTc[:, :, j * PAGE:(j + 1) * PAGE],
                                   A["cache_kT"][bass.ds(page, 1)].rearrange("a d h s -> (a d) h s"))\
                        .then_inc(sem("keys_in"), 16)
                    pool.dma_start(lfp[:, 2 * (b % 2) + j, :], A["cache_lf"][bass.ds(page, 1)].rearrange("a s h -> (a s) h"))\
                        .then_inc(sem("keys_in"), 16)

            def values(b):
                if b >= 2:
                    pe_past(("FS3", b - 2, 0))
                for j, page in enumerate(pages(b)):
                    pool.dma_start(Vc[b % 2][:, j, :], A["cache_v"][bass.ds(page, 1)].rearrange("a s f -> (a s) f"))\
                        .then_inc(sem(f"values_in{b % 2}"), 16)

            pool.wait_ge(sem("cx_done"), HM)
            out(O["C_prompt"], Cx, "stored")
            for n in range(HM * BS):
                pool.wait_ge(sem("cout_full"), n + 1)
                pool.dma_start(O["C_sample"][n % BS, n // BS], Cout[n % NCOUT]).then_inc(sem(f"cout_out{n % NCOUT}"), 16)
            pool.wait_ge(sem("k_normed"), 3)
            out(O["k_prompt"], fk[:, 0:2, :], "k_stored")
            out(O["k_sample"], fk[0:NS, 2, :], "k_stored")
            keys(0)
            pool.wait_ge(sem("k_stored"), 32)
            pool.wait_ge(sem("t_copied"), 12)
            g(nc.gpsimd.memset(PTm, 0.0))
            g(nc.gpsimd.memset(qms, 0.0))
            g(nc.gpsimd.memset(Ps[0:NS, :], 0.0), sem("att_zeroed"))
            values(0)
            for b in range(1, BS):
                if b == 3:
                    pool.wait_ge(sem("unit_free_a"), units(first("bm"))[0])
                    out(O["v_prompt"], fv[:, 0:2, :], "v_stored")
                    out(O["v_sample"], fv[0:NS, 2, :], "v_stored")
                keys(b)
                values(b)
            pool.wait_ge(sem("o_split"), KC)
            g(nc.gpsimd.iota(iota, pattern=[[1, SLOTS]], base=0, channel_multiplier=0,
                             allow_small_or_imprecise_dtypes=True), sem("iota_ready"))
            pool.wait_ge(sem("x1_full"), 1)
            pool.dma_start(x1_dram, x1).then_inc(sem("x1_stored"), 16)

            def run_experts(base, total, table, rows):
                def packed(v, u, before=None):
                    place = pool.value_load(table[:, bass.ds(v - base, 1)], min_val=0, max_val=SLOTS)
                    src = xs[:, :, bass.ds(place, CAP)]
                    dst = pack[u % 2]
                    if before is not None:
                        pool.wait_ge(sem("e_used"), nth_unit(before, u, 1)[0] + 1)
                    nc.gpsimd.tensor_copy(dst[:, :, 0:CAP], src).then_inc(sem("e_pack_hi"), 1)
                    pool.wait_ge(sem("e_pack_hi"), v + 1)
                    nc.gpsimd.tensor_tensor(small[0:1, 91:92], small[0:1, 93:94], small[0:1, 93:94], ALU.add)
                    nc.gpsimd.tensor_tensor(dst[:, :, CAP:2 * CAP], src, dst[:, :, 0:CAP], ALU.subtract)\
                        .then_inc(sem("e_packed"), 1)

                def step(i, u, v, left):
                    if left >= 2:
                        packed(v + 2, u, v)
                    pool.wait_ge(sem("e_y_taken"), v + 1)
                    pool.dma_start(rows[bass.ds((v - base) * CAP, CAP), :], yrow[64 * (u % 2):64 * (u % 2) + CAP, :])\
                        .then_inc(sem(f"e_y_stored{u % 2}"), 16)

                if base == 0:
                    pool.wait_ge(sem("e_packed"), 1)
                else:
                    packed(base, 0)
                packed(base + 1, 1)
                experts(pool, base, total, step)
                for u in range(2):
                    pool.wait_ge(sem(f"e_y_stored{u}"), (base + total) // 2 * 16)

            def gather(rows, places):
                for t in range(3):
                    for k in range(2):
                        idx = places[0:ROWS[t], 2 * t + k:2 * t + k + 1].bitcast(U32)
                        pool.indirect_dma_start(gat[2 * t + k][0:ROWS[t], :], None, rows,
                                                bass.IndirectOffsetOnAxis(ap=idx, axis=0)).then_inc(sem(f"gathered{t}"), 16)

            pool.wait_ge(sem("xs_ready"), 1)
            run_experts(0, NE, off_i, y_rows)
            nc.gpsimd.memset(small[0:1, 93:94], 0.0).then_inc(sem("blocks_stored"), 1)

            def crowd():
                run_experts(NE, NE * JB, blk_i, y_crowd)
                nc.gpsimd.memset(small[0:1, 92:93], 0.0).then_inc(sem("experts_done"), 1)
                gather(y_crowd, crowd_i)

            either(pool, crowd, lambda: gather(y_rows, slot_i))
            pool.wait_ge(sem("stored"), 16 * 5)
            pool.wait_ge(sem("k_stored"), 16 * 2)
            pool.wait_ge(sem("v_stored"), 16 * 2)
            for i in range(NCOUT):
                pool.wait_ge(sem(f"cout_out{i}"), 16 * (HM * BS // NCOUT))

        @block.scalar
        def _(act):
            s = Steps(act, sem("act_step"))
            A_ = nc.scalar.activation

            def got(st, b):
                act.wait_ge(sem(f"bank_full{b}"), fill[st, b] + 1)

            def pe_past(st):
                b = banks_of(st)[-1]
                act.wait_ge(sem(f"bank_full{b}"), fill[st, b] + 1)

            def done(ins, b):
                s(ins, sem(f"bank_free{b}"))

            def split_hi(c):
                act.wait_ge(sem(f"raw_in{c % RAW1}"), 16 * (c // RAW1 + 1))
                if c >= 2:
                    act.wait_ge(sem("unit_full"), units(c - 1)[0])
                s(A_(pair[c % 2][0], cube(raw[c % RAW1], KC), ACT.Copy), sem("hi_done"))

            def evac(c, u):
                sec, cc = SECTIONS[c // CPS], c % CPS
                n0, n = units(c)
                if sec == "fk" and cc == 0 and u == 0:
                    act.wait_ge(sem("stored"), 16 * 5)
                    for i in range(NCOUT):
                        act.wait_ge(sem(f"cout_out{i}"), 16 * (HM * BS // NCOUT))
                b = (n0 + u) % NRING
                if u == 2:
                    act.wait_ge(sem("unit_full"), n0 + u + 1)
                    if n_low(c):
                        act.wait_ge(sem("low_added"), n_low(c))
                    s(A_(low[0:NS, :], bank[b][NS:2 * NS, 0:CW], ACT.Copy), sem("low_taken"))
                    if sec != "out":
                        act.wait_ge(sem("low_added"), n_low(c) + 1)
                        s(A_(small[0:1, 95:96], small[0:1, 95:96], ACT.Copy), sem("unit_free_a"))
                    return
                if sec in ("bm", "bf", "out"):
                    return
                act.wait_ge(sem("unit_full"), n0 + u + 1)
                if sec in BY_FEATURE:
                    src, j = bank[b][:, 0:NT], 2 * cc + u
                    if sec == "mk":
                        ins = A_(kT[:, j, :], src, ACT.Copy, scale=DM ** -0.5)
                    elif sec == "mq":
                        ins = A_(qT[:, j, :], src, ACT.Copy)
                    else:
                        ins = A_({"mo": sgm, "ga": sga, "gb": sgb}[sec][:, j, :], src, ACT.Sigmoid)
                else:
                    r = ROWS[u]
                    src = bank[b][0:r, 0:CW]
                    if sec == "mv":
                        ins = A_(vx(u, cc, DM), src, ACT.Copy)
                    else:
                        ins = A_({"fk": fk, "fq": fq, "fv": fv}[sec][0:r, u, CW * cc:CW * (cc + 1)], src, ACT.Copy)
                s(ins, sem("unit_free_a"))

            for t in range(3):
                r = ROWS[t]
                act.wait_ge(sem(f"x_in{t}"), 16)
                s(A_(fm[0:r, base_gb:base_gb + D], xt[0:r, t, :], ACT.Square, accum_out=small[0:r, t:t + 1]), sem("x_squared"))
            act.wait_ge(sem("x_var"), 1)
            s(A_(small[:, 6:9], small[:, 3:6], ACT.Sqrt), sem("x_rooted"))
            split_hi(0)
            for n in range(6):
                t, half = n // 2, n % 2
                act.wait_ge(sem("xT_full"), n + 1)
                r = ROWS[t]
                s(A_(r1[0][:, 4 * half:4 * half + 4, TILE0[t]:TILE0[t] + r],
                     cube(bank[3 + n % 2][:, :], 4)[:, :, 0:r], ACT.Copy), sem("xT_hi"))
            split_hi(1)
            s(A_(samp[:, :, 0:NS], r1[0][:, :, TP:NT], ACT.Copy), sem("samp_hi"))

            def gate_exps():
                act.wait_ge(sem("gate_abs"), 1)
                s(A_(lf, cum, ACT.Exp, scale=-1.0))
                s(A_(lf, lf, ACT.Ln, bias=1.0), sem("gate_ln"))

            gate_exps()
            act.wait_ge(sem("consts"), 1)

            def G(st):
                if st[1] == 4:
                    act.wait_ge(sem("gate_args"), 1)
                    s(A_(ew, ew, ACT.Exp), sem("gate_exp"))
                    for t in range(3):
                        r = ROWS[t]
                        for h in range(HM):
                            ins = A_(W[0:r, t, h, 0:r], W[0:r, t, h, 0:r], ACT.Exp, bias=aa[0:r, t, h:h + 1])
                            if (t, h) == (2, HM - 1):
                                s(ins, sem("gate_W"))

            def KT(st):
                t = st[1]
                for i, b in enumerate((6, 7)):
                    got(st, b)
                    dst = kM01[:, t, 512 * i:512 * (i + 1)] if t < 2 else kM2[0:NS, 512 * i:512 * (i + 1)]
                    done(A_(dst, bank[b][0:ROWS[t], 0:512], ACT.Copy), b)

            def P1(st):
                _, c, h = st
                n = c * HM + h
                if n == 0:
                    act.wait_ge(sem("gate_exp"), 1)
                if n >= 2:
                    pe_past(("P2", (n - 2) // HM, (n - 2) % HM))
                s(A_(kw[n % 2], kM(c, h), ACT.Copy, scale=ew[:, c, 8 + h:9 + h]), sem("kw_ready"))

            def take_inter(st, c, h, n):
                got(st, 5)
                r = ROWS[c]
                if n >= 1:
                    act.wait_ge(sem("inter_used"), n)
                ins = A_(inter[0:r, :], bank[5][0:r, 0:DE], ACT.Copy, scale=ew[0:r, c, h:h + 1])
                done(ins, 5)

            def P2(st):
                _, c, h = st
                if c == 1:
                    take_inter(st, c, h, h)

            def F1(st):
                t = st[1]
                r = ROWS[t]
                act.wait_ge(sem("num_full"), HM * (t + 1))
                for h in range(HM):
                    s(A_(hv[0:r, 0:DM], num[0:r, h, 0:DM], ACT.Square, accum_out=small[0:r, 20 + h:21 + h]))
                s(A_(small[0:r, 24:28], small[0:r, 20:24], ACT.Copy), sem("num_squared"))
                act.wait_ge(sem("num_var"), t + 1)
                s(A_(small[0:r, 36:40], small[0:r, 32:36], ACT.Sqrt), sem("num_rooted"))

            def F2(st):
                t = st[1]
                r = ROWS[t]
                for i, b in enumerate((6, 7)):
                    act.wait_ge(sem("hv_full"), 2 * t + i + 1)
                    s(A_(r2[0][:, 4 * i:4 * i + 4, TILE0[t]:TILE0[t] + r], cube(hv, 4)[:, :, 0:r], ACT.Copy),
                      sem("ha_hi"))

            def SA(st):
                h = st[1]
                n = 2 * HM + h
                pe_past(("P2", 1, HM - 2 + h) if h < 2 else ("SB", h - 2, BS - 1))
                s(A_(kw[n % 2][0:NS, :], kM(2, h), ACT.Copy, scale=ew[0:NS, 2, 8 + h:9 + h]), sem("kw_ready"))

            def SB(st):
                _, h, b = st
                n = h * BS + b
                if n >= 2:
                    pe_past(("SB", (n - 2) // BS, (n - 2) % BS))
                s(A_(kwm[n % 2][0:NS, :], kw[h % 2][0:NS, :], ACT.Copy, scale=blk8[0:NS, b:b + 1]), sem("kwm_ready"))
                if b == BS - 1:
                    take_inter(st, 2, h, HM + h)

            def N1(st):
                _, w, t = st
                r = ROWS[t]
                src = (fk, fq)[w]
                n = 3 * w + t
                if n >= 1:
                    act.wait_ge(sem("sq_summed"), n)
                s(A_(sqt[0:r, :], src[0:r, t, :], ACT.Square), sem("squared"))
                act.wait_ge(sem("qk_var"), n + 1)
                s(A_(small[0:r, 60:68], small[0:r, 52:60], ACT.Sqrt), sem("qk_rooted"))

            def N2(st):
                _, w, t = st
                r = ROWS[t]
                for i, b in enumerate((6, 7)):
                    got(st, b)
                    ins = A_((fkT, fqT)[w][:, 4 * i:4 * i + 4, TILE0[t]:TILE0[t] + r],
                             cube(bank[b][:, :], 4)[:, :, 0:r], ACT.Copy)
                    done(ins, b)
                    s(A_(small[0:1, 95:96], small[0:1, 95:96], ACT.Copy), sem("t_copied"))

            def FP1(st):
                h = st[1]
                act.wait_ge(sem("fp_max"), h + 1)
                if h >= 1:
                    pe_past(("FP2", h - 1, 0))
                s(A_(Pp[:, 0:128], sS[:, 0:128], ACT.Exp, bias=small[:, 42:43], accum_out=small[:, 44:45]))
                s(A_(Pp[:, 128:384], sS[:, 128:384], ACT.Exp, bias=small[:, 43:44], accum_out=small[:, 45:46]),
                  sem("fp_exp"))

            def FP2(st):
                h = st[1]
                got(st, 5)
                if h >= 1:
                    pe_past(("FP3", h - 1, 0))
                ins = A_(PT, bank[5][:, 0:384], ACT.Copy)
                done(ins, 5)
                s(A_(small[0:1, 95:96], small[0:1, 95:96], ACT.Copy), sem("fp_pt"))

            def FS1(st):
                b = st[1]
                act.wait_ge(sem("fs_max"), b + 1)
                if b >= 1:
                    pe_past(("FS2", b - 1, 0))
                q = NS
                s(A_(Ps[0:q, 0:PAST], bank[3][0:q, 0:PAST], ACT.Exp, bias=small[0:q, 71:72],
                     accum_out=small[0:q, 72:73]))
                done(A_(Ps[0:q, PAST + TS * b:PAST + TS * (b + 1)], bank[3][0:q, PAST:KEYS], ACT.Exp,
                        bias=small[0:q, 71:72], accum_out=small[0:q, 73:74]), 3)
                s(A_(small[0:1, 95:96], small[0:1, 95:96], ACT.Copy), sem("fs_exp"))

            run = dict(G=G, KT=KT, P1=P1, P2=P2, F1=F1, F2=F2, SA=SA, SB=SB, N1=N1, N2=N2, FP1=FP1, FP2=FP2,
                       FS1=FS1)
            def take_turned(t):
                r = ROWS[t]
                for n in (2 * t, 2 * t + 1):
                    act.wait_ge(sem("h2T_full"), n + 1)
                    s(A_(h2T[:, 4 * (n % 2):4 * (n % 2) + 4, TILE0[t]:TILE0[t] + r],
                         cube(bank[3 + n % 2][:, :], 4)[:, :, 0:r], ACT.Copy), sem("h2T_taken"))

            for c in range(NCH):
                for u in range(units_of(c)):
                    evac(c, u)
                    due = u == units_of(c) - 1 and c + 2 < NCH
                    late = any(st[0] in LATE for st in AT[c, u])
                    if due and not late:
                        split_hi(c + 2)
                    for st in AT[c, u]:
                        if st[0] in run:
                            run[st[0]](st)
                    if due and late:
                        split_hi(c + 2)
                    if (c, u) == LAST_ATT:
                        act.wait_ge(sem("o_full"), HF + BS)
                        for k in range(KC):
                            s(A_(r1[0][:, k, :], oT[:, k, :], ACT.Copy), sem("o_hi"))
                    if c == NCH - 1:
                        if u < 2:
                            act.wait_ge(sem("unit_free_v"), units(c)[0] + u + 1 - units(first("bm"))[0])
                        else:
                            act.wait_ge(sem("x1_full"), 1)
                        s(A_(squares[0:ROWS[u], :], x1[0:ROWS[u], u, :], ACT.Square, accum_out=small[0:ROWS[u], u:u + 1]),
                          sem("x_squared"))
                        if u >= 1:
                            take_turned(u - 1)
                if SECTIONS[c // CPS] == "bf":
                    cc = c % CPS
                    for j in (2 * cc, 2 * cc + 1):
                        act.wait_ge(sem("merged"), j + 1)
                        s(A_(r2[0][:, j, :], sga[:, j, :], ACT.Copy), sem("m_hi"))
                        s(A_(samp[:, j, 0:NS], sga[:, j, TP:NT], ACT.Copy), sem("samp_hi"))

            def expert_hi(n, m):
                if m % 3 == 0:
                    act.wait_ge(sem(f"e_raw{m % RAWM // 3}"), (n - m % RAWM + RAWM) * (48 // RAWM))
                if not (isinstance(n, int) and n < NSPLIT):
                    act.wait_ge(sem("e_used"), n - (NSPLIT - 1))
                A_(e_half[m % NSPLIT][0], rawm[m % RAWM], ACT.Copy).then_inc(sem("e_hi"), 1)

            act.wait_ge(sem("x_var"), 2)
            s(A_(small[:, 6:9], small[:, 3:6], ACT.Sqrt), sem("x_rooted"))
            take_turned(2)
            act.wait_ge(sem("rms_ready"), 1)
            for t in range(3):
                r = ROWS[t]
                s(A_(h2s[0][0:r, t, :], h2[0:r, t, :], ACT.Copy, scale=small[0:r, 9 + t:10 + t]), sem("h2_hi"))
            expert_hi(0, 0)
            expert_hi(1, 1)
            act.wait_ge(sem("router_args"), 1)
            s(A_(gexp, gexp, ACT.Exp))
            act.wait_ge(sem("router_args"), 2)
            s(A_(second, gap, ACT.Exp), sem("router_exps"))
            act.wait_ge(sem("x1_stored"), 16)
            for n in range(0, 2 * KC, 2):
                k, half = n // 2, n % 2
                act.wait_ge(sem("sorted_full"), n + 1)
                s(A_(xs[:, k, NT * half:NT * (half + 1)], bank[n % 4][:, 0:NT], ACT.Copy), sem("sorted_free_a"))

            def run_experts(base, total):
                def hi(v, u, j, to_come=EB):
                    expert_hi(*nth_unit(v, u, j, to_come))

                def take_y(v, u, before, to_come=EB):
                    act.wait_ge(sem("e_used"), nth_unit(v, u, 2, to_come)[0] + 1)
                    if not (isinstance(v, int) and v < 2):
                        act.wait_ge(sem(f"e_y_stored{u % 2}"), before * 16)
                    rows = slice(64 * (u % 2), 64 * (u % 2) + CAP)
                    for j in range(2):
                        ins = A_(yrow[rows, 512 * j:512 * (j + 1)], bank[4 + 2 * (u % 2) + j][0:CAP, :], ACT.Copy)
                    ins.then_inc(sem("e_y_taken"), 1)

                def step(i, u, v, left):
                    act.wait_ge(sem("e_used"), nth_unit(v, u, 1)[0] + 1)
                    A_(tmp[0:CAP, :], bank[u % 2][CAP:2 * CAP, :], ACT.Copy).then_inc(sem("e_low_taken"), 1)
                    act.wait_ge(sem("e_gu"), v + 1)
                    A_(tmp[0:CAP, 0:FE], gu[0:CAP, 0:FE], ACT.Silu).then_inc(sem("e_silu"), 1)
                    if left >= 1:
                        hi(v, u, 2, left)
                    if not (isinstance(v, int) and v == base):
                        take_y(v - 1, u - 1, i * (EB // 2) + (u - 1) // 2)
                    if left >= 2:
                        hi(v + 2, u + 2, 0)
                    act.wait_ge(sem("e_hT_full"), v + 1)
                    A_(htp[:, :, 0:CAP], cube(bank[2][:, 0:2 * CAP], 2), ACT.Copy).then_inc(sem("e_hT_hi"), 1)
                    if left >= 2:
                        hi(v + 2, u + 2, 1)
                    elif left == 1:
                        hi(v + 1, u + 1, 2, 0)

                for u in range(0 if base else 1, 2):
                    for j in range(2):
                        hi(base + u, u, j)
                experts(act, base, total, step)
                take_y(base + total - 1, EB - 1, (base + total - 1) // 2, 0)

            act.wait_ge(sem("sorted_free_v"), KC)
            A_(pack[0][:, :, 0:CAP], xs[:, :, 0:CAP], ACT.Copy).then_inc(sem("e_pack_hi"), 1)
            act.wait_ge(sem("sorted_full"), 2 * KC)
            run_experts(0, NE)
            either(act, lambda: run_experts(NE, NE * JB), act.nop)

        @block.vector
        def _(dve):
            s = Steps(dve, sem("dve_step"))
            v = nc.vector
            TT, TSC, STT, CP = v.tensor_tensor, v.tensor_scalar, v.scalar_tensor_tensor, v.tensor_copy

            def got(st, b):
                dve.wait_ge(sem(f"bank_full{b}"), fill[st, b] + 1)

            def pe_past(st):
                b = banks_of(st)[-1]
                dve.wait_ge(sem(f"bank_full{b}"), fill[st, b] + 1)

            def done(ins, b):
                s(ins, sem(f"bank_free{b}"))

            def split_lo(c):
                dve.wait_ge(sem("hi_done"), c + 1)
                s(TT(pair[c % 2][1], cube(raw[c % RAW1], KC), pair[c % 2][0], ALU.subtract), sem("split_done"))

            dve.wait_ge(sem("x_squared"), 3)
            s(TSC(small[:, 3:5], small[:, 0:2], 1.0 / D, EPS, ALU.mult, ALU.add))
            s(v.memset(small[:, 5:6], 1.0))
            s(TSC(small[0:NS, 5:6], small[0:NS, 2:3], 1.0 / D, EPS, ALU.mult, ALU.add), sem("x_var"))
            dve.wait_ge(sem("x_rooted"), 1)
            dve.wait_ge(sem("small_in"), 80)
            s(v.reciprocal(small[:, 9:12], small[:, 6:9]))
            for t in range(3):
                r = ROWS[t]
                s(STT(xt[0:r, t, :], xt[0:r, t, :], small[0:r, 9 + t:10 + t], g1row[0:r, :], ALU.mult, ALU.mult),
                  sem("xn"))
            for n in range(6):
                t, half = n // 2, n % 2
                dve.wait_ge(sem("xT_hi"), n + 1)
                r = ROWS[t]
                w = (slice(None), slice(4 * half, 4 * half + 4), slice(TILE0[t], TILE0[t] + r))
                s(TT(r1[1][w], cube(bank[3 + n % 2][:, :], 4)[:, :, 0:r], r1[0][w], ALU.subtract), sem("xT_free"))
            s(CP(wgs[0], cube(wg, KC)))
            s(TT(wgs[1], cube(wg, KC), wgs[0], ALU.subtract), sem("wg_split"))
            split_lo(0)
            dve.wait_ge(sem("gates_full"), 1)
            s(CP(dg[0:16, 0, 0:NT], bank[7][0:16, 0:NT]), sem("gates_taken"))
            split_lo(1)
            s(CP(samp[:, :, NS:2 * NS], r1[1][:, :, TP:NT]), sem("samp_lo"))
            dve.wait_ge(sem("gates_full"), 2)
            dve.wait_ge(sem("consts"), 1)
            s(v.memset(gin, 0.0))
            s(TT(gin[:, 0:2, :], cube(bank[7][:, NT:NT + 32], 2), bias16.unsqueeze(1).broadcast_to([P, 2, 16]), ALU.add))
            s(TT(gin[0:NS, 2, :], bank[7][0:NS, NT + 32:NT + 48], bias16[0:NS, :], ALU.add))
            s(TSC(cum, gin[:, :, 4:16], -1.0, None, ALU.mult))
            s(TT(cum, cum, gin[:, :, 4:16], ALU.max), sem("gate_abs"))
            dve.wait_ge(sem("gate_ln"), 1)
            s(TSC(cum, gin[:, :, 4:16], 0.0, None, ALU.min))
            s(TT(lf, cum, lf, ALU.subtract), sem("gates_out"))
            s(TSC(lfn[0:NS, :].rearrange("p (h t) -> p h t", t=TS),
                  lf[0:NS, 2, HM:HM + HF].unsqueeze(2).broadcast_to([NS, HF, TS]), -1.0, None, ALU.mult))
            s(v.tensor_reduce(maskHT[0:NS, :], mask8[0:NS, :].rearrange("p (b t) -> p t b", t=TS), AX_X, ALU.max),
              sem("lfn_ready"))

            def ident_bc(r):
                return ident[0:r, 0:r].unsqueeze(1).broadcast_to([r, HM, r])

            def diagonals(t, vals):
                r = ROWS[t]
                s(TT(dg[0:r, t, 0:HM * r].rearrange("p (h s) -> p h s", h=HM), ident_bc(r),
                     vals.unsqueeze(2).broadcast_to([r, HM, r]), ALU.mult))

            def gate_tops(t, r):
                s(TT(mtop[0:r, t, 0:HM], amax[0:r, t, :], mprev[0:r, t, :], ALU.max))
                s(TT(mtop[0:r, t, HM:8], mtop[0:r, t, 0:HM], cum[0:r, t, 0:HM], ALU.add))

            def minus_diagonals(t):
                r = ROWS[t]
                s(TSC(small[0:r, 12:16], mtop[0:r, t, 0:HM], -1.0, None, ALU.mult))
                diagonals(t, small[0:r, 12:16])

            def G(st):
                n = st[1]
                if n == 1:
                    got(st, 3)
                    s(CP(cum[:, 0:2, :], cube(bank[3][:, 0:24], 2)))
                    done(CP(cum[0:NS, 2, :], bank[3][0:NS, 24:36]), 3)
                    s(TT(aa, gin[:, :, 0:HM], cum[:, :, 0:HM], ALU.subtract))
                    for t in range(3):
                        diagonals(t, aa[0:ROWS[t], t, :])
                    s(v.memset(small[:, 14:16], 0.0), sem("gate_diag"))
                if n == 2:
                    for t, b in enumerate((4, 5, 6)):
                        r = ROWS[t]
                        got(st, b)
                        p = bank[b][0:r, 0:HM * r].rearrange("p (h s) -> p h s", h=HM)
                        m = (mask if t < 2 else mask8)[0:r, 0:r].unsqueeze(1).broadcast_to([r, HM, r])
                        s(TT(p, p, m, ALU.add))
                        done(v.tensor_reduce(amax[0:r, t, :], p, AX_X, ALU.max), b)
                    gate_tops(0, P)
                    s(v.memset(small[:, 14:16], 0.0), sem("gate_top0"))
                if n == 3:
                    got(st, 3)
                    s(CP(mprev[:, 1, :], bank[3][:, HM:8]))
                    done(CP(lastv[:, 0, :], bank[3][:, 0:8]), 3)
                    got(st, 7)
                    done(CP(mprev[0:NS, 2, :], bank[7][0:NS, 0:HM]), 7)
                    gate_tops(1, P)
                    gate_tops(2, NS)
                    for t in range(3):
                        minus_diagonals(t)
                    s(v.memset(small[:, 14:16], 0.0), sem("gate_tops"))
                if n == 4:
                    got(st, 3)
                    done(CP(lastv[:, 1, :], bank[3][:, 0:8]), 3)
                    got(st, 7)
                    done(CP(lastv[0:NS, 2, :], bank[7][0:NS, 0:8]), 7)
                    s(v.memset(small[:, 14:16], 0.0), sem("m_last"))
                    s(v.memset(ew[NS:P, 2, :], 0.0))
                    for t in range(3):
                        r = ROWS[t]
                        s(TT(ew[0:r, t, 0:4], mprev[0:r, t, :], mtop[0:r, t, 0:HM], ALU.subtract))
                        s(TSC(ew[0:r, t, 4:8], mtop[0:r, t, HM:8], -1.0, None, ALU.mult))
                        s(TT(ew[0:r, t, 8:12], aa[0:r, t, :], lastv[0:r, t, 0:HM], ALU.subtract))
                        s(TT(ew[0:r, t, 12:16], mprev[0:r, t, :], lastv[0:r, t, 0:HM], ALU.subtract))
                    for t, b in enumerate((4, 5, 6)):
                        r = ROWS[t]
                        got(st, b)
                        p = bank[b][0:r, 0:HM * r].rearrange("p (h s) -> p h s", h=HM)
                        m = (maskT if t < 2 else maskT8)[0:r, 0:r].unsqueeze(1).broadcast_to([r, HM, r])
                        done(TT(W[0:r, t, :, 0:r], p, m, ALU.add), b)
                    s(v.memset(small[:, 14:16], 0.0), sem("gate_args"))
                    dve.wait_ge(sem("gate_exp"), 1)
                    s(TT(small[0:NS, 52:84].rearrange("p (b h) -> p b h", b=BS),
                         first8[0:NS, :].unsqueeze(2).broadcast_to([NS, BS, HM]),
                         ew[0:NS, 2, 12:16].unsqueeze(1).broadcast_to([NS, BS, HM]), ALU.mult), sem("decay_rows"))
                if n == 5:
                    got(st, 3)
                    done(CP(dec8, bank[3][:, 0:32]), 3)

            def P1(st):
                _, c, h = st
                n = c * HM + h
                got(st, 3)
                if n == 0:
                    dve.wait_ge(sem("gate_W"), 1)
                if n >= 2:
                    pe_past(("P2", (n - 2) // HM, (n - 2) % HM))
                done(TT(SW[n % 2], bank[3][:, 0:128], W[:, c, h, :], ALU.mult), 3)

            def P2(st):
                _, c, h = st
                got(st, 4)
                if c == 0:
                    done(CP(num[:, h, :], bank[4][:, 0:DE]), 4)
                    s(v.memset(small[0:1, 94:95], 0.0), sem("num_full"))
                else:
                    dve.wait_ge(sem("bank_free5"), fill[st, 5] + 1)
                    done(TT(num[:, h, :], bank[4][:, 0:DE], inter, ALU.add), 4)
                    s(v.memset(small[0:1, 94:95], 0.0), sem("num_full"))
                    s(v.memset(small[0:1, 94:95], 0.0), sem("inter_used"))
                for k, b in enumerate((6, 7)):
                    got(st, b)
                    if c == 0:
                        done(CP(Cx[:, h, k, :], bank[b][:, 0:DE]), b)
                    else:
                        done(STT(Cx[:, h, k, :], Cx[:, h, k, :], ew[:, 1, 12 + h:13 + h], bank[b][:, 0:DE],
                                 ALU.mult, ALU.add), b)
                s(v.memset(small[0:1, 94:95], 0.0), sem("cx_first" if c == 0 else "cx_done"))

            def F1(st):
                t = st[1]
                r = ROWS[t]
                dve.wait_ge(sem("num_squared"), t + 1)
                d = num[0:r, :, DM]
                s(TSC(small[0:r, 28:32], d, -1.0, None, ALU.mult))
                s(TT(small[0:r, 28:32], small[0:r, 28:32], d, ALU.max))
                s(TT(small[0:r, 28:32], small[0:r, 28:32], ew[0:r, t, 4:8], ALU.max))
                s(v.reciprocal(small[0:r, 40:44], small[0:r, 28:32]))
                s(TT(small[0:r, 32:36], small[0:r, 40:44], small[0:r, 40:44], ALU.mult))
                s(TT(small[0:r, 32:36], small[0:r, 32:36], small[0:r, 24:28], ALU.mult))
                s(TSC(small[0:r, 32:36], small[0:r, 32:36], 1.0 / DM, EPS, ALU.mult, ALU.add), sem("num_var"))
                dve.wait_ge(sem("num_rooted"), t + 1)
                s(v.reciprocal(small[0:r, 44:48], small[0:r, 36:40]))
                s(TT(small[0:r, 44:48], small[0:r, 44:48], small[0:r, 40:44], ALU.mult))
                for h in range(HM):
                    s(TSC(num[0:r, h, 0:DM], num[0:r, h, 0:DM], small[0:r, 44 + h:45 + h], None, ALU.mult),
                      sem("num_normed"))

            def F2(st):
                t = st[1]
                r = ROWS[t]
                for i, b in enumerate((6, 7)):
                    got(st, b)
                    w = (slice(None), slice(4 * i, 4 * i + 4), slice(TILE0[t], TILE0[t] + r))
                    done(TT(cube(hv, 4)[:, :, 0:r], cube(bank[b][:, :], 4)[:, :, 0:r], sgm[w], ALU.mult), b)
                    s(v.memset(small[0:1, 94:95], 0.0), sem("hv_full"))
                    dve.wait_ge(sem("ha_hi"), 2 * t + i + 1)
                    s(TT(r2[1][w], cube(hv, 4)[:, :, 0:r], r2[0][w], ALU.subtract), sem("ha_split"))

            def SA(st):
                h = st[1]
                got(st, 3)
                n = 2 * HM + h
                pe_past(("P2", 1, HM - 2 + h) if h < 2 else ("SB", h - 2, BS - 1))
                done(TT(SW[n % 2][0:NS, 0:64], bank[3][0:NS, 0:64], W[0:NS, 2, h, 0:64], ALU.mult), 3)
                if h == 0:
                    s(v.memset(qm, 0.0))
                else:
                    pe_past(("SB", h - 1, BS - 1))
                for k in range(2):
                    s(CP(diag(qm[:, 576 * k:576 * (k + 1)]), qT[:, 2 * h + k, TP:NT].rearrange("p (b t) -> p b t", t=TS)),
                      sem("qm_full"))

            def SB(st):
                _, h, b = st
                n = h * BS + b
                if n >= NCOUT:
                    dve.wait_ge(sem(f"cout_out{n % NCOUT}"), 16 * (n // NCOUT))
                for k, bk in enumerate((6, 7)):
                    got(st, bk)
                    done(STT(Cout[n % NCOUT][:, k, :], Cin[n % 3][:, k, :], dec8[:, HM * b + h:HM * b + h + 1],
                             bank[bk][:, 0:DE], ALU.mult, ALU.add), bk)
                s(v.memset(small[0:1, 94:95], 0.0), sem("cout_full"))
                s(v.memset(small[0:1, 94:95], 0.0), sem("cin_used"))
                if b == BS - 1:
                    got(st, 4)
                    dve.wait_ge(sem("bank_free5"), fill[st, 5] + 1)
                    done(TT(num[0:NS, h, :], bank[4][0:NS, 0:DE], inter[0:NS, :], ALU.add), 4)
                    s(v.memset(small[0:1, 94:95], 0.0), sem("num_full"))
                    s(v.memset(small[0:1, 94:95], 0.0), sem("inter_used"))

            def N1(st):
                _, w, t = st
                r = ROWS[t]
                src = (fk, fq)[w]
                n = 3 * w + t
                dve.wait_ge(sem("squared"), n + 1)
                s(v.tensor_reduce(small[0:r, 52:60], cube(sqt[0:r, :], HF), AX_X, ALU.add), sem("sq_summed"))
                s(TSC(small[0:r, 52:60], small[0:r, 52:60], 1.0 / DF, EPS, ALU.mult, ALU.add), sem("qk_var"))
                dve.wait_ge(sem("qk_rooted"), n + 1)
                s(v.reciprocal(small[0:r, 68:76], small[0:r, 60:68]))
                x3 = cube(src[0:r, t, :], HF)
                s(TT(x3, x3, small[0:r, 68:76].unsqueeze(2).broadcast_to([r, HF, DF]), ALU.mult))
                if n == 0:
                    dve.wait_ge(sem("qk_gain_in"), 32)
                    s(TSC(gq, gq, DF ** -0.5, None, ALU.mult))
                g = (gk, gq)[w][0:r, :].unsqueeze(1).broadcast_to([r, HF, DF])
                s(TT(x3, x3, g, ALU.mult), sem("k_normed" if w == 0 else "q_normed"))

            def FP1(st):
                h = st[1]
                got(st, 7)
                if h >= 1:
                    dve.wait_ge(sem("fp_exp"), h)
                done(TT(sS[:, 0:128], bank[7][:, 0:128], mask, ALU.add), 7)
                got(st, 4)
                s(CP(sS[:, 128:256], bank[4][:, 0:128]))
                done(TT(sS[:, 256:384], bank[4][:, 128:256], mask, ALU.add), 4)
                s(v.tensor_reduce(small[:, 40:41], sS[:, 0:128], AX_X, ALU.max))
                s(v.tensor_reduce(small[:, 41:42], sS[:, 128:384], AX_X, ALU.max))
                s(TSC(small[:, 42:44], small[:, 40:42], -1.0, None, ALU.mult), sem("fp_max"))
                dve.wait_ge(sem("fp_exp"), h + 1)
                s(v.reciprocal(small[:, 46:48], small[:, 44:46]))
                s(TSC(Pp[:, 0:128], Pp[:, 0:128], small[:, 46:47], None, ALU.mult))
                s(TSC(Pp[:, 128:384], Pp[:, 128:384], small[:, 47:48], None, ALU.mult), sem("fp_prob"))

            def FP3(st):
                h = st[1]
                got(st, 6)
                done(CP(oT[:, h, 0:TP], bank[6][:, 0:TP]), 6)
                s(v.memset(small[0:1, 94:95], 0.0), sem("o_full"))

            def FS0(st):
                b = st[1]
                if b == 0:
                    dve.wait_ge(sem("att_zeroed"), 1)
                else:
                    pe_past(("FS1", b - 1, 0))
                new = slice(TP + TS * b, TP + TS * (b + 1))
                s(CP(KTc[:, :, PAST:KEYS], fkT[:, :, new]))
                s(CP(diag(qms), fqT[:, :, new]))
                dve.wait_ge(sem("keys_in"), 16 * 2 * NPAGES * (b + 1))
                w = slice(2 * (b % 2), 2 * (b % 2) + 2)
                s(CP(lfe[:, w, :].rearrange("p j (h t) -> p j h t", t=TS),
                     lfp[:, w, :].unsqueeze(3).broadcast_to([P, 2, HF, TS])), sem("fs_ready"))

            def FS1(st):
                b = st[1]
                q = NS
                got(st, 3)
                s(TT(bank[3][0:q, PAST:KEYS], bank[3][0:q, PAST:KEYS], maskHT[0:q, :], ALU.add))
                s(v.tensor_reduce(small[0:q, 70:71], bank[3][0:q, 0:KEYS], AX_X, ALU.max))
                s(TSC(small[0:q, 71:72], small[0:q, 70:71], -1.0, None, ALU.mult))
                if b >= 1:
                    pe_past(("FS2", b - 1, 0))
                    s(v.memset(Ps[0:q, PAST + TS * (b - 1):PAST + TS * b], 0.0))
                s(v.memset(small[0:1, 94:95], 0.0), sem("fs_max"))
                dve.wait_ge(sem("fs_exp"), b + 1)
                s(TT(small[0:q, 74:75], small[0:q, 72:73], small[0:q, 73:74], ALU.add))
                s(v.reciprocal(small[0:q, 75:76], small[0:q, 74:75]))
                s(TSC(Ps[0:q, :], Ps[0:q, :], small[0:q, 75:76], None, ALU.mult), sem("fs_prob"))

            def FS2(st):
                b = st[1]
                got(st, 5)
                if b >= 1:
                    pe_past(("FS3", b - 1, 0))
                for j in range(2):
                    s(CP(diag(PTm[:, j, :]), bank[5][:, 64 * j:64 * (j + 1)].rearrange("p (h t) -> p h t", t=TS)))
                done(CP(diag(PTm[0:NS, 2, :]), bank[5][0:NS, 128:192].rearrange("p (h t) -> p h t", t=TS)), 5)
                s(v.memset(small[0:1, 94:95], 0.0), sem("fs_pt"))

            def FS3(st):
                b = st[1]
                got(st, 4)
                if b >= 1:
                    dve.wait_ge(sem("bank_full6"), fill[("FS4", b - 1, 0), 6] + 1)
                done(CP(Ob[0:NS, :], bank[4][0:NS, 0:DF]), 4)
                s(v.memset(small[0:1, 94:95], 0.0), sem("fs_o"))

            def FS4(st):
                b = st[1]
                got(st, 6)
                done(CP(oT[:, :, TP + TS * b:TP + TS * (b + 1)],
                        bank[6][:, 0:64].rearrange("p (h t) -> p h t", t=TS)), 6)
                s(v.memset(small[0:1, 94:95], 0.0), sem("o_full"))

            run = dict(G=G, P1=P1, P2=P2, F1=F1, F2=F2, SA=SA, SB=SB, N1=N1, FP1=FP1, FP3=FP3, FS0=FS0,
                       FS1=FS1, FS2=FS2, FS3=FS3, FS4=FS4)

            def evac(c, u):
                sec, cc = SECTIONS[c // CPS], c % CPS
                n0, n = units(c)
                j = 2 * cc + u
                if sec == "mo":
                    dve.wait_ge(sem("unit_free_a"), n0 + u + 1)
                    s(TSC(sgm[:, j, :], sgm[:, j, :], mg[:, j:j + 1], None, ALU.mult))
                b = (n0 + u) % NRING
                if u == 2 and sec != "out":
                    dve.wait_ge(sem("low_taken"), n_low(c) + 1)
                    dst = vx(u, cc, DM) if sec == "mv" else \
                        {"fk": fk, "fq": fq, "fv": fv}[sec][0:NS, u, CW * cc:CW * (cc + 1)]
                    s(TT(dst, bank[b][0:NS, 0:CW], low[0:NS, :], ALU.add), sem("low_added"))
                if sec not in ("bm", "bf", "out"):
                    return
                dve.wait_ge(sem("unit_full"), n0 + u + 1)
                if sec == "bm":
                    s(TT(sga[:, j, :], bank[b][:, 0:NT], sga[:, j, :], ALU.mult), sem("unit_free_v"))
                elif sec == "bf":
                    s(TT(sgb[:, j, :], bank[b][:, 0:NT], sgb[:, j, :], ALU.mult), sem("unit_free_v"))
                    s(TT(sga[:, j, :], sga[:, j, :], sgb[:, j, :], ALU.add), sem("merged"))
                else:
                    r = ROWS[u]
                    if cc == 0 and u == 0:
                        dve.wait_ge(sem("xr_in"), 16 * 5)
                        dve.wait_ge(sem("v_stored"), 32)
                        s(v.memset(x1[NS:P, 2, :], 0.0))
                    w = slice(CW * cc, CW * (cc + 1))
                    if u == 2:
                        dve.wait_ge(sem("low_taken"), n_low(c) + 1)
                        s(TT(xr[0:r, u, w], low[0:r, :], xr[0:r, u, w], ALU.add), sem("low_added"))
                    s(TT(x1[0:r, u, w], bank[b][0:r, 0:CW], xr[0:r, u, w], ALU.add),
                      sem("x1_full" if (c, u) == (NCH - 1, 2) else "unit_free_v"))
                    if c == NCH - 1:
                        s(TT(h2[0:r, u, :], x1[0:r, u, :], g2row[0:r, :], ALU.mult), sem("h2_full"))

            for c in range(NCH):
                for u in range(units_of(c)):
                    evac(c, u)
                    due = u == units_of(c) - 1 and c + 2 < NCH
                    late = any(st[0] in LATE for st in AT[c, u])
                    if due and not late:
                        split_lo(c + 2)
                    for st in AT[c, u]:
                        if st[0] in run:
                            run[st[0]](st)
                    if due and late:
                        split_lo(c + 2)
                    if (c, u) == LAST_ATT:
                        for k in range(KC):
                            dve.wait_ge(sem("o_hi"), k + 1)
                            s(TT(r1[1][:, k, :], oT[:, k, :], r1[0][:, k, :], ALU.subtract), sem("o_split"))
                if SECTIONS[c // CPS] == "bf":
                    for j in (2 * (c % CPS), 2 * (c % CPS) + 1):
                        dve.wait_ge(sem("m_hi"), j + 1)
                        s(TT(r2[1][:, j, :], sga[:, j, :], r2[0][:, j, :], ALU.subtract), sem("m_split"))
                        s(CP(samp[:, j, NS:2 * NS], r2[1][:, j, TP:NT]), sem("samp_lo"))

            dve.wait_ge(sem("x_squared"), 6)
            s(TSC(small[:, 3:5], small[:, 0:2], 1.0 / D, EPS, ALU.mult, ALU.add))
            s(v.memset(small[:, 5:6], 1.0))
            s(TSC(small[0:NS, 5:6], small[0:NS, 2:3], 1.0 / D, EPS, ALU.mult, ALU.add), sem("x_var"))
            dve.wait_ge(sem("x_rooted"), 2)
            s(v.reciprocal(small[:, 9:12], small[:, 6:9]), sem("rms_ready"))
            s(v.memset(gl8, NEG))
            s(v.memset(lg[NS:P, 2, :], 0.0))

            def h2_low(t):
                r = ROWS[t]
                dve.wait_ge(sem("h2_hi"), t + 1)
                s(STT(h2s[1][0:r, t, :], h2[0:r, t, :], small[0:r, 9 + t:10 + t], h2s[0][0:r, t, :], ALU.mult, ALU.subtract),
                  sem("h2_split"))

            dve.wait_ge(sem("router_full"), 1)
            for t in range(3):
                r = ROWS[t]
                s(STT(lg[0:r, t, :], bank[5][0:r, 36 * t:36 * (t + 1)], small[0:r, 9 + t:10 + t], rb36[0:r, :],
                      ALU.mult, ALU.add))
            s(CP(gl8[:, :, 0:NG], lg[:, :, 0:NG]))
            gi, ei = (m.rearrange("p (t e) -> p t e", t=3) for m in mxi)
            for t in range(3):
                s(v.max(gtop[:, t, :], gl8[:, t, :]))
                s(v.max_index(gi[:, t, :], gtop[:, t, :], gl8[:, t, :]))
            s(CP(gidx, gi))
            s(TT(gexp, lg[:, :, 0:NG], gtop[:, :, 0:1].broadcast_to([P, 3, NG]), ALU.subtract), sem("router_args"))
            dve.wait_ge(sem("iota_ready"), 1)
            s(TT(ghot, iota[:, 0:NG].unsqueeze(1).broadcast_to([P, 3, NG]), gidx[:, :, 0:1].broadcast_to([P, 3, NG]),
                 ALU.is_equal))
            for t in range(3):
                s(TT(esel[:, t, :].rearrange("p (g e) -> p g e", g=NG),
                     lg[:, t, NG:36].rearrange("p (g e) -> p g e", g=NG),
                     ghot[:, t, :].unsqueeze(2).broadcast_to([P, NG, EPG]), ALU.mult))
                s(v.tensor_reduce(el8[:, t, :], esel[:, t, :].rearrange("p (g e) -> p e g", g=NG), AX_X, ALU.add))
                s(v.max(etop[:, t, :], el8[:, t, :]))
                s(v.max_index(ei[:, t, :], etop[:, t, :], el8[:, t, :]))
            s(CP(eidx, ei))
            s(TT(gap, etop[:, :, 1], etop[:, :, 0], ALU.subtract), sem("router_args"))
            for k in range(2):
                s(STT(picks[:, :, k], gidx[:, :, 0], float(EPG), eidx[:, :, k], ALU.mult, ALU.add))
                s(TT(hot[k], iota[:, 0:NE].unsqueeze(1).broadcast_to([P, 3, NE]),
                     picks[:, :, k:k + 1].broadcast_to([P, 3, NE]), ALU.is_equal))
            s(TT(chosen, hot[0], hot[1], ALU.add), sem("chosen"))
            h2_low(0)
            dve.wait_ge(sem("router_full"), 2)
            s(CP(cnts[0:NE, 0:1], bank[7][0:NE, 0:1]), sem("chosen"))
            h2_low(1)
            s(v.memset(rank[NS:P, 2, :], 0.0))
            dve.wait_ge(sem("router_full"), 3)
            s(CP(offs, bank[6][:, 96:96 + NE]))
            s(v.tensor_reduce(most[:, 0:1], bank[6][:, 96 + NE:96 + 2 * NE], AX_X, ALU.max))
            s(CP(rank[:, 0:2, :], cube(bank[6][:, 0:2 * NE], 2)))
            s(CP(rank[0:NS, 2, :], bank[6][0:NS, 2 * NE:3 * NE]))
            for k in range(2):
                s(TT(esel, hot[k], rank, ALU.mult))
                s(v.tensor_reduce(scal[3 * k], esel, AX_X, ALU.add))
                s(TT(esel, hot[k], offs.unsqueeze(1).broadcast_to([P, 3, NE]), ALU.mult))
                s(v.tensor_reduce(scal[3 * k + 1], esel, AX_X, ALU.add))
                s(TT(place[:, :, k], scal[3 * k], scal[3 * k + 1], ALU.add))
            for t in range(3):
                r = ROWS[t]
                s(TSC(onehot[0:r, t, :], iota[0:r, :], place[0:r, t, 0:1], None, ALU.is_equal))
                s(STT(onehot[0:r, t, :], iota[0:r, :], place[0:r, t, 1:2], onehot[0:r, t, :], ALU.is_equal, ALU.add),
                  sem("onehot"))
                if t == 0:
                    h2_low(2)
                    s(v.memset(small[0:1, 94:95], 0.0), sem("router_words"))
            dve.wait_ge(sem("router_exps"), 1)
            s(v.tensor_reduce(wsum, gexp, AX_X, ALU.add))
            s(TSC(wden, second, 1.0, None, ALU.add))
            s(TT(wsum, wsum, wden, ALU.mult))
            s(v.reciprocal(wts[:, :, 0], wsum))
            s(TT(wts[:, :, 1], wts[:, :, 0], second, ALU.mult))
            slot3, crowd3 = (m.rearrange("p (t k) -> p t k", t=3) for m in (slot_i, crowd_i))
            for k in range(2):
                s(STT(slot3[:, :, k], picks[:, :, k], float(CAP), scal[3 * k], ALU.mult, ALU.add))
                s(STT(crowd3[:, :, k], picks[:, :, k], float(JB * CAP), scal[3 * k], ALU.mult, ALU.add))
            s(CP(flag_i, most[0:1, 0:1]))
            s(CP(off_i, offs[0:1, :]))
            for j in range(JB):
                s(TSC(blkf[0:1, :, j], offs[0:1, :], float(CAP * j), float(SLOTS), ALU.add, ALU.min))
            s(CP(blk_i, blkf[0:1, :, :].rearrange("p e j -> p (e j)")))
            def expert_lo(n, m):
                dve.wait_ge(sem("e_hi"), n + 1)
                hi_half, lo_half = e_half[m % NSPLIT]
                TT(lo_half, rawm[m % RAWM], hi_half, ALU.subtract).then_inc(sem("e_split"), 1)

            dve.wait_ge(sem("x1_stored"), 16)
            s(v.memset(xs[:, :, SLOTS:XC], 0.0))
            for n in range(1, 2 * KC, 2):
                k, half = n // 2, n % 2
                dve.wait_ge(sem("sorted_full"), n + 1)
                s(CP(xs[:, k, NT * half:NT * (half + 1)], bank[n % 4][:, 0:NT]), sem("sorted_free_v"))
                if n in (5, 11):
                    expert_lo(n // 6, n // 6)
            dve.wait_ge(sem("sorted_free_a"), KC)
            s(v.memset(small[0:1, 94:95], 0.0), sem("xs_ready"))
            dve.wait_ge(sem("e_pack_hi"), 1)
            TT(pack[0][:, :, CAP:2 * CAP], xs[:, :, 0:CAP], pack[0][:, :, 0:CAP], ALU.subtract)\
                .then_inc(sem("e_packed"), 1)

            def run_experts(base, total):
                def lo(v, u, j, to_come=EB):
                    expert_lo(*nth_unit(v, u, j, to_come))

                def step(i, u, v, left):
                    dve.wait_ge(sem("e_low_taken"), v + 1)
                    TT(gu[0:CAP, :], bank[u % 2][0:CAP, :], tmp[0:CAP, :], ALU.add).then_inc(sem("e_gu"), 1)
                    dve.wait_ge(sem("e_silu"), v + 1)
                    TT(tmp[0:CAP, FE:2 * FE], tmp[0:CAP, 0:FE], gu[0:CAP, FE:2 * FE], ALU.mult).then_inc(sem("e_hact"), 1)
                    if left >= 1:
                        lo(v + 1, u + 1, 1)
                    if left >= 1:
                        lo(v, u, 2, left)
                    dve.wait_ge(sem("e_hT_hi"), v + 1)
                    TT(htp[:, :, CAP:2 * CAP], cube(bank[2][:, 0:2 * CAP], 2), htp[:, :, 0:CAP], ALU.subtract)\
                        .then_inc(sem("e_hT_split"), 1)
                    if left >= 2:
                        lo(v + 2, u + 2, 0)
                    elif left == 1:
                        lo(v + 1, u + 1, 2, 0)

                if base:
                    lo(base, 0, 0)
                    lo(base, 0, 1)
                lo(base + 1, 1, 0)
                experts(dve, base, total, step)

            run_experts(0, NE)

            def crowd():
                run_experts(NE, NE * JB)
                dve.wait_ge(sem("xe_in"), 32)

            either(dve, crowd, dve.nop)
            dve.wait_ge(sem("xe_in"), 16)
            for t in range(3):
                r = ROWS[t]
                dve.wait_ge(sem(f"gathered{t}"), 32)
                for k in range(2):
                    s(STT(xe[0:r, t, :], gat[2 * t + k][0:r, :], wts[0:r, t, k:k + 1], xe[0:r, t, :], ALU.mult, ALU.add),
                      sem("y_done") if k else None)

        @block.tensor
        def _(pe):
            mm = nc.tensor.matmul
            n_act = units(SECTIONS.index("bm") * CPS)[0]

            def claim(st, b):
                if fill[st, b]:
                    pe.wait_ge(sem(f"bank_free{b}"), fill[st, b])

            def full(ins, b):
                ins.then_inc(sem(f"bank_full{b}"), 1)

            def dense(c, u):
                sec, cc = SECTIONS[c // CPS], c % CPS
                if u == 0:
                    pe.wait_ge(sem("split_done"), c + 1)
                hi, lo = pair[c % 2]
                x = r1 if sec not in ("bm", "out") else r2
                if u == 0 and c == 0:
                    pe.wait_ge(sem("xT_free"), 6)
                if u == 0 and sec == "bm" and cc == 0:
                    pe.wait_ge(sem("ha_split"), 6)
                if u == 0 and sec == "bf" and cc == 0:
                    pe.wait_ge(sem("o_split"), KC)
                n0, n = units(c)
                m = n0 + u - NRING
                if m >= n_act:
                    pe.wait_ge(sem("unit_free_v"), m - n_act + 1)
                elif m >= 0:
                    pe.wait_ge(sem("unit_free_a"), m + 1)
                b = (n0 + u) % NRING
                if u == 2:
                    for s in ("samp_hi", "samp_lo"):
                        pe.wait_ge(sem(s), 1 if sec != "out" else 1 + KC)
                    for k in range(KC):
                        for i, w in enumerate((hi, lo)):
                            ins = mm(bank[b][:, 0:CW], samp[:, k, :], w[:, k, :], start=(k == 0 and i == 0),
                                     stop=(k == KC - 1 and i == 1))
                    ins.then_inc(sem("unit_full"), 1)
                    return
                for k in range(KC):
                    if u == 0 and sec == "out" and cc == 0:
                        pe.wait_ge(sem("m_split"), k + 1)
                    for i, (w, a) in enumerate(((hi, x[0]), (hi, x[1]), (lo, x[0]))):
                        first, final = k == 0 and i == 0, k == KC - 1 and i == 2
                        if sec in BY_FEATURE:
                            ins = mm(bank[b][:, 0:NT], w[:, k, P * u:P * (u + 1)], a[:, k, :],
                                     start=first, stop=final)
                        else:
                            r = ROWS[u]
                            ins = mm(bank[b][0:r, 0:CW], a[:, k, TILE0[u]:TILE0[u] + r], w[:, k, :],
                                     start=first, stop=final)
                ins.then_inc(sem("unit_full"), 1)

            pe.wait_ge(sem("ident_ready"), 1)
            for n in range(6):
                t, half = n // 2, n % 2
                r = ROWS[t]
                pe.wait_ge(sem("xn"), t + 1)
                if n >= 2:
                    pe.wait_ge(sem("xT_free"), n - 1)
                for i in range(4):
                    k = 4 * half + i
                    ins = nc.tensor.transpose(bank[3 + n % 2][:, P * i:P * i + r], xt[0:r, t, P * k:P * (k + 1)],
                                              ident[0:r, 0:r])
                ins.then_inc(sem("xT_full"), 1)
            pe.wait_ge(sem("xT_free"), 6)
            pe.wait_ge(sem("wg_split"), 1)
            for k in range(KC):
                for i, (w, a) in enumerate(((0, 0), (0, 1), (1, 0))):
                    ins = mm(bank[7][0:16, 0:NT], wgs[w][:, k, :], r1[a][:, k, :], start=(k == 0 and i == 0),
                             stop=(k == KC - 1 and i == 2))
            ins.then_inc(sem("gates_full"), 1)

            def turn_gates():
                pe.wait_ge(sem("gates_taken"), 1)
                for t in range(3):
                    r = ROWS[t]
                    ins = nc.tensor.transpose(bank[7][0:r, NT + 16 * t:NT + 16 * (t + 1)],
                                              dg[0:16, 0, TILE0[t]:TILE0[t] + r], ident[0:16, 0:16])
                ins.then_inc(sem("gates_full"), 1)

            def G(st):
                n = st[1]
                if n == 1:
                    pe.wait_ge(sem("gates_out"), 1)
                    for t in range(3):
                        r = ROWS[t]
                        ins = mm(bank[3][0:r, 12 * t:12 * t + 12], (upto if t < 2 else upto8)[0:r, 0:r], lf[0:r, t, :],
                                 start=True, stop=True, skip_group_check=True)
                    full(ins, 3)
                if n == 2:
                    pe.wait_ge(sem("gate_diag"), 1)
                    for t, b in enumerate((4, 5, 6)):
                        r = ROWS[t]
                        full(mm(bank[b][0:r, 0:HM * r], ones[0:r, 0:r], dg[0:r, t, 0:HM * r], start=True, stop=True), b)
                if n == 3:
                    pe.wait_ge(sem("gate_top0"), 1)
                    claim(st, 3)
                    full(mm(bank[3][:, 0:8], last, mtop[:, 0, :], start=True, stop=True), 3)
                    claim(st, 7)
                    full(mm(bank[7][0:NS, 0:HM], e8[0:BS, :], small[0:BS, 90:94], start=True, stop=True), 7)
                if n == 4:
                    pe.wait_ge(sem("gate_tops"), 1)
                    claim(st, 3)
                    full(mm(bank[3][:, 0:8], last, mtop[:, 1, :], start=True, stop=True), 3)
                    claim(st, 7)
                    full(mm(bank[7][0:NS, 0:8], last8[0:NS, :], mtop[0:NS, 2, :], start=True, stop=True), 7)
                    for t, b in enumerate((4, 5, 6)):
                        r = ROWS[t]
                        claim(st, b)
                        full(mm(bank[b][0:r, 0:HM * r], ones[0:r, 0:r], dg[0:r, t, 0:HM * r], start=True, stop=True), b)
                if n == 5:
                    pe.wait_ge(sem("decay_rows"), 1)
                    claim(st, 3)
                    full(mm(bank[3][:, 0:32], ones[0:NS, :], small[0:NS, 52:84], start=True, stop=True), 3)

            def KT(st):
                t = st[1]
                r = ROWS[t]
                if t == 0:
                    pe.wait_ge(sem("unit_free_a"), units(first("mk") + CPS)[0])
                for i, b in enumerate((6, 7)):
                    claim(st, b)
                    for j in range(4):
                        ins = nc.tensor.transpose(bank[b][0:r, P * j:P * (j + 1)],
                                                  kT[:, 4 * i + j, TILE0[t]:TILE0[t] + r], ident)
                    full(ins, b)

            def scores(b, c, h):
                r, w = ROWS[c], slice(TILE0[c], TILE0[c] + ROWS[c])
                for k in range(2):
                    ins = mm(bank[b][0:r, 0:r], kT[:, 2 * h + k, w], qT[:, 2 * h + k, w], start=(k == 0), stop=(k == 1))
                full(ins, b)

            def P1(st):
                _, c, h = st
                claim(st, 3)
                scores(3, c, h)

            def P2(st):
                _, c, h = st
                n = c * HM + h
                if c == 1:
                    pe.wait_ge(sem("cx_first"), h + 1)
                    claim(st, 5)
                    for k in range(2):
                        ins = mm(bank[5][:, 0:DE], qT[:, 2 * h + k, P:2 * P], Cx[:, h, k, :], start=(k == 0), stop=(k == 1))
                    full(ins, 5)
                pe.wait_ge(sem("bank_free3"), fill[("P1", c, h), 3] + 1)
                claim(st, 4)
                if c == 0:
                    pe.wait_ge(sem("unit_free_a"), units(first("mv") + h + 1)[0])
                full(mm(bank[4][:, 0:DE], SW[n % 2], vx(c, h), start=True, stop=True), 4)
                pe.wait_ge(sem("kw_ready"), n + 1)
                for k, b in enumerate((6, 7)):
                    claim(st, b)
                    full(mm(bank[b][:, 0:DE], kw[n % 2][:, P * k:P * (k + 1)], vx(c, h), start=True, stop=True), b)

            def F2(st):
                t = st[1]
                r = ROWS[t]
                for i, b in enumerate((6, 7)):
                    claim(st, b)
                    for j in range(4):
                        k = 4 * i + j
                        if j % 2 == 0:
                            pe.wait_ge(sem("num_normed"), HM * t + k // 2 + 1)
                        ins = nc.tensor.transpose(bank[b][:, P * j:P * j + r],
                                                  num[0:r, k // 2, P * (k % 2):P * (k % 2 + 1)], ident[0:r, 0:r])
                    full(ins, b)

            def SA(st):
                _, h, _ = st
                claim(st, 3)
                scores(3, 2, h)

            def SB(st):
                _, h, b = st
                n = h * BS + b
                if b == 0:
                    claim(("SB", h, BS - 1), 5)
                    pe.wait_ge(sem("qm_full"), 2 * (h + 1))
                pe.wait_ge(sem(f"cin_in{n % 3}"), 16 * (n // 3 + 1))
                for k in range(2):
                    ins = mm(bank[5][0:NS, 0:DE], qm[:, 576 * k + 64 * b:576 * k + 64 * (b + 1)], Cin[n % 3][:, k, :],
                             start=(b == 0 and k == 0), stop=(b == BS - 1 and k == 1))
                if b == BS - 1:
                    full(ins, 5)
                    pe.wait_ge(sem("bank_free3"), fill[("SA", h, 0), 3] + 1)
                    claim(st, 4)
                    full(mm(bank[4][0:NS, 0:DE], SW[(2 * HM + h) % 2][0:NS, 0:64], vx(2, h), start=True, stop=True), 4)
                pe.wait_ge(sem("kwm_ready"), n + 1)
                for k, bk in enumerate((6, 7)):
                    claim(st, bk)
                    ins = mm(bank[bk][:, 0:DE], kwm[n % 2][0:NS, P * k:P * (k + 1)], vx(2, h), start=True, stop=True)
                    full(ins, bk)

            def N2(st):
                _, w, t = st
                r = ROWS[t]
                pe.wait_ge(sem(("k_normed", "q_normed")[w]), t + 1)
                for i, b in enumerate((6, 7)):
                    claim(st, b)
                    for j in range(4):
                        ins = nc.tensor.transpose(bank[b][:, P * j:P * j + r],
                                                  (fk, fq)[w][0:r, t, P * (4 * i + j):P * (4 * i + j + 1)],
                                                  ident[0:r, 0:r])
                    full(ins, b)

            def FP1(st):
                h = st[1]
                col = [lf[:, t, HM + h:HM + h + 1].broadcast_to([P, P]) for t in range(2)]
                claim(st, 7)
                mm(bank[7][:, 0:P], fqT[:, h, 0:P], fkT[:, h, 0:P], start=True, stop=False)
                full(mm(bank[7][:, 0:P], col[0], negs[:, 0:P], start=False, stop=True), 7)
                claim(st, 4)
                mm(bank[4][:, 0:TP], fqT[:, h, P:TP], fkT[:, h, 0:TP], start=True, stop=False)
                mm(bank[4][:, 0:TP], col[0], negs, start=False, stop=False)
                full(mm(bank[4][:, P:TP], col[1], negs[:, 0:P], start=False, stop=True), 4)

            def FP2(st):
                h = st[1]
                pe.wait_ge(sem("fp_prob"), h + 1)
                claim(st, 5)
                for j in range(3):
                    ins = nc.tensor.transpose(bank[5][:, P * j:P * (j + 1)], Pp[:, P * j:P * (j + 1)], ident)
                full(ins, 5)

            def FP3(st):
                h = st[1]
                pe.wait_ge(sem("fp_pt"), h + 1)
                claim(st, 6)
                mm(bank[6][:, 0:TP], fv[:, 0, DF * h:DF * (h + 1)], PT[:, 0:TP], start=True, stop=False)
                full(mm(bank[6][:, P:TP], fv[:, 1, DF * h:DF * (h + 1)], PT[:, TP:TP + P], start=False, stop=True), 6)

            def FS1(st):
                b = st[1]
                q = NS
                pe.wait_ge(sem("fs_ready"), b + 1)
                pe.wait_ge(sem("keys_in"), 16 * 2 * NPAGES * (b + 1))
                claim(st, 3)
                for h in range(HF):
                    mm(bank[3][0:q, 0:KEYS], qms[:, 64 * h:64 * (h + 1)], KTc[:, h, :], start=(h == 0), stop=False)
                l0, l1 = lfe[:, 2 * (b % 2), :], lfe[:, 2 * (b % 2) + 1, :]
                mm(bank[3][0:q, 0:P], l0, after, start=False, stop=False)
                mm(bank[3][0:q, 0:P], l1, ones, start=False, stop=False)
                mm(bank[3][0:q, P:2 * P], l1, after, start=False, stop=False)
                full(mm(bank[3][0:q, PAST:KEYS], lfn[0:q, :], upto8[0:q, TS * b:TS * (b + 1)],
                        start=False, stop=True), 3)

            def FS2(st):
                b = st[1]
                pe.wait_ge(sem("fs_prob"), b + 1)
                claim(st, 5)
                for j, w in enumerate((P, P, NS)):
                    ins = nc.tensor.transpose(bank[5][0:w, 64 * j:64 * (j + 1)], Ps[0:NS, P * j:P * j + w],
                                              ident[0:NS, 0:NS])
                full(ins, 5)

            def FS3(st):
                b = st[1]
                if b == 0:
                    pe.wait_ge(sem("unit_free_a"), units(first("fv") + CPS)[0])
                pe.wait_ge(sem("fs_pt"), b + 1)
                pe.wait_ge(sem(f"values_in{b % 2}"), 16 * NPAGES * (b // 2 + 1))
                claim(st, 4)
                for h in range(HF):
                    for j in range(3):
                        r = P if j < 2 else NS
                        rhs = (Vc[b % 2][:, j, DF * h:DF * (h + 1)] if j < 2 else fv[0:NS, 2, DF * h:DF * (h + 1)])
                        ins = mm(bank[4][0:NS, 0:DF], PTm[0:r, j, 64 * h:64 * (h + 1)], rhs,
                                 start=(h == 0 and j == 0), stop=(h == HF - 1 and j == 2))
                full(ins, 4)

            def FS4(st):
                b = st[1]
                pe.wait_ge(sem("fs_o"), b + 1)
                claim(st, 6)
                full(nc.tensor.transpose(bank[6][:, 0:64], Ob[0:NS, :], ident[0:NS, 0:NS]), 6)

            run = dict(G=G, KT=KT, P1=P1, P2=P2, F2=F2, SA=SA, SB=SB, N2=N2, FP1=FP1, FP2=FP2, FP3=FP3,
                       FS1=FS1, FS2=FS2, FS3=FS3, FS4=FS4)
            def turn(t):
                r = ROWS[t]
                pe.wait_ge(sem("h2_full"), t + 1)
                for n in (2 * t, 2 * t + 1):
                    if n >= 2:
                        pe.wait_ge(sem("h2T_taken"), n - 1)
                    for i in range(4):
                        k = 4 * (n % 2) + i
                        ins = nc.tensor.transpose(bank[3 + n % 2][:, P * i:P * i + r], h2[0:r, t, P * k:P * (k + 1)],
                                                  ident[0:r, 0:r])
                    ins.then_inc(sem("h2T_full"), 1)

            def logits(t):
                r = ROWS[t]
                pe.wait_ge(sem("h2T_taken"), 2 * t + 2)
                for k in range(KC):
                    ins = mm(bank[5][0:r, 36 * t:36 * (t + 1)], h2T[:, k, TILE0[t]:TILE0[t] + r], wr3[:, k, :],
                             start=(k == 0), stop=(k == KC - 1), skip_group_check=True)
                if t == 2:
                    ins.then_inc(sem("router_full"), 1)

            for c in range(NCH):
                for u in range(units_of(c)):
                    dense(c, u)
                    if (c, u) == (0, 0):
                        turn_gates()
                    if (c, u) == (NCH - 1, 1):
                        turn(0)
                    for st in AT[c, u]:
                        if st[0] in run:
                            run[st[0]](st)

            turn(1)
            logits(0)
            turn(2)
            logits(1)
            logits(2)
            pe.wait_ge(sem("chosen"), 1)
            for t in range(3):
                r = ROWS[t]
                ins = mm(bank[7][0:NE, 0:1], chosen[0:r, t, :], ones[0:r, 0:1], start=(t == 0), stop=(t == 2))
            ins.then_inc(sem("router_full"), 1)
            for t in range(3):
                r = ROWS[t]
                for e in range(t):
                    mm(bank[6][0:r, NE * t:NE * (t + 1)], ones[:, 0:r], chosen[:, e, :], start=(e == 0), stop=False,
                       skip_group_check=True)
                mm(bank[6][0:r, NE * t:NE * (t + 1)], before[0:r, 0:r], chosen[0:r, t, :], start=(t == 0), stop=True,
                   skip_group_check=True)
            for t in range(3):
                r = ROWS[t]
                mm(bank[6][:, 128:160], ones[0:r, :], chosen[0:r, t, :], start=(t == 0), stop=(t == 2),
                   skip_group_check=True)
            pe.wait_ge(sem("chosen"), 2)
            mm(bank[6][:, 96:96 + NE], cnts[0:NE, 0:1].broadcast_to([NE, P]), before[0:NE, 0:NE], start=True, stop=True,
               skip_group_check=True).then_inc(sem("router_full"), 1)
            for n in range(2 * KC):
                k, half = n // 2, n % 2
                if n >= 4:
                    pe.wait_ge(sem(("sorted_free_a", "sorted_free_v")[half]), n // 2 - 1)
                for t in range(3):
                    r = ROWS[t]
                    if n == 0:
                        pe.wait_ge(sem("h2_split"), t + 1)
                        pe.wait_ge(sem("onehot"), t + 1)
                    for i in range(2):
                        ins = mm(bank[n % 4][:, 0:NT], h2s[i][0:r, t, P * k:P * (k + 1)],
                                 onehot[0:r, t, NT * half:NT * (half + 1)], start=(t == 0 and i == 0),
                                 stop=(t == 2 and i == 1))
                ins.then_inc(sem("sorted_full"), 1)

            def run_experts(base, total):
                def gate_up(v, u, j, between=None):
                    if j == 0:
                        pe.wait_ge(sem("e_packed"), v + 1)
                        if not (isinstance(v, int) and v < 2):
                            pe.wait_ge(sem("e_gu"), v - 1)
                    n, m = nth_unit(v, u, j)
                    pe.wait_ge(sem("e_split"), n + 1)
                    w = [cube(x, KC) for x in e_half[m % NSPLIT]]
                    for k in range(KC):
                        for i in range(2):
                            ins = mm(bank[u % 2][:, FE * j:FE * (j + 1)], pack[u % 2][:, k, :], w[i][:, k, :],
                                     start=(k == 0 and i == 0), stop=(k == KC - 1 and i == 1), skip_group_check=True)
                        if k == 0 and between:
                            between()
                    ins.then_inc(sem("e_used"), 1)

                def step(i, u, v, left):
                    def transposes():
                        for j in range(2):
                            ins = nc.tensor.transpose(bank[2][:, CAP * j:CAP * (j + 1)],
                                                      tmp[0:CAP, FE + P * j:FE + P * (j + 1)], ident[0:CAP, 0:CAP])
                        ins.then_inc(sem("e_hT_full"), 1)

                    if left >= 1:
                        gate_up(v + 1, u + 1, 0)
                        pe.wait_ge(sem("e_hact"), v + 1)
                        gate_up(v + 1, u + 1, 1, transposes)
                    else:
                        pe.wait_ge(sem("e_hact"), v + 1)
                        transposes()
                    n, m = nth_unit(v, u, 2, left)
                    down = [cube(x, 2) for x in e_half[m % NSPLIT]]
                    pe.wait_ge(sem("e_split"), n + 1)
                    pe.wait_ge(sem("e_hT_split"), v + 1)
                    if not (isinstance(v, int) and v < 2):
                        pe.wait_ge(sem("e_y_taken"), v - 1)
                    for j in range(2):
                        for k in range(2):
                            for n, (a, w) in enumerate(((0, 0), (0, 1), (1, 0))):
                                ins = mm(bank[4 + 2 * (u % 2) + j][0:CAP, :], htp[:, k, CAP * a:CAP * (a + 1)],
                                         down[w][:, k, 512 * j:512 * (j + 1)], start=(k == 0 and n == 0),
                                         stop=(k == 1 and n == 2))
                    ins.then_inc(sem("e_used"), 1)

                gate_up(base, 0, 0)
                gate_up(base, 0, 1)
                experts(pe, base, total, step)

            run_experts(0, NE)
            either(pe, lambda: run_experts(NE, NE * JB), pe.nop)


def kernel(**inputs):
    import numpy as np
    import concourse.bacc as bacc
    from concourse.bass_utils import run_bass_kernel_spmd

    x = {k: np.ascontiguousarray(v) for k, v in inputs.items()}
    w_in = x["w_in"][0]
    widths = (1024, 1024, 1024, 1024, HM, HM, 1024, 1024, 1024, HF, 1024, 1024)
    cuts = np.cumsum((0,) + widths)
    part = dict(zip(("mq", "mk", "mv", "mo", "mi", "mf", "fq", "fk", "fv", "ff", "ga", "gb"),
                    (w_in[:, a:b] for a, b in zip(cuts[:-1], cuts[1:]))))
    part |= {"bm": x["w_branch_mlstm"][0], "bf": x["w_branch_fox"][0], "out": x["w_out"][0]}

    def by_partition(w):
        return np.ascontiguousarray(w.reshape(-1, P, w.shape[-1]).transpose(1, 0, 2))

    dense = np.stack([by_partition(part[s][:, CW * c:CW * (c + 1)]).reshape(P, UN) for s in SECTIONS for c in range(CPS)])
    moe = np.stack([by_partition(x[w][0, e]).reshape(P, UN) for e in range(NE) for w in ("w_gate", "w_up", "w_down")])
    xp = x["x_prompt"][0]
    state = np.concatenate([x["state_C"][0], x["state_n"][0][..., None]], axis=-1)
    arrays = {
        "x_prompt": by_partition(xp), "x_sample": x["x_sample"].reshape(NS, D),
        "norm1_g": x["norm1_g"][0], "norm2_g": x["norm2_g"][0],
        "w_dense": dense, "w_moe": moe,
        "w_gates": by_partition(np.concatenate([part["mi"], part["mf"], part["ff"]], axis=1)).reshape(P, 128),
        "b_gates": np.concatenate([x["b_igate"][0], x["b_fgate_mlstm"][0], x["b_fgate_fox"][0]]),
        "mlstm_norm_g": np.ascontiguousarray(x["mlstm_norm_g"][0].reshape(KC, P).T),
        "q_norm_g": x["q_norm_g"][0], "k_norm_g": x["k_norm_g"][0],
        "state_C": np.ascontiguousarray(state.reshape(BS, HM, 2, P, DE).transpose(0, 1, 3, 2, 4)),
        "state_m": x["state_m"][0],
        "cache_kT": np.ascontiguousarray(x["cache_k"][0].transpose(0, 3, 2, 1)),
        "cache_v": x["cache_v"][0].reshape(NPHYS, PAGE, D),
        "cache_lf": x["cache_lf"][0],
        "page_table": x["page_table"].reshape(1, BS * NPAGES).astype(np.int32),
        "w_router": by_partition(np.concatenate([x["w_router_group"][0], x["w_router_expert"][0]], axis=1)).reshape(P, KC * 36),
        "b_router": np.concatenate([x["b_router_group"][0], x["b_router_expert"][0]]),
    }
    outs = {
        "y_prompt": (P, 2, D), "y_sample": (NS, D), "k_prompt": (P, 2, D), "v_prompt": (P, 2, D),
        "lf_prompt": (P, 2, HF), "k_sample": (NS, D), "v_sample": (NS, D), "lf_sample": (NS, HF),
        "C_prompt": (P, HM, 2, DE), "m_prompt": (1, HM), "C_sample": (BS, HM, P, 2, DE), "m_sample": (BS, HM),
    }
    nc = bacc.Bacc("TRN2", target_bir_lowering=False, num_devices=1)
    A = {k: nc.dram_tensor(f"in_{k}", v.shape, mybir.dt.from_np(v.dtype), kind="ExternalInput").ap()
         for k, v in arrays.items()}
    O = {k: nc.dram_tensor(f"out_{k}", s, F32, kind="ExternalOutput").ap() for k, s in outs.items()}
    hybrid_step(nc, A, O)
    r = run_bass_kernel_spmd(nc, [{f"in_{k}": v for k, v in arrays.items()}], core_ids=[0])
    o = {k: r.results[0][f"out_{k}"] for k in outs}

    def rows(a, *shape):
        return np.ascontiguousarray(a.transpose(1, 0, 2)).reshape(shape)

    Cp = np.ascontiguousarray(o["C_prompt"].transpose(1, 2, 0, 3)).reshape(1, 1, HM, DM, DE)
    Cs = np.ascontiguousarray(o["C_sample"].transpose(0, 1, 3, 2, 4)).reshape(1, BS, HM, DM, DE)
    return (rows(o["y_prompt"], 1, TP, D), o["y_sample"].reshape(BS, TS, D),
            rows(o["k_prompt"], 1, 1, TP, HF, DF), rows(o["v_prompt"], 1, 1, TP, HF, DF),
            rows(o["lf_prompt"], 1, 1, TP, HF),
            o["k_sample"].reshape(1, BS, TS, HF, DF), o["v_sample"].reshape(1, BS, TS, HF, DF),
            o["lf_sample"].reshape(1, BS, TS, HF),
            np.ascontiguousarray(Cp[..., :DM]), np.ascontiguousarray(Cp[..., DM]), o["m_prompt"].reshape(1, 1, HM),
            np.ascontiguousarray(Cs[..., :DM]), np.ascontiguousarray(Cs[..., DM]), o["m_sample"].reshape(1, BS, HM))
```
